# Optimizing a Trainium2 kernel written in Bass

```python
import jax, jax.numpy as jnp
from jax import lax
import numpy as np

D_MODEL = 1024
BATCH = 1
SEQ = 256
DEPTH = 1
DEC_BATCH = 8
DEC_SEQ = 4
PAST_LEN = 2048
PAGE_SIZE = 128

POOL_WINDOWS = (2, 4, 8, 16)
POOL_GROUPS = len(POOL_WINDOWS)
POOL_GROUP_DIM = 128
POOL_DIM = POOL_GROUPS * POOL_GROUP_DIM
POOL_BUF = max(POOL_WINDOWS) - 1
N_HEADS = 8
HEAD_DK = 128
HEAD_DV = 128
QK_DIM = N_HEADS * HEAD_DK
V_DIM = N_HEADS * HEAD_DV
CONV_WIDTH = 4
CONV_DIM = 2 * QK_DIM + V_DIM
DELTA_CHUNK = 64
N_GROUPS = 4
EXPERTS_PER_GROUP = 8
N_EXPERTS = N_GROUPS * EXPERTS_PER_GROUP
TOP_K = 2
D_EXPERT = 256
IN_DIM = POOL_DIM + CONV_DIM + 2 * N_HEADS + V_DIM + 2 * D_MODEL
SPLITS = [int(s) for s in np.cumsum([POOL_DIM, CONV_DIM, N_HEADS, N_HEADS, V_DIM, D_MODEL])]
EPS = 1e-6

kernel_name = 'hybrid_pool_gdn_hmoe_step'

def rmsnorm(x, w):
    xf = x.astype(jnp.float32)
    y = xf * lax.rsqrt(jnp.mean(xf * xf, axis=-1, keepdims=True) + EPS)
    return (y * w.astype(jnp.float32)).astype(x.dtype)

def l2norm(x):
    xf = x.astype(jnp.float32)
    return xf * lax.rsqrt(jnp.sum(xf * xf, axis=-1, keepdims=True) + EPS)

def pool_mix(u, buf, pos0, w_pool, pool_scale):
    B, T, _ = u.shape
    ext = jnp.concatenate([buf.astype(u.dtype), u], axis=1)
    cs = jnp.cumsum(ext.astype(jnp.float32), axis=1)
    cs = jnp.pad(cs, ((0, 0), (1, 0), (0, 0)))
    pos = pos0 + jnp.arange(T)
    means = []
    for gi, win in enumerate(POOL_WINDOWS):
        sl = slice(gi * POOL_GROUP_DIM, (gi + 1) * POOL_GROUP_DIM)
        s = cs[:, POOL_BUF + 1:POOL_BUF + 1 + T, sl] - cs[:, POOL_BUF + 1 - win:POOL_BUF + 1 - win + T, sl]
        cnt = jnp.minimum(win, pos + 1).astype(jnp.float32)
        means.append(s / cnt[None, :, None])
    pooled = jnp.stack(means, axis=2) - u.astype(jnp.float32).reshape(B, T, POOL_GROUPS, POOL_GROUP_DIM)
    y = jnp.einsum('btgc,gcd->btgd', pooled.astype(u.dtype), w_pool)
    y = y * pool_scale.reshape(POOL_GROUPS, POOL_GROUP_DIM)
    return y.reshape(B, T, POOL_DIM), ext[:, -POOL_BUF:]

def causal_conv(u, buf, w_conv):
    T = u.shape[1]
    ext = jnp.concatenate([buf.astype(u.dtype), u], axis=1)
    out = ext[:, 0:T] * w_conv[0]
    for j in range(1, CONV_WIDTH):
        out = out + ext[:, j:j + T] * w_conv[j]
    return jax.nn.silu(out), ext[:, -(CONV_WIDTH - 1):]

def gated_delta_chunked(q, k, v, g, beta, s0, chunk):
    B, T, H, DK = q.shape
    DV = v.shape[-1]
    n = T // chunk
    f32 = jnp.float32

    def blocks(a):
        a = a.astype(f32).reshape((B, n, chunk) + a.shape[2:])
        return jnp.moveaxis(a, 2, 3)

    q = blocks(q) * DK ** -0.5
    k = blocks(k)
    v = blocks(v)
    g = blocks(g)
    beta = blocks(beta)
    G = jnp.cumsum(g, axis=-1)
    idx = jnp.arange(chunk)
    causal = idx[:, None] >= idx[None, :]
    strict = idx[:, None] > idx[None, :]
    decay = jnp.exp(jnp.where(causal, G[..., :, None] - G[..., None, :], -jnp.inf))
    kb = k * beta[..., None]
    A = jnp.einsum('bnhid,bnhjd->bnhij', kb, k) * decay * strict
    eye = jnp.eye(chunk, dtype=f32)
    t_inv = lax.linalg.triangular_solve(eye + A, jnp.broadcast_to(eye, A.shape),
                                        left_side=True, lower=True, unit_diagonal=True)
    w = jnp.einsum('bnhij,bnhjd->bnhid', t_inv, kb * jnp.exp(G)[..., None])
    u = jnp.einsum('bnhij,bnhjd->bnhid', t_inv, v * beta[..., None])
    q_dec = q * jnp.exp(G)[..., None]
    a_qk = jnp.einsum('bnhid,bnhjd->bnhij', q, k) * decay
    g_last = G[..., -1]
    k_dec = k * jnp.exp(g_last[..., None] - G)[..., None]

    def step(S, xs):
        w_c, u_c, qd_c, aqk_c, kd_c, gl_c = xs
        v_new = u_c - jnp.einsum('bhcd,bhde->bhce', w_c, S)
        o_c = jnp.einsum('bhcd,bhde->bhce', qd_c, S) + jnp.einsum('bhij,bhje->bhie', aqk_c, v_new)
        S = S * jnp.exp(gl_c)[..., None, None] + jnp.einsum('bhcd,bhce->bhde', kd_c, v_new)
        return S, o_c

    xs = (jnp.moveaxis(w, 1, 0), jnp.moveaxis(u, 1, 0), jnp.moveaxis(q_dec, 1, 0),
          jnp.moveaxis(a_qk, 1, 0), jnp.moveaxis(k_dec, 1, 0), jnp.moveaxis(g_last, 1, 0))
    S, o = lax.scan(step, s0.astype(f32), xs)
    o = jnp.moveaxis(jnp.moveaxis(o, 0, 1), 3, 2).reshape(B, T, H, DV)
    return o, S

def hier_moe(h, w_router_group, b_router_group, w_router_expert, b_router_expert, w_gate, w_up, w_down):
    hf = h.astype(jnp.float32)
    lg = hf @ w_router_group.astype(jnp.float32) + b_router_group.astype(jnp.float32)
    p_group = jax.nn.softmax(lg, axis=-1)
    gsel = jnp.argmax(lg, axis=-1)
    pg = jnp.take_along_axis(p_group, gsel[..., None], axis=-1)
    le = jnp.einsum('btd,dge->btge', hf, w_router_expert.astype(jnp.float32)) + b_router_expert.astype(jnp.float32)
    le_sel = jnp.take_along_axis(le, gsel[..., None, None], axis=2)[..., 0, :]
    top_v, top_i = lax.top_k(le_sel, TOP_K)
    w_k = jax.nn.softmax(top_v, axis=-1) * pg
    expert_id = gsel[..., None] * EXPERTS_PER_GROUP + top_i
    combine = jnp.sum(jax.nn.one_hot(expert_id, N_EXPERTS, dtype=jnp.float32) * w_k[..., None], axis=-2)
    a = jnp.einsum('btd,edf->btef', h, w_gate)
    b = jnp.einsum('btd,edf->btef', h, w_up)
    act = jax.nn.silu(a) * b * combine[..., None].astype(h.dtype)
    return jnp.einsum('btef,efd->btd', act, w_down)

def trunk_layer(x, pool_buf, conv_buf, s0, pos0, chunk, norm1_w, w_in, w_pool, pool_scale, w_conv, a_log,
                dt_bias, o_norm_w, w_branch_pool, w_branch_delta, w_out, norm2_w, w_router_group,
                b_router_group, w_router_expert, b_router_expert, w_gate, w_up, w_down):
    B, T, _ = x.shape
    f32 = jnp.float32
    h = rmsnorm(x, norm1_w)
    proj = jnp.einsum('btd,de->bte', h, w_in)
    u_pool, u_qkv, b_raw, a_raw, z, gate_pool, gate_delta = jnp.split(proj, SPLITS, axis=-1)
    y_pool, pool_buf_new = pool_mix(u_pool, pool_buf, pos0, w_pool, pool_scale)
    qkv, conv_buf_new = causal_conv(u_qkv, conv_buf, w_conv)
    q, k, v = jnp.split(qkv, [QK_DIM, 2 * QK_DIM], axis=-1)
    q = l2norm(q.reshape(B, T, N_HEADS, HEAD_DK))
    k = l2norm(k.reshape(B, T, N_HEADS, HEAD_DK))
    v = v.reshape(B, T, N_HEADS, HEAD_DV)
    beta = jax.nn.sigmoid(b_raw.astype(f32))
    g = -jnp.exp(a_log.astype(f32)) * jax.nn.softplus(a_raw.astype(f32) + dt_bias.astype(f32))
    o, s_new = gated_delta_chunked(q, k, v, g, beta, s0, chunk)
    o = rmsnorm(o, o_norm_w) * jax.nn.silu(z.reshape(B, T, N_HEADS, HEAD_DV).astype(f32))
    y_delta = o.reshape(B, T, V_DIM).astype(x.dtype)
    branch_pool = jnp.einsum('btc,cd->btd', y_pool, w_branch_pool)
    branch_delta = jnp.einsum('btc,cd->btd', y_delta, w_branch_delta)
    merged = jax.nn.sigmoid(gate_pool) * branch_pool + jax.nn.sigmoid(gate_delta) * branch_delta
    x = x + jnp.einsum('btd,de->bte', merged, w_out)
    x = x + hier_moe(rmsnorm(x, norm2_w), w_router_group, b_router_group, w_router_expert,
                     b_router_expert, w_gate, w_up, w_down)
    return x, pool_buf_new, conv_buf_new, s_new.astype(x.dtype)

def setup_inputs(seed: int = 0) -> dict:
    key = jax.random.key(seed)
    ks = jax.random.split(key, 28)
    f32 = jnp.float32
    L = DEPTH

    def nrm(k, shape, scale):
        return jax.random.normal(k, shape, f32) * scale

    dt = jax.random.uniform(ks[11], (L, N_HEADS), f32, 0.001, 0.1)
    return {
        'x_prompt': nrm(ks[0], (BATCH, SEQ, D_MODEL), 1.0),
        'x_sample': nrm(ks[1], (DEC_BATCH, DEC_SEQ, D_MODEL), 1.0),
        'cache_pool': nrm(ks[2], (L, DEC_BATCH, POOL_BUF, POOL_DIM), 1.0),
        'cache_conv': nrm(ks[3], (L, DEC_BATCH, CONV_WIDTH - 1, CONV_DIM), 1.0),
        'state_delta': nrm(ks[4], (L, DEC_BATCH, N_HEADS, HEAD_DK, HEAD_DV), 0.3),
        'norm1_w': 1.0 + nrm(ks[5], (L, D_MODEL), 0.02),
        'w_in': nrm(ks[6], (L, D_MODEL, IN_DIM), D_MODEL ** -0.5),
        'w_pool': nrm(ks[7], (L, POOL_GROUPS, POOL_GROUP_DIM, POOL_GROUP_DIM), POOL_GROUP_DIM ** -0.5),
        'pool_scale': 1.0 + nrm(ks[8], (L, POOL_DIM), 0.1),
        'w_conv': nrm(ks[9], (L, CONV_WIDTH, CONV_DIM), CONV_WIDTH ** -0.5),
        'a_log': jnp.log(jax.random.uniform(ks[10], (L, N_HEADS), f32, 1.0, 16.0)),
        'dt_bias': jnp.log(jnp.expm1(dt)),
        'o_norm_w': 1.0 + nrm(ks[12], (L, HEAD_DV), 0.02),
        'w_branch_pool': nrm(ks[13], (L, POOL_DIM, D_MODEL), POOL_DIM ** -0.5),
        'w_branch_delta': nrm(ks[14], (L, V_DIM, D_MODEL), V_DIM ** -0.5),
        'w_out': nrm(ks[15], (L, D_MODEL, D_MODEL), D_MODEL ** -0.5),
        'norm2_w': 1.0 + nrm(ks[16], (L, D_MODEL), 0.02),
        'w_router_group': nrm(ks[17], (L, D_MODEL, N_GROUPS), D_MODEL ** -0.5),
        'b_router_group': nrm(ks[18], (L, N_GROUPS), 0.01),
        'w_router_expert': nrm(ks[19], (L, D_MODEL, N_GROUPS, EXPERTS_PER_GROUP), D_MODEL ** -0.5),
        'b_router_expert': nrm(ks[20], (L, N_GROUPS, EXPERTS_PER_GROUP), 0.01),
        'w_gate': nrm(ks[21], (L, N_EXPERTS, D_MODEL, D_EXPERT), D_MODEL ** -0.5),
        'w_up': nrm(ks[22], (L, N_EXPERTS, D_MODEL, D_EXPERT), D_MODEL ** -0.5),
        'w_down': nrm(ks[23], (L, N_EXPERTS, D_EXPERT, D_MODEL), D_EXPERT ** -0.5),
        'final_norm_w': 1.0 + nrm(ks[24], (D_MODEL,), 0.02),
    }

def reference(x_prompt, x_sample, cache_pool, cache_conv, state_delta, norm1_w, w_in, w_pool, pool_scale,
              w_conv, a_log, dt_bias, o_norm_w, w_branch_pool, w_branch_delta, w_out, norm2_w,
              w_router_group, b_router_group, w_router_expert, b_router_expert, w_gate, w_up, w_down,
              final_norm_w):
    B, T = x_prompt.shape[0], x_prompt.shape[1]
    dt = x_prompt.dtype
    xp, xs = x_prompt, x_sample
    pool_p, conv_p, delta_p, pool_s, conv_s, delta_s = [], [], [], [], [], []
    for layer in range(DEPTH):
        lp = (norm1_w[layer], w_in[layer], w_pool[layer], pool_scale[layer], w_conv[layer], a_log[layer],
              dt_bias[layer], o_norm_w[layer], w_branch_pool[layer], w_branch_delta[layer], w_out[layer],
              norm2_w[layer], w_router_group[layer], b_router_group[layer], w_router_expert[layer],
              b_router_expert[layer], w_gate[layer], w_up[layer], w_down[layer])
        xp, pb, cb, sb = trunk_layer(
            xp, jnp.zeros((B, POOL_BUF, POOL_DIM), dt), jnp.zeros((B, CONV_WIDTH - 1, CONV_DIM), dt),
            jnp.zeros((B, N_HEADS, HEAD_DK, HEAD_DV), jnp.float32), 0, min(DELTA_CHUNK, T), *lp)
        pool_p.append(pb)
        conv_p.append(cb)
        delta_p.append(sb)
        xs, pb, cb, sb = trunk_layer(
            xs, cache_pool[layer], cache_conv[layer], state_delta[layer], PAST_LEN, xs.shape[1], *lp)
        pool_s.append(pb)
        conv_s.append(cb)
        delta_s.append(sb)
    y_prompt = rmsnorm(xp, final_norm_w)
    y_sample = rmsnorm(xs, final_norm_w)
    return (y_prompt, y_sample, jnp.stack(pool_p), jnp.stack(conv_p), jnp.stack(delta_p),
            jnp.stack(pool_s), jnp.stack(conv_s), jnp.stack(delta_s))


_drawn_inputs = setup_inputs


def setup_inputs(seed=0):
    import zlib

    import numpy as np

    out = dict(_drawn_inputs(seed))
    spreads = {}
    factors = {'b_router_expert': 5.374, 'final_norm_w': 2.856}
    for name, (base, spread) in spreads.items():
        noise = np.random.default_rng([zlib.crc32(name.encode()), seed]).standard_normal(out[name].shape)
        drawn = base * np.exp(spread * noise) if base else spread * noise
        out[name] = __import__('jax').numpy.asarray(drawn.astype(out[name].dtype))
    for name, factor in factors.items():
        out[name] = (out[name] * factor).astype(out[name].dtype)
    return out
```

```python
from contextlib import ExitStack

import concourse.bass as bass
from concourse import mybir

F32 = mybir.dt.float32
I32 = mybir.dt.int32
U32 = mybir.dt.uint32
ALU = mybir.AluOpType
ACT = mybir.ActivationFunctionType
AX = mybir.AxisListType

P = 128
D = 1024
KD = D // P
TP = 256
BD, TD = 8, 4
TS = BD * TD
T = TP + TS
TILES = [P, P, TS]
NT = len(TILES)
H = 8
DK = 128
NG = 4
PBUF = 15
CW = 4
NQKV = 3 * H
POOL_C, QKV_C = 0, NG * P
AB_C = QKV_C + NQKV * P
Z_C = AB_C + 2 * H
GATE_C = Z_C + H * P
NE, NGR, EPG = 32, 4, 8
FE = 256
CAP = 64
ROUNDS = -(-T // CAP)
PAIRS = NE // 2
TBL = ROUNDS * PAIRS
SKIP = 100000
EPS = 1e-6
SLOT = 8 * 256
RA = 6

PROJ = ([QKV_C + P * c for c in range(NQKV)] + [POOL_C + P * g for g in range(NG)]
        + [Z_C + P * h for h in range(H)] + [GATE_C + P * m for m in range(2 * KD)])
N_V, N_POOL, N_Z, N_GATE, N_PROJ = 2 * H, NQKV, NQKV + NG, NQKV + NG + H, len(PROJ)
IN_ITEMS = N_PROJ // 2
BP_ITEMS, BD_ITEMS, WO_ITEMS = 2, 4, 4
A_ITEMS = IN_ITEMS + BP_ITEMS + BD_ITEMS + WO_ITEMS

ARENA = 50560
CE = CW - 1 + TP
EW = CE + BD * (CW - 1 + TD)
PE0 = PBUF + TP
EPW = PE0 + BD * (PBUF + TD)
NACC = EW - (CW - 1)
RAWC = CE - (CW - 1)
RAWN = EW - RAWC

LEAD_GATES = 6
GATE_AT = {2 * j: N_GATE + LEAD_GATES + j for j in range(2 * KD - LEAD_GATES)}
STATE_AT = {2 * h + 2: h for h in range(H)}
BP_AT = {2 * d + 2: d for d in range(KD)}
KDD_AT, RTD_AT, VND_AT, OD_AT, ODT_AT = 1, 3, 5, 7, 9
OSQ = [n + 1 + (H if n >= ODT_AT - 1 else 0) for n in range(2 * H)]
PEEL = 2


def hybrid_step(nc, x_prompt, x_sample, cache_pool, cache_conv, state_delta, norm1_w, w_in, w_pool,
                pool_scale, w_conv, a_log, dt_bias, o_norm_w, w_branch_pool, w_branch_delta, w_out,
                norm2_w, w_router_group, b_router_group, w_router_expert, b_router_expert, w_gate,
                w_up, w_down, final_norm_w, y_prompt, y_sample, new_pool_prompt, new_conv_prompt,
                new_delta_prompt, new_pool_sample, new_conv_sample, new_delta_sample):
    x_rows = [x_prompt[0, 0:P, :], x_prompt[0, P:TP, :], x_sample.rearrange("b t d -> (b t) d")]
    y_rows = [y_prompt[0, 0:P, :], y_prompt[0, P:TP, :], y_sample.rearrange("b t d -> (b t) d")]

    def dram(name, shape, dt=F32):
        return nc.dram_tensor(name, shape, dt, kind="Internal").ap()

    diag_in = dram("diag_in", (8, 16, 2 * H, 16))
    diag_out = dram("diag_out", (8, 2 * H, 16, 16))
    h2_dram = dram("h2_dram", (T, D))
    tbl_dram = dram("tbl_dram", (P * TBL, 1), I32)
    two_dram = dram("two_dram", (2 * T, D))

    with ExitStack() as ctx:
        def sb(name, shape, dt=F32):
            return ctx.enter_context(nc.sbuf_tensor(name, shape, dt))

        def sem(name):
            return ctx.enter_context(nc.semaphore(name))

        ps = [ctx.enter_context(nc.psum_tensor(f"ps{i}", [P, 512], F32)) for i in range(8)]

        arena = sb("arena", [P, ARENA])

        class Cut:
            def __init__(self, at):
                self.at = at

            def take(self, n, parts=P):
                self.at += n
                assert self.at <= ARENA, self.at
                return arena[0:parts, self.at - n:self.at]

        slots = [arena[:, SLOT * i:SLOT * (i + 1)] for i in range(2 * RA)]

        low = Cut(RA * SLOT)
        AT = low.take(2 * H * P).rearrange("p (g i) -> p g i", i=P)
        X = low.take(2 * H * P).rearrange("p (g i) -> p g i", i=P)
        XT = low.take(2 * H * P).rearrange("p (g i) -> p g i", i=P)
        aqT = low.take(2 * H * P).rearrange("p (g i) -> p g i", i=P)
        Sd = low.take(2 * BD * P).rearrange("p (u b v) -> p u b v", u=2, b=BD)
        rows_d = low.take(4 * H * TS).rearrange("p (r h i) -> p r h i", r=4, h=H)
        rbd_room = low.take(4 * H * TS)
        rbd = rbd_room[0:TS, :].rearrange("p (r h i) -> p r h i", r=4, h=H)
        assert low.at <= 2 * RA * SLOT
        conv_raw = arena[0:BD * (CW - 1), RA * SLOT:RA * SLOT + NQKV * P]
        pool_raw = arena[0:BD * PBUF, RA * SLOT + NQKV * P:RA * SLOT + NQKV * P + NG * P]
        pooled = Sd.rearrange("p u b v -> p (u b v)")[:, 0:NG * T].rearrange("p (g t) -> p g t", g=NG)
        dec = Cut(RA * SLOT)
        Rd = dec.take(H * P, TS).rearrange("p (h e) -> p h e", h=H)
        vnd = dec.take(H * P, TS).rearrange("p (h e) -> p h e", h=H)
        kdd = dec.take(H * P, TS).rearrange("p (h e) -> p h e", h=H)
        St = dec.take(H * P).rearrange("p (h v) -> p h v", h=H)
        vx = [v.rearrange("p (b e) -> p b e", b=BD) for v in
              (Rd.rearrange("p h e -> p (h e)"), St.rearrange("p h v -> p (h v)")[0:TS, :])]
        assert dec.at <= RA * SLOT + 2 * 2 * H * P

        high = Cut(2 * RA * SLOT)
        base_b = high.at
        hT = high.take(KD * T).rearrange("p (k t) -> p k t", k=KD)
        merged = hT
        qkvT = high.take(NQKV * T).rearrange("p (c t) -> p c t", c=NQKV)
        zT = high.take(H * T).rearrange("p (c t) -> p c t", c=H)
        gT = high.take(2 * KD * T).rearrange("p (c t) -> p c t", c=2 * KD)
        xt = gT.rearrange("p c t -> p (c t)")[:, 0:NT * D].rearrange("p (n d) -> p n d", n=NT)
        work0 = high.at
        E = [high.take(EW) for _ in range(3)]
        EP = [high.take(EPW) for _ in range(2)]
        C = [high.take(NACC) for _ in range(2)]
        SQ = [high.take(T) for _ in range(2)]
        wa = [Sd.rearrange("p u b v -> p (u b v)")[:, NG * T + EPW * j:NG * T + EPW * (j + 1)] for j in range(2)]
        work1 = high.at
        stage = high.take(NQKV * P)
        b_end = high.at
        oTok = stage.rearrange("p (n d) -> p n d", n=NT)
        ypT = high.take(NG * T).rearrange("p (g t) -> p g t", g=NG)
        cT = rows_d.rearrange("p r h i -> p (r h i)")[:, 0:NQKV * BD * (CW - 1)].rearrange("p (c r) -> p c r", c=NQKV)
        pcT = rbd_room[:, 0:NG * BD * PBUF].rearrange("p (c r) -> p c r", c=NG)
        RB = high.take(3 * TP).rearrange("p (r t) -> p r t", r=3)
        Dt = high.take(TP)
        egq = high.take(P)
        smallrows = RB[0:109, 0, 0:P]
        smallT = high.take(P)
        ident = high.take(P)
        ones = high.take(P)
        triU = high.take(P)
        lvl = [high.take(P) for _ in range(3)]
        rb_room = RB.rearrange("p r t -> p (r t)")
        wpool = rb_room[:, P:P + NG * P].rearrange("p (g d) -> p g d", g=NG)
        wab = rb_room[:, P + NG * P:P + NG * P + KD * 2 * H].rearrange("p (k n) -> p k n", k=KD)
        wk = Cut(work0)
        Xd = wk.take(256)
        And = wk.take(256)
        prod = wk.take(256)
        egd = wk.take(H * TS).rearrange("p (h i) -> p h i", h=H)
        tmpd = wk.take(H * TS).rearrange("p (h i) -> p h i", h=H)
        Dd = wk.take(H * TS).rearrange("p (h i) -> p h i", h=H)
        Nd = wk.take(H * TS).rearrange("p (h i) -> p h i", h=H)
        IAd = wk.take(H * TS).rearrange("p (h i) -> p h i", h=H)
        N2d = wk.take(H * TS).rearrange("p (h i) -> p h i", h=H)
        aqd = wk.take(H * TS).rearrange("p (h i) -> p h i", h=H)
        TTd = wk.take(H * TS, TS).rearrange("p (h i) -> p h i", h=H)
        assert wk.at <= work1, (wk.at, work1)
        am = [Dt, RB[:, 2, :]]
        Y = [RB[:, 0, :], RB[:, 1, :]]
        rbf = RB.rearrange("p r t -> p (r t)")
        R = [rbf[:, 0:P], rbf[:, P:2 * P]]
        vn = [rbf[:, 2 * P:3 * P], rbf[:, 3 * P:4 * P]]
        kd = [rbf[:, 4 * P:5 * P], rbf[:, 5 * P:6 * P]]
        osq = [prod[:, 0:P], prod[:, P:2 * P]]

        sc = sb("sc", [P, 640])
        scat = [0]

        def scal(*dims):
            n = 1
            for d in dims:
                n *= d
            v = sc[:, scat[0]:scat[0] + n]
            scat[0] += n
            assert scat[0] <= 640
            if len(dims) == 2:
                v = v.rearrange("p (a b) -> p a b", a=dims[0])
            return v

        ss1, rs1 = scal(NT), scal(NT)
        ab = scal(NT, 2 * H)
        beta, g_ = scal(NT, H), scal(NT, H)
        t1, t2, t3, t4 = scal(NT, H), scal(NT, H), scal(NT, H), scal(NT, H)
        Gc, Gl = scal(NT, H), scal(NT, H)
        rqk = scal(NT, 2 * H)
        brk, nber, kds, eGl = scal(NT, H), scal(NT, H), scal(NT, H), scal(NT, H)
        eGd = scal(H, BD)
        oss, orr = scal(NT, H), scal(NT, H)
        gbd = scal(H, BD)
        sb_small = sb("sb_small", [P, 64])
        dtb, alog = sb_small[:, 8:8 + H], sb_small[:, 16:16 + H]
        bmask, invc = sb_small[:, 24:24 + BD], sb_small[:, 32:48]
        U4 = sb("U4", [TS, TS])
        B4 = sb("B4", [TS, TS])
        S4 = sb("S4", [TS, TS])

        qk_at = base_b + KD * T
        b = Cut(qk_at)
        x2 = b.take(NT * D).rearrange("p (n d) -> p n d", n=NT)
        xr = b.take(NT * D).rearrange("p (n d) -> p n d", n=NT)
        h2 = xr
        assert b.at <= qk_at + NQKV * T
        b = Cut(qk_at + NQKV * T)
        n2b = b.take(D)
        fnb = b.take(D)
        h2T = b.take(KD * T).rearrange("p (k t) -> p k t", k=KD)
        xg = [b.take(D) for _ in range(2)]
        xgT_room = b.take(2 * KD * P)
        xgT = [xgT_room[:, KD * P * j:KD * P * (j + 1)].rearrange("p (k t) -> p k t", k=KD) for j in range(2)]
        sg = [b.take(FE) for _ in range(2)]
        act_ = [b.take(FE) for _ in range(2)]
        actT = [b.take(FE).rearrange("p (c t) -> p c t", c=2) for _ in range(2)]
        assert b.at <= b_end, (b.at, b_end)
        b = Cut(base_b)
        dn = [b.take(D) for _ in range(2)]
        assert b.at <= qk_at
        yb = Cut(qk_at + NT * D)
        yg = [yb.take(2 * D), xgT_room[:, 0:2 * D], h2T.rearrange("p k t -> p (k t)")[:, 0:2 * D]]

        wr = sb("wr", [P, KD, 36])
        rb_ = sb("rb_", [P, 36])
        r = sb("r", [P, NT, 36 + 8 * 8 + 7 * 32])
        places = sb("places", [P, NT, 4], I32)
        mi = sb("mi", [P, NT, 16], U32)
        tbl_sb = sb("tbl_sb", [P, TBL], I32)
        put = sb("put", [P, TBL], I32)
        get = sb("get", [P, TBL], I32)
        idc = sb("idc", [P, 4], I32)
        ecst = sb("ecst", [P, 2, NE])
        more_i = sb("more_i", [P, 1], I32)
        strU = sb("strU", [P, P])
        ones_eps = sb_small[:, 0:1]
        RTd, oTd = N2d, IAd
        sdv = ps[7][:, :].rearrange("p (h r t) -> p h r t", h=H, r=2)

        rcat = [0]

        def rcut(*dims):
            n = 1
            for d in dims:
                n *= d
            v = r[:, :, rcat[0]:rcat[0] + n]
            rcat[0] += n
            assert rcat[0] <= r.shape[2]
            return v.rearrange("p t (a b) -> p t a b", a=dims[0]) if len(dims) == 2 else v

        lg, lg8, mx8, les = rcut(NGR + NE), rcut(8), rcut(8), rcut(EPG)
        prodr = rcut(NGR, EPG)
        oh = [rcut(NE), rcut(NE)]
        picks, rk_, prode = rcut(NE), rcut(NE), rcut(NE)
        eg4, ed, gs, goh, eid = rcut(NGR), rcut(1), rcut(1), rcut(NGR), rcut(2)
        pg, w12, rank, rnd, tpos = rcut(1), rcut(2), rcut(2), rcut(2), rcut(2)
        cnt, itf = sb_small[:, 1:2], sb_small[:, 2:3]

        class Sems(dict):
            def __missing__(self, n):
                self[n] = sem(n)
                return self[n]

        S = Sems()
        ring_in = [sem(f"ring_in{i}") for i in range(2 * RA)]

        def item_read(i):
            if i < IN_ITEMS:
                return S["proj"], 2 * i + 2
            i -= IN_ITEMS
            if i < BP_ITEMS:
                return S["bp_pe"], 4 * (i + 1)
            i -= BP_ITEMS
            if i < BD_ITEMS:
                return S["bd_pe"], 2 * (i + 1)
            return S["wo_pe"], NT * (i - BD_ITEMS + 1)

        free = [0] * N_PROJ
        for n in range(N_PROJ):
            free[n] = (free[n - 1] if n else 0) + (2 if n < N_POOL else 3 if n < N_Z else 1)

        block = ctx.enter_context(nc.Block())

        @block.sync
        def _(sp):
            for n in range(NT):
                sp.dma_start(xt[0:TILES[n], n, :], x_rows[n]).then_inc(S["x_in"], 16)
            sp.dma_start(wab, w_in[0, :, AB_C:Z_C].rearrange("(k p) n -> p k n", p=P)).then_inc(S["misc_in"], 16)
            for i in range(A_ITEMS):
                if i >= RA:
                    s, v = item_read(i - RA)
                    sp.wait_ge(s, v)
                to = slots[i % RA]
                if i < IN_ITEMS:
                    c = PROJ[2 * i]
                    src = w_in[0, :, c:c + 256].rearrange("(k p) n -> p k n", p=P)
                elif i < IN_ITEMS + BP_ITEMS:
                    c = 512 * (i - IN_ITEMS)
                    src = w_branch_pool[0, :, c:c + 512].rearrange("(k p) n -> p k n", p=P)
                else:
                    j = i - IN_ITEMS - BP_ITEMS
                    w = w_branch_delta if j < BD_ITEMS else w_out
                    c = 256 * (j % BD_ITEMS)
                    src = w[0, :, c:c + 256].rearrange("(k p) n -> p k n", p=P)
                sp.dma_start(to.rearrange("p (k n) -> p k n", n=src.shape[2]), src).then_inc(ring_in[i % RA], 16)

            def expert_weights(i, u, w):
                for j, (t, ex) in enumerate([(w_gate, 0), (w_up, 0), (w_gate, 1), (w_up, 1), (w_down, 0), (w_down, 1)]):
                    if isinstance(i, int):
                        src = t[0, w + ex]
                        if u == 0:
                            s, v = item_read(A_ITEMS - RA + j)
                            sp.wait_ge(s, v)
                        elif j == 0:
                            sp.wait_ge(S["y_done"], 6)
                            sp.wait_ge(S["sd_out"], 16 * H)
                    else:
                        src = t[0, bass.ds(w + ex, 1)].rearrange("e a b -> (e a) b")
                        if j == 0:
                            sp.wait_ge(S["m_gu"], 2 * i + u - 1)
                        if j == 4:
                            sp.wait_ge(S["m_dn"], 2 * i + u - 1)
                    a = src.shape[0] // P
                    sp.dma_start(slots[RA * u + j].rearrange("p (a n) -> p a n", a=a),
                                 src.rearrange("(p a) n -> p a n", a=a)).then_inc(ring_in[RA * u + j], 16)

            for u in (1, 0):
                expert_weights(0, u, 2 * u)
            sp.wait_ge(S["route"], 1)
            end = sp.value_load(more_i[0:1, 0:1], min_val=0, max_val=(ROUNDS - 1) * PAIRS // 2) + PAIRS // 2
            with sp.Fori(1, end) as i:
                for u in range(2):
                    expert_weights(i, u, (i % (PAIRS // 2)) * 4 + 2 * u)

        @block.gpsimd
        def _(pool):
            chain = [0]

            def link(ins):
                chain[0] += 1
                ins.then_inc(S["pool_chain"], 1)
                pool.wait_ge(S["pool_chain"], chain[0])

            def fill(view, parts, pattern, base, mult, op, keep=1.0, other=0.0):
                link(nc.gpsimd.memset(view, keep))
                link(nc.gpsimd.affine_select(out=view, in_=view, compare_op=op, fill=other, base=base,
                                             pattern=pattern, channel_multiplier=mult))

            fill(ident, P, [[1, P]], 0, -1, ALU.is_equal)
            link(nc.gpsimd.memset(ones, 1.0))
            fill(triU, P, [[1, P]], 0, -1, ALU.is_ge)
            fill(strU[:, :], P, [[1, P]], -1, -1, ALU.is_ge)
            for u in (U4, B4, S4):
                link(nc.gpsimd.memset(u[:, :], 1.0))
                v = u[:, :].rearrange("p (b t) -> p b t", t=TD)
                link(nc.gpsimd.affine_select(out=v, in_=v, compare_op=ALU.is_ge, fill=0.0, base=0,
                                             pattern=[[-TD, BD], [0, TD]], channel_multiplier=1))
                link(nc.gpsimd.affine_select(out=v, in_=v, compare_op=ALU.is_ge, fill=0.0, base=TD - 1,
                                             pattern=[[TD, BD], [0, TD]], channel_multiplier=-1))
            for u, b0 in ((U4, 0), (S4, -1)):
                link(nc.gpsimd.affine_select(out=u[:, :], in_=u[:, :], compare_op=ALU.is_ge, fill=0.0, base=b0,
                                             pattern=[[1, TS]], channel_multiplier=-1))
            for s, m in zip((16, 32, 64), lvl):
                link(nc.gpsimd.memset(m, 0.0))
                for q in range(P // (2 * s)):
                    sub = m[:, 2 * s * q + s:2 * s * (q + 1)]
                    link(nc.gpsimd.memset(sub, 1.0))
                    link(nc.gpsimd.affine_select(out=sub, in_=sub, compare_op=ALU.is_ge, fill=0.0,
                                                 base=-2 * s * q, pattern=[[0, s]], channel_multiplier=1))
                    link(nc.gpsimd.affine_select(out=sub, in_=sub, compare_op=ALU.is_ge, fill=0.0,
                                                 base=2 * s * q + s - 1, pattern=[[0, s]], channel_multiplier=-1))
            link(nc.gpsimd.memset(bmask, 1.0))
            link(nc.gpsimd.affine_select(out=bmask, in_=bmask, compare_op=ALU.is_ge, fill=0.0, base=0,
                                         pattern=[[-TD, BD]], channel_multiplier=1))
            link(nc.gpsimd.affine_select(out=bmask, in_=bmask, compare_op=ALU.is_ge, fill=0.0, base=TD - 1,
                                         pattern=[[TD, BD]], channel_multiplier=-1))
            link(nc.gpsimd.iota(invc, pattern=[[1, 16]], base=1, channel_multiplier=0,
                                allow_small_or_imprecise_dtypes=True))
            link(nc.gpsimd.iota(ecst[:, 0, :], pattern=[[1, NE]], base=0, channel_multiplier=0,
                                allow_small_or_imprecise_dtypes=True))
            link(nc.gpsimd.iota(ecst[:, 1, :].rearrange("p (a b) -> p a b", b=2),
                                pattern=[[1, PAIRS], [CAP * TBL, 2]], base=0, channel_multiplier=0,
                                allow_small_or_imprecise_dtypes=True))
            link(nc.gpsimd.iota(places[:, :, 2:4], pattern=[[2 * P, NT], [1, 2]], base=0, channel_multiplier=2))
            nc.gpsimd.iota(tbl_sb[:, :], pattern=[[1, TBL]], base=SKIP, channel_multiplier=TBL).then_inc(S["masks"], 1)
            pool.wait_ge(S["masks"], 1)
            pool.dma_start(tbl_dram.rearrange("(p g) o -> p (g o)", p=P), tbl_sb[:, :]).then_inc(S["tbl"], 16)
            for e in E:
                link(nc.gpsimd.memset(e[:, 0:CW - 1], 0.0))
            for e in EP:
                ins = nc.gpsimd.memset(e[:, 0:PBUF], 0.0)
                if e is EP[0]:
                    link(ins)
            ins.then_inc(S["pads"], 1)
            pool.wait_ge(S["small_ev"], 4)
            for n in range(NQKV):
                if n >= 3:
                    pool.wait_ge(S["conv"], n - 2)
                    pool.wait_ge(S["raw_t"], n - 2)
                nc.gpsimd.tensor_copy(
                    E[n % 3][:, CE:EW].rearrange("p (b r) -> p b r", b=BD)[:, :, 0:CW - 1],
                    cT[:, n, :].rearrange("p (b r) -> p b r", b=BD)).then_inc(S["e_cache"], 1)
            for g in range(NG):
                if g >= 2:
                    pool.wait_ge(S["pool_dve"], g - 1)
                    pool.wait_ge(S["newp_t"], g - 1)
                nc.gpsimd.tensor_copy(
                    EP[g % 2][:, PE0:EPW].rearrange("p (b r) -> p b r", b=BD)[:, :, 0:PBUF],
                    pcT[:, g, :].rearrange("p (b r) -> p b r", b=BD)).then_inc(S["e_cache"], 1)
            nc.gpsimd.memset(X, 0.0).then_inc(S["memsets"], 1)
            pool.wait_ge(S["pool_dve"], NG)
            pool.wait_ge(S["newp_t"], NG)
            link(nc.gpsimd.memset(Xd, 0.0))
            xd = Xd.rearrange("p (i c) -> p i c", i=16)
            nc.gpsimd.affine_select(out=xd, in_=xd, compare_op=ALU.not_equal, fill=1.0, base=0,
                                    pattern=[[1, 16], [-1, 16]], channel_multiplier=0).then_inc(S["memsets"], 1)
            pool.wait_ge(S["prep_done"], H)
            for m in range(8):
                pool.dma_start(diag_in[m], AT[16 * m:16 * m + 16, :, 16 * m:16 * m + 16]).then_inc(S["diag"], 16)
            pool.wait_ge(S["diag"], 16 * 8)
            for m in range(8):
                pool.dma_start(And[16 * m:16 * m + 16, :].rearrange("g (j i) -> g j i", i=16),
                               diag_in[m].rearrange("j g i -> g j i")).then_inc(S["diag"], 16)
            pool.wait_ge(S["sub_done"], 1)
            pool.dma_start(diag_out.rearrange("m g i c -> (m g) (i c)"), Xd).then_inc(S["diag"], 16)
            pool.wait_ge(S["diag"], 16 * 16 + 16)
            pool.wait_ge(S["memsets"], 1)
            for m in range(8):
                pool.dma_start(X[16 * m:16 * m + 16, :, 16 * m:16 * m + 16],
                               diag_out[m].rearrange("g i c -> i g c")).then_inc(S["diag"], 16)

            for h in range(H):
                pool.wait_ge(S[f"s2_in{h % 2}"], 16 * (h // 2 + 1))
                nc.gpsimd.tensor_tensor(Sd[:, h % 2], Sd[:, h % 2],
                                        eGd[:, h, :].unsqueeze(2).to_broadcast([P, BD, P]),
                                        ALU.mult).then_inc(S["sd_mul"], 1)

            pool.wait_ge(S["route"], 1)
            pool.wait_ge(S["tbl"], 16)
            for n in range(NT):
                for k in range(2):
                    pool.indirect_dma_start(
                        out=tbl_dram[:, :], out_offset=bass.IndirectOffsetOnAxis(ap=places[0:TILES[n], n, k:k + 1], axis=0),
                        in_=places[0:TILES[n], n, 2 + k:3 + k], in_offset=None).then_inc(S["tbl"], 16)
            pool.wait_ge(S["tbl"], 16 + 16 * 2 * NT)
            pool.dma_start(put[:, :], tbl_dram.rearrange("(p g) o -> p (g o)", p=P)).then_inc(S["tbl"], 16)
            for u in range(2):
                link(nc.gpsimd.memset(xg[u], 0.0))
            pool.wait_ge(S["get_done"], 1)
            pool.wait_ge(S["h2_out"], 16 * NT)
            last_row = pool.alloc_register("last_row")
            pool.reg_mov(last_row, T - 1)
            last_two = pool.alloc_register("last_two")
            pool.reg_mov(last_two, 2 * T - 1)

            def column(table, p, to, n):
                src = table[:, p:p + 1] if isinstance(p, int) else table[:, bass.ds(p, 1)]
                nc.gpsimd.tensor_copy(idc[:, to:to + 1], src).then_inc(S["idc_done"], 1)
                pool.wait_ge(S["idc_done"], n)
                pool.sem_inc(S["idc_seen"], 1)

            def gather(p, u, n):
                if not isinstance(p, int) or p >= 2:
                    pool.wait_ge(S["m_T"], p - 1)
                column(get, p, u, n)
                pool.indirect_dma_start(
                    out=xg[u], out_offset=None, in_=h2_dram[:, :],
                    in_offset=bass.IndirectOffsetOnAxis(ap=idc[:, u:u + 1], axis=0),
                    bounds_check=last_row, oob_is_err=False).then_inc(S[f"gather{u}"], 16)

            def scatter(q, v, n):
                pool.wait_ge(S["m_dnA"], q + 1)
                pool.wait_ge(S["m_dnV"], q + 1)
                column(put, q, 2 + v, n)
                pool.indirect_dma_start(
                    out=two_dram[:, :], out_offset=bass.IndirectOffsetOnAxis(ap=idc[:, 2 + v:3 + v], axis=0),
                    in_=dn[v], in_offset=None,
                    bounds_check=last_two, oob_is_err=False).then_inc(S[f"dn_out{v}"], 16)

            for p in range(2 * PEEL):
                gather(p, p % 2, p + 1 if p < 3 else 2 * p - 2)
                if p >= 3:
                    scatter(p - 3, (p - 3) % 2, 2 * p - 1)
            end = pool.value_load(more_i[0:1, 0:1], min_val=0, max_val=(ROUNDS - 1) * PAIRS // 2) + PAIRS // 2
            with pool.Fori(PEEL, end) as i:
                for u in range(2):
                    gather(2 * i + u, u, i * 4 + (2 * u - 2))
                    scatter(2 * i + (u - 3), 1 - u, i * 4 + (2 * u - 1))
            for j in (3, 2, 1):
                scatter(end * 2 - j, j % 2, end * 4 + (1 - j))

        @block.scalar
        def _(act):
            chain = [0]

            def link(ins):
                chain[0] += 1
                ins.then_inc(S["act_chain"], 1)
                act.wait_ge(S["act_chain"], chain[0])

            for a, rows in ((w_conv[0].rearrange("j (c p) -> (j c) p", p=P), (0, 96)),
                            (norm1_w[0].rearrange("(k p) -> k p", p=P), (96, 104)),
                            (pool_scale[0].rearrange("(k p) -> k p", p=P), (104, 108)),
                            (o_norm_w, (108, 109))):
                act.dma_start(smallrows[rows[0]:rows[1], :], a).then_inc(S["small_in"], 16)
            act.dma_start(conv_raw, cache_conv[0].rearrange("b r c -> (b r) c")).then_inc(S["cache_in"], 16)
            act.dma_start(pool_raw, cache_pool[0].rearrange("b r c -> (b r) c")).then_inc(S["cache_in"], 16)
            for to, src in ((dtb, dt_bias.partition_broadcast(P).rearrange("p a b -> p (a b)")),
                            (alog, a_log.partition_broadcast(P).rearrange("p a b -> p (a b)")),
                            (wpool, w_pool[0].rearrange("g c d -> c g d")),
                            (wr[:, :, 0:NGR], w_router_group[0].rearrange("(p k) g -> p k g", k=KD)),
                            (wr[:, :, NGR:NGR + NE], w_router_expert[0].rearrange("(p k) g e -> p k (g e)", k=KD)),
                            (rb_[:, 0:NGR], b_router_group.partition_broadcast(P).rearrange("p a b -> p (a b)")),
                            (rb_[:, NGR:NGR + NE], b_router_expert.partition_broadcast(P).rearrange("p a b c -> p (a b c)"))):
                act.dma_start(to, src).then_inc(S["misc_in"], 16)
            act.dma_start(new_pool_sample[0, :, 0:PBUF - TD, :], cache_pool[0, :, TD:PBUF, :]).then_inc(S["out_dma"], 16)

            def load_state(h, again):
                act.dma_start(Sd[:, h % 2], state_delta[0, :, h].rearrange("b k v -> k b v")).then_inc(
                    S[f"s{'2' if again else ''}_in{h % 2}"], 16)

            act.wait_ge(S["x_in"], 16 * NT)
            act.wait_ge(S["sc_one"], 1)
            for n, m in enumerate(TILES):
                nc.scalar.activation(hT.rearrange("p k t -> p (k t)")[0:m, 0:D], xt[0:m, n, :], ACT.Square,
                                     accum_out=ss1[0:m, n:n + 1]).then_inc(S["sq_sum"], 1)
                act.wait_ge(S["sq_sum"], n + 1)
            act.wait_ge(S["mean_sq"], 1)
            nc.scalar.activation(rs1, rs1, ACT.Sqrt).then_inc(S["root"], 1)

            act.wait_ge(S["ab_ev"], 1)
            nc.scalar.activation(t2, t2, ACT.Exp, scale=-1.0).then_inc(S["soft"], 1)
            nc.scalar.activation(beta, ab[:, :, 0:H], ACT.Exp, scale=-1.0).then_inc(S["soft"], 1)
            nc.scalar.activation(alog, alog, ACT.Exp).then_inc(S["soft"], 1)
            act.wait_ge(S["ab_ev"], 2)
            nc.scalar.activation(t3, t4, ACT.Ln).then_inc(S["soft"], 1)

            def evac(n):
                act.wait_ge(S["proj"], n + 1)
                src = ps[n % 2]
                if n < NQKV:
                    if n >= 3:
                        act.wait_ge(S["conv"], n - 2)
                        act.wait_ge(S["raw_t"], n - 2)
                    else:
                        act.wait_ge(S["pads"], 1)
                    dst, at, lead, w = E[n % 3], CW - 1, CE, CW - 1
                elif n < N_Z:
                    g = n - NQKV
                    if g >= 2:
                        act.wait_ge(S["pool_dve"], g - 1)
                        act.wait_ge(S["newp_t"], g - 1)
                    dst, at, lead, w = EP[g % 2], PBUF, PE0, PBUF
                if n < N_Z:
                    nc.scalar.activation(dst[:, at:at + TP], src[:, 0:TP], ACT.Copy).then_inc(S["proj_free"], 1)
                    nc.scalar.activation(dst[:, lead:].rearrange("p (b r) -> p b r", b=BD)[:, :, w:],
                                         src[:, TP:T].rearrange("p (b t) -> p b t", b=BD),
                                         ACT.Copy).then_inc(S["proj_free"], 1)
                    if n >= N_POOL:
                        nc.scalar.activation(C[n % 2][:, 0:TS], src[:, TP:T], ACT.Copy).then_inc(S["proj_free"], 1)
                elif n < N_GATE:
                    nc.scalar.activation(zT[:, n - N_Z, :], src[:, 0:T], ACT.Silu).then_inc(S["proj_free"], 1)
                else:
                    nc.scalar.activation(gT[:, n - N_GATE, :], src[:, 0:T], ACT.Tanh, scale=0.5).then_inc(S["proj_free"], 1)

            def silu(n):
                act.wait_ge(S["conv"], n + 1)
                nc.scalar.activation(qkvT[:, n, 0:TP], C[n % 2][:, 0:TP], ACT.Silu).then_inc(S["silu"], 1)
                nc.scalar.activation(qkvT[:, n, TP:T - TD].rearrange("p (b t) -> p b t", t=TD),
                                     C[n % 2][:, CE:CE + 7 * (BD - 1)].rearrange("p (b t) -> p b t", t=7)[:, :, 0:TD],
                                     ACT.Silu).then_inc(S["silu"], 1)
                nc.scalar.activation(qkvT[:, n, T - TD:T], C[n % 2][:, NACC - TD:NACC], ACT.Silu).then_inc(S["silu"], 1)
                if n < N_V:
                    if n >= 2:
                        act.wait_ge(S["ssd"], n - 1)
                    act.wait_ge(S["silu"], 3 * n + 3)
                    nc.scalar.activation(SQ[n % 2], qkvT[:, n, :], ACT.Square).then_inc(S["sqd"], 1)

            def raw_rows(j):
                act.wait_ge(S["raw_t"], 4 * j + 4)
                nc.scalar.activation(stage[0:RAWN, 512 * j:512 * j + 512], ps[2 + j % 2][0:RAWN, :],
                                     ACT.Copy).then_inc(S["raw_ev"], 1)

            for n in range(NQKV):
                evac(n)
                if n >= 1:
                    silu(n - 1)
                if n == 3:
                    act.wait_ge(S["g_scal"], 1)
                    nc.scalar.activation(t1, Gc, ACT.Exp).then_inc(S["g_exp"], 1)
                    nc.scalar.activation(kds, kds, ACT.Exp).then_inc(S["g_exp"], 1)
                    nc.scalar.activation(eGl, Gl, ACT.Exp).then_inc(S["g_exp"], 1)
                    nc.scalar.activation(eGd, eGd, ACT.Exp).then_inc(S["g_exp"], 1)
                if n % 4 == 1 and n >= 5:
                    raw_rows(n // 4 - 1)
                if n == N_V + 2:
                    act.wait_ge(S["ss_sc"], 1)
                    nc.scalar.activation(rqk, rqk, ACT.Sqrt).then_inc(S["ss_sqrt"], 1)
            silu(NQKV - 1)
            raw_rows(NQKV // 4 - 1)
            act.wait_ge(S["raw_ev"], NQKV // 4)
            act.dma_start(new_conv_prompt[0, 0], stage[0:CW - 1, :]).then_inc(S["stage_out"], 16)
            for b_ in range(BD):
                at = CW - 1 + 7 * b_ + TD
                act.dma_start(new_conv_sample[0, b_], stage[at:at + CW - 1, :]).then_inc(S["stage_out"], 16)

            def rows_exp(h):
                act.wait_ge(S["dt"], 2 * h + 2)
                nc.scalar.activation(egq, ps[3][:, P:TP], ACT.Exp).then_inc(S["expd"], 1)
                nc.scalar.activation(Dt, Dt, ACT.Exp).then_inc(S["expd"], 1)

            def pool_rows(g):
                act.wait_ge(S["wp_pe"], g + 1)
                nc.scalar.activation(ypT[:, g, :], ps[7][:, 0:T], ACT.Copy,
                                     scale=smallT[:, 104 + g:105 + g]).then_inc(S["wp_ev"], 1)

            for n in range(N_POOL, N_Z):
                evac(n)
            act.wait_ge(S["stage_out"], 16 * (1 + BD))
            act.wait_ge(S["newp_t"], NG)
            nc.scalar.activation(stage[0:PBUF, 0:512], ps[2][0:PBUF, :], ACT.Copy).then_inc(S["newp_ev"], 1)
            nc.scalar.activation(stage[0:TS, 512:1024], ps[6][0:TS, :], ACT.Copy).then_inc(S["newp_ev"], 1)
            act.wait_ge(S["newp_ev"], 2)
            act.dma_start(new_pool_prompt[0, 0], stage[0:PBUF, 0:512]).then_inc(S["newo"], 16)
            for b_ in range(BD):
                act.dma_start(new_pool_sample[0, b_, PBUF - TD:PBUF, :],
                              stage[TD * b_:TD * b_ + TD, 512:1024]).then_inc(S["newo"], 16)
            for g in range(NG):
                pool_rows(g)
            for h in range(H):
                rows_exp(h)
                evac(N_Z + h)

            act.wait_ge(S["decrows"], 1)
            rows_f = rows_d.rearrange("p r h i -> p (r h i)")
            nc.scalar.activation(rows_f[:, 0:512], ps[3][:, :], ACT.Copy).then_inc(S["dec_act"], 1)
            nc.scalar.activation(rows_f[:, 512:1024], ps[4][:, :], ACT.Copy).then_inc(S["dec_act"], 1)
            act.wait_ge(S["dec_act"], 1)
            nc.scalar.activation(egd, rows_d[:, 0], ACT.Exp).then_inc(S["dec_act"], 1)
            act.wait_ge(S["decdve"], 1)
            nc.scalar.activation(Dd[0:TS], Dd[0:TS], ACT.Exp).then_inc(S["dec_act"], 1)
            for h in range(2):
                load_state(h, False)
            for n in range(N_GATE, N_GATE + LEAD_GATES):
                evac(n)

            for j in range(4):
                act.wait_ge(S["xt_pe"], j + 1)
                nc.scalar.activation(XT[:, 4 * j:4 * j + 4, :].rearrange("p g i -> p (g i)"), ps[2 + j][:, :],
                                     ACT.Copy).then_inc(S["xt_ev"], 1)
            for n in range(3 * H):
                if n in GATE_AT:
                    evac(GATE_AT[n])
                act.wait_ge(S["y_pe"], n + 1)
                if n >= 2:
                    act.wait_ge(S["xx_pe"], n - 1)
                nc.scalar.activation(Y[n % 2], ps[2 + n % 2][:, 0:TP], ACT.Copy).then_inc(S["y_ev"], 1)
                if n - 1 in STATE_AT:
                    h = STATE_AT[n - 1]
                    act.wait_ge(S["sd_pe"], h + 1)
                    load_state((h + 2) % H, h + 2 >= H)

            def scan_vn(n):
                act.wait_ge(S["vn_pe"], n + 1)
                if n >= 2:
                    act.wait_ge(S["s_pe"], n - 1)
                nc.scalar.activation(vn[n % 2], ps[4][:, 0:P], ACT.Copy).then_inc(S["vn_ev"], 1)

            squares = [0]

            def o_square(src, t, h):
                n, m = squares[0], TILES[t]
                squares[0] += 1
                if n >= 2:
                    act.wait_ge(S["osq"], n - 1)
                nc.scalar.activation(osq[n % 2][0:m], src, ACT.Square,
                                     accum_out=oss[0:m, t, h:h + 1]).then_inc(S["osq"], 1)

            def scan_o(n):
                c, h = divmod(n, H)
                act.wait_ge(S["o_pe"], n + 1)
                src = ps[6][:, 0:P]
                nc.scalar.activation(oTok[:, c, h * P:(h + 1) * P], src, ACT.Copy).then_inc(S["oev"], 1)
                o_square(src, c, h)

            act.wait_ge(S["newo"], 16 * (1 + BD))
            for n in range(2 * H + 1):
                if n in (RTD_AT, VND_AT, ODT_AT):
                    done, to, ev = {RTD_AT: ("rtd_t", Rd, "rtd_ev"), VND_AT: ("vnd_pe", vnd, "vnd_ev"),
                                    ODT_AT: ("od_t", None, "od_ev")}[n]
                    act.wait_ge(S[done], 1)
                    for j in range(2):
                        dst = oTok[0:TS, 2, 512 * j:512 * j + 512] if to is None else to[:, 4 * j:4 * j + 4, :].rearrange("p h e -> p (h e)")
                        nc.scalar.activation(dst, ps[5 + 2 * j][0:TS, :], ACT.Copy).then_inc(S[ev], 1)
                    if n == ODT_AT:
                        for h in range(H):
                            o_square(ps[5 + 2 * (h // 4)][0:TS, P * (h % 4):P * (h % 4) + P], 2, h)
                if n < 2 * H:
                    scan_vn(n)
                if n >= 1:
                    scan_o(n - 1)
            act.wait_ge(S["s_ev"], 2 * H)
            act.dma_start(new_delta_prompt[0, 0].rearrange("h k v -> k h v"), St).then_inc(S["out_dma"], 16)

            act.wait_ge(S["mean_sq"], 1 + 1)
            nc.scalar.activation(orr, orr, ACT.Sqrt).then_inc(S["root"], 1)

            for h in range(H):
                act.wait_ge(S["sdn_dve"], 2 * h + 2)
                act.dma_start(new_delta_sample[0, :, h].rearrange("b k v -> k b v"), Sd[:, h % 2]).then_inc(S["sd_out"], 16)
                if h + 2 < H:
                    act.wait_ge(S["sd_out"], 16 * (h + 1))
                    load_state(h + 2, True)

            act.wait_ge(S["y_done"], 6)
            for n, m in enumerate(TILES):
                act.dma_start(xr[0:m, n, :], x_rows[n]).then_inc(S["xr_in"], 16)
            act.wait_ge(S["bd_dve"], KD)
            act.dma_start(n2b, norm2_w.partition_broadcast(P).rearrange("p a b -> p (a b)")).then_inc(S["nb_in"], 16)
            act.dma_start(fnb, final_norm_w.partition_broadcast(P)).then_inc(S["nb_in"], 16)

            act.wait_ge(S["wo_dve"], NT * WO_ITEMS)
            for n, m in enumerate(TILES):
                nc.scalar.activation(xg[n % 2][0:m, :], x2[0:m, n, :], ACT.Square,
                                     accum_out=ss1[0:m, n:n + 1]).then_inc(S["sq_sum"], 1)
                act.wait_ge(S["sq_sum"], NT + n + 1)
            act.wait_ge(S["mean_sq"], 2 + 1)
            nc.scalar.activation(rs1, rs1, ACT.Sqrt).then_inc(S["root"], 1)
            for n, m in enumerate(TILES):
                act.wait_ge(S["h2_dve"], 1 + n)
                act.dma_start(h2_dram[P * n:P * n + m, :], h2[0:m, n, :]).then_inc(S["h2_out"], 16)
            for j in range(2):
                for t, m in enumerate(TILES):
                    act.wait_ge(S["h2_t"], NT * j + t + 1)
                    nc.scalar.activation(h2T[:, 4 * j:4 * j + 4, P * t:P * t + m],
                                         ps[NT * j + t][:, 0:4 * m].rearrange("p (k t) -> p k t", k=4),
                                         ACT.Copy).then_inc(S["h2_ev"], 1)
            act.wait_ge(S["rt_d"], 1)
            nc.scalar.activation(eg4, eg4, ACT.Exp).then_inc(S["rt_e"], 1)
            act.wait_ge(S["rt_d"], 2)
            nc.scalar.activation(ed, ed, ACT.Exp).then_inc(S["rt_e"], 1)
            act.wait_ge(S["route"], 1)

            def wait_from(s, v):
                if not isinstance(v, int) or v >= 1:
                    act.wait_ge(s, v)

            def results(q, v, cnt):
                act.wait_ge(S["m_dn"], q + 1)
                wait_from(S[f"dn_out{v}"], cnt * 16)
                nc.scalar.activation(dn[v][:, 0:512], ps[5][:, :], ACT.Copy).then_inc(S["m_dnA"], 1)

            def act_rows(q, v):
                act.wait_ge(S["m_aT"], q + 1)
                nc.scalar.activation(actT[v].rearrange("p c t -> p (c t)"), ps[4][:, 0:FE], ACT.Copy).then_inc(S["m_aTev"], 1)

            def pair(i, u):
                p = 2 * i + u
                before = not isinstance(p, int) or p >= 1
                act.wait_ge(S["m_T"], p + 1)
                nc.scalar.activation(xgT[u][:, 4:8, :].rearrange("p k t -> p (k t)"), ps[1][:, :],
                                     ACT.Copy).then_inc(S["m_TevA"], 1)
                if before:
                    act_rows(p - 1, 1 - u)
                act.wait_ge(S["m_gu"], p + 1)
                wait_from(S["m_act"], p - 1)
                nc.scalar.activation(sg[u], ps[2 + u][:, 0:FE], ACT.Silu).then_inc(S["m_sg"], 1)
                if before:
                    results(p - 1, 1 - u, i if u else i - 1)

            for i in range(PEEL):
                for u in range(2):
                    pair(i, u)
            end = act.value_load(more_i[0:1, 0:1], min_val=0, max_val=(ROUNDS - 1) * PAIRS // 2) + PAIRS // 2
            with act.Fori(PEEL, end) as i:
                for u in range(2):
                    pair(i, u)
            act_rows(2 * end - 1, 1)
            results(2 * end - 1, 1, end - 1)

            for v in range(2):
                act.wait_ge(S[f"dn_out{v}"], end * 16)
            for n, m in enumerate(TILES):
                act.dma_start(yg[n][0:m, :], two_dram[2 * P * n:2 * P * n + 2 * m, :].rearrange("(p k) d -> p (k d)", k=2)).then_inc(S["fin_in"], 16)

            for n, m in enumerate(TILES):
                act.wait_ge(S["fin_sum"], n + 1)
                nc.scalar.activation(xg[n % 2][0:m, :], x2[0:m, n, :], ACT.Square,
                                     accum_out=ss1[0:m, n:n + 1]).then_inc(S["sq_sum"], 1)
                act.wait_ge(S["sq_sum"], 2 * NT + n + 1)
            act.wait_ge(S["mean_sq"], 3 + 1)
            nc.scalar.activation(rs1, rs1, ACT.Sqrt).then_inc(S["root"], 1)
            for n, m in enumerate(TILES):
                act.wait_ge(S["fin_y"], 1 + n)
                act.dma_start(y_rows[n], x2[0:m, n, :]).then_inc(S["yout"], 16)
            act.wait_ge(S["yout"], 16 * NT)
            act.wait_ge(S["sd_out"], 16 * H)
            act.wait_ge(S["out_dma"], 32)

        @block.tensor
        def _(pe):
            mm = nc.tensor.matmul

            def flip(out, in_, m):
                return nc.tensor.transpose(out, in_, ident[0:m, 0:m])

            pe.wait_ge(S["masks"], 1)
            pe.wait_ge(S["small_in"], 16 * 4)
            flip(ps[2][:, 0:109], smallrows, 109).then_inc(S["small_t"], 1)
            pe.wait_ge(S["cache_in"], 32)
            for c in range(NQKV):
                last = flip(ps[3 + c // 12][:, 24 * (c % 12):24 * (c % 12) + 24], conv_raw[:, c * P:(c + 1) * P], 24)
                if c % 12 == 11:
                    last.then_inc(S["small_t"], 1)
            for g in range(NG):
                last = flip(ps[5][:, 120 * g:120 * g + 120], pool_raw[:, g * P:(g + 1) * P], 120)
            last.then_inc(S["small_t"], 1)
            XB = [6, 7, 0, 1, 2, 3]
            for t, m in enumerate(TILES):
                pe.wait_ge(S["xn"], t + 1)
                for j in range(2):
                    if 2 * t + j == 4:
                        pe.wait_ge(S["small_ev"], 4)
                    for q in range(4):
                        k = 4 * j + q
                        last = flip(ps[XB[2 * t + j]][:, q * m:(q + 1) * m], xt[0:m, t, k * P:(k + 1) * P], m)
                    last.then_inc(S["x_t"], 1)
            pe.wait_ge(S["ht_done"], 6)
            pe.wait_ge(S["misc_in"], 16 * 8)
            for t, m in enumerate(TILES):
                for k in range(KD):
                    last = mm(ps[6][0:m, 16 * t:16 * t + 16], hT[:, k, P * t:P * t + m], wab[:, k, :],
                              start=(k == 0), stop=(k == KD - 1))
            last.then_inc(S["pe_ab"], 1)

            def proj(n):
                item = n // 2
                if n % 2 == 0:
                    pe.wait_ge(ring_in[item % RA], 16 * (item // RA + 1))
                if n >= 2:
                    pe.wait_ge(S["proj_free"], free[n - 2])
                w = slots[item % RA].rearrange("p (k n) -> p k n", k=KD)
                for k in range(KD):
                    last = mm(ps[n % 2][:, 0:T], w[:, k, P * (n % 2):P * (n % 2) + P], hT[:, k, :],
                              start=(k == 0), stop=(k == KD - 1))
                last.then_inc(S["proj"], 1)

            def squares(n):
                pe.wait_ge(S["sqd"], n + 1)
                for t, m in enumerate(TILES):
                    last = mm(ps[7][0:m, 16 * t + n:16 * t + n + 1], SQ[n % 2][:, P * t:P * t + m], ones[:, 0:1],
                              start=True, stop=True)
                last.then_inc(S["ssd"], 1)

            def raw_flip(n):
                pe.wait_ge(S["proj_free"], free[n])
                pe.wait_ge(S["e_cache"], n + 1)
                j = n // 4
                if n % 4 == 0 and j >= 2:
                    pe.wait_ge(S["raw_ev"], j - 1)
                flip(ps[2 + j % 2][0:RAWN, P * (n % 4):P * (n % 4) + P], E[n % 3][:, RAWC:EW], P).then_inc(S["raw_t"], 1)

            for n in range(NQKV + 1):
                if n < NQKV:
                    proj(n)
                if n == 1:
                    pe.wait_ge(S["g_done"], 1)
                    for t in range(2):
                        mm(ps[6][:, 64 + 8 * t:72 + 8 * t], triU, g_[:, t], start=True, stop=True)
                        mm(ps[6][:, 96 + 8 * t:104 + 8 * t], ones, g_[:, t], start=True, stop=True)
                    mm(ps[6][0:TS, 80:88], U4[:, :], g_[0:TS, 2], start=True, stop=True)
                    mm(ps[6][0:TS, 112:120], B4[:, :], g_[0:TS, 2], start=True, stop=True)
                    mm(ps[6][:, 128:192], ones[0:TS, :], gbd[0:TS].rearrange("p h b -> p (h b)"),
                       start=True, stop=True).then_inc(S["pe_G"], 1)
                if n >= 1:
                    raw_flip(n - 1)
                if n >= 2 and n - 2 < N_V:
                    squares(n - 2)

            def new_pool(g):
                pe.wait_ge(S["proj_free"], free[N_POOL + g])
                if g == 0:
                    pe.wait_ge(S["raw_ev"], NQKV // 4)
                    pe.wait_ge(S["g_scal"], 1)
                flip(ps[2][0:PBUF, g * P:(g + 1) * P], EP[g % 2][:, TP:TP + PBUF], P)
                flip(ps[6][0:TS, g * P:(g + 1) * P], C[g % 2][:, 0:TS], P).then_inc(S["newp_t"], 1)

            def pool_mix(g):
                pe.wait_ge(S["pool_dve"], g + 1)
                if g == 0:
                    pe.wait_ge(S["ss_sc"], 1)
                else:
                    pe.wait_ge(S["wp_ev"], g)
                mm(ps[7][:, 0:T], wpool[:, g, :], pooled[:, g, :], start=True, stop=True).then_inc(S["wp_pe"], 1)

            for g in range(NG):
                proj(N_POOL + g)
                if g >= 1:
                    new_pool(g - 1)
            new_pool(NG - 1)
            for g in range(NG):
                pool_mix(g)

            def prep(h):
                pe.wait_ge(S["rb"], 3 * h + 3)
                if h >= 1:
                    pe.wait_ge(S["prep_done"], h)
                mm(ps[3][:, 0:TP], ones, RB[:, 0, :], start=True, stop=True)
                mm(ps[3][:, TP:2 * TP], ones, RB[:, 1, :], start=True, stop=True)
                mm(ps[4][:, 0:TP], ones, RB[:, 2, :], start=True, stop=True).then_inc(S["rows"], 1)
                for c in range(2):
                    last = mm(ps[5][:, TP * c:TP * c + TP].rearrange("p (r t) -> p r t", r=2),
                              qkvT[:, H + h, P * c:P * c + P], qkvT[:, h:h + H + 1:H, P * c:P * c + P],
                              start=True, stop=True)
                last.then_inc(S["qk_pe"], 1)

            pe.wait_ge(S["silu"], 3 * NQKV)
            for h in range(H):
                proj(N_Z + h)
                prep(h)

            pe.wait_ge(S["decrb"], 4)
            pe.wait_ge(S["prep_done"], H)
            for r_ in range(4):
                last = mm(ps[3 + r_ // 2][:, TP * (r_ % 2):TP * (r_ % 2) + TP], ones[0:TS, :],
                          rbd[:, r_].rearrange("p h i -> p (h i)"), start=True, stop=True)
            last.then_inc(S["decrows"], 1)
            d5 = ps[5][0:TS, :].rearrange("p (h r t) -> p h r t", h=H, r=2)
            for h in range(H):
                last = mm(d5[:, h], qkvT[:, H + h, TP:T], qkvT[:, h:h + H + 1:H, TP:T], start=True, stop=True)
            last.then_inc(S["decqk"], 1)

            for n in range(N_GATE, N_GATE + LEAD_GATES):
                proj(n)
                if n == N_GATE + 1:
                    pe.wait_ge(S["decdve"], 3)
                    for h in range(H):
                        last = flip(ps[6][0:TS, TS * h:TS * h + TS], Nd[0:TS, h, :], TS)
                    last.then_inc(S["dinv_pe"], 1)
                if n == N_GATE + 2:
                    pe.wait_ge(S["dinv_dve"], 1)
                    for h in range(H):
                        last = mm(ps[7][0:TS, TS * h:TS * h + TS], tmpd[0:TS, h, :], Nd[0:TS, h, :], start=True, stop=True)
                    last.then_inc(S["dinv_pe"], 1)
                if n == N_GATE + 3:
                    pe.wait_ge(S["dinv_dve"], 3)
                    for h in range(H):
                        last = mm(ps[6][0:TS, TS * h:TS * h + TS], IAd[0:TS, h, :], N2d[0:TS, h, :], start=True, stop=True)
                    last.then_inc(S["dinv_pe"], 1)

            pe.wait_ge(S["diag"], 16 * 17 + 16 * 8)
            pe.wait_ge(S["newp_ev"], 2)
            pe.wait_ge(S["decdve"], 3)
            pe.wait_ge(S["dec_act"], 2)
            for j in range(4):
                for q in range(4):
                    last = flip(ps[2 + j][:, P * q:P * q + P], X[:, 4 * j + q, :], P)
                last.then_inc(S["xt_pe"], 1)

            def state_products(h):
                pe.wait_ge(S[f"s_in{h % 2}"], 16 * (h // 2 + 1))
                for b_ in range(BD):
                    at = TP + TD * b_
                    last = mm(sdv[:, h, :, TD * b_:TD * b_ + TD], Sd[:, h % 2, b_, :], qkvT[:, h:h + H + 1:H, at:at + TD],
                              start=True, stop=True)
                last.then_inc(S["sd_pe"], 1)

            def merge_y(n):
                L, h = divmod(n, H)
                pe.wait_ge(S["atm"], n + 1)
                if n == 0:
                    pe.wait_ge(S["xt_ev"], 4)
                if n >= 2:
                    pe.wait_ge(S["y_ev"], n - 1)
                if n >= H:
                    pe.wait_ge(S["merge"], n - H + 1)
                for c in range(2):
                    last = mm(ps[2 + n % 2][:, P * c:P * c + P], am[n % 2][:, P * c:P * c + P], X[:, 2 * h + c, :],
                              start=True, stop=True)
                last.then_inc(S["y_pe"], 1)

            def merge_x(n):
                L, h = divmod(n, H)
                pe.wait_ge(S["y_ev"], n + 1)
                if n >= 2:
                    pe.wait_ge(S["merge"], n - 1)
                for c in range(2):
                    if L < 2:
                        mm(ps[4 + n % 2][:, P * c:P * c + P], XT[:, 2 * h + c, :], Y[n % 2][:, P * c:P * c + P],
                           start=True, stop=True)
                    last = mm(ps[4 + n % 2][:, TP + P * c:TP + P * c + P], Y[n % 2][:, P * c:P * c + P],
                              XT[:, 2 * h + c, :], start=True, stop=True)
                last.then_inc(S["xx_pe"], 1)

            for n in range(3 * H + 1):
                if n in GATE_AT:
                    proj(GATE_AT[n])
                if n < 3 * H:
                    merge_y(n)
                if n >= 1:
                    merge_x(n - 1)
                if n in STATE_AT:
                    state_products(STATE_AT[n])

            def scan_a(n):
                c, h = divmod(n, H)
                if n >= 2:
                    pe.wait_ge(S["kd_done"], n - 1)
                bank = ps[2 + n % 2]
                flip(bank[:, 0:P], qkvT[:, 2 * H + h, P * c:P * c + P], P)
                last = flip(bank[:, P:2 * P], qkvT[:, H + h, P * c:P * c + P], P)
                if c == 1:
                    pe.wait_ge(S["s_ev"], h + 1)
                    last = mm(bank[:, 2 * P:3 * P], qkvT[:, H + h, P:TP], St[:, h, :], start=True, stop=True)
                last.then_inc(S["vt_pe"], 1)

            def scan_b(n):
                c, h = divmod(n, H)
                pe.wait_ge(S["R_done"], n + 1)
                if n >= 1:
                    pe.wait_ge(S["vn_ev"], n)
                mm(ps[4][:, 0:P], XT[:, 2 * h + c, :], R[n % 2], start=True, stop=True).then_inc(S["vn_pe"], 1)

            def scan_c(n):
                c, h = divmod(n, H)
                pe.wait_ge(S["vn_ev"], n + 1)
                pe.wait_ge(S["kd_done"], n + 1)
                if n >= 1:
                    pe.wait_ge(S["osq"], OSQ[n - 1])
                if n >= 1:
                    pe.wait_ge(S["s_ev"], n)
                o = ps[6][:, 0:P]
                if c == 1:
                    mm(o, qkvT[:, h, P:TP], St[:, h, :], start=True, stop=False)
                mm(o, aqT[:, 2 * h + c, :], vn[n % 2], start=(c == 0), stop=True).then_inc(S["o_pe"], 1)
                mm(ps[0][:, 0:P], kd[n % 2], vn[n % 2], start=True, stop=True).then_inc(S["s_pe"], 1)

            def by_rows(src, done):
                for h in range(H):
                    last = flip(ps[5 + 2 * (h // 4)][0:TS, P * (h % 4):P * (h % 4) + P], src(h), P)
                last.then_inc(S[done], 1)

            def ring_wait(item):
                pe.wait_ge(ring_in[item % RA], 16 * (item // RA + 1))

            def branch_pool(d):
                item = IN_ITEMS + d // 4
                if d % 4 == 0:
                    ring_wait(item)
                if d >= 1:
                    pe.wait_ge(S["bp_dve"], d)
                w = slots[item % RA].rearrange("p (k n) -> p k n", k=NG)
                for k in range(NG):
                    last = mm(ps[1][:, 0:T], w[:, k, P * (d % 4):P * (d % 4) + P], ypT[:, k, :],
                              start=(k == 0), stop=(k == NG - 1))
                last.then_inc(S["bp_pe"], 1)

            pe.wait_ge(S["merge"], 3 * H)
            pe.wait_ge(S["proj_free"], free[N_PROJ - 1])
            pe.wait_ge(S["dinv_dve"], 4)
            for n in range(2 * H + 2):
                if n < 2 * H:
                    scan_a(n)
                if 1 <= n < 2 * H + 1:
                    scan_b(n - 1)
                if n >= 2:
                    scan_c(n - 2)
                if n in BP_AT:
                    branch_pool(BP_AT[n])
                if n == KDD_AT:
                    pe.wait_ge(S["rtd"], 1)
                    by_rows(lambda h: qkvT[:, H + h, TP:T], "kdd_pe")
                if n == RTD_AT:
                    pe.wait_ge(S["kdd_ev"], 2)
                    by_rows(lambda h: RTd[:, h, :], "rtd_t")
                if n == VND_AT:
                    pe.wait_ge(S["rtd_ev"], 2)
                    for h in range(H):
                        last = mm(ps[5 + 2 * (h // 4)][0:TS, P * (h % 4):P * (h % 4) + P], TTd[:, h, :], Rd[:, h, :],
                                  start=True, stop=True)
                    last.then_inc(S["vnd_pe"], 1)
                if n == OD_AT:
                    pe.wait_ge(S["vnd_ev"], 2)
                    for h in range(H):
                        last = mm(ps[5][:, TS * h:TS * h + TS], vnd[:, h, :], aqd[0:TS, h, :], start=True, stop=True)
                    last.then_inc(S["vnd_pe"], 1)
                if n == ODT_AT:
                    pe.wait_ge(S["od_dve"], 1)
                    by_rows(lambda h: oTd[:, h, :], "od_t")

            def decode_state(h):
                pe.wait_ge(S["vx_done"], h + 1)
                if h >= 1:
                    pe.wait_ge(S["sdn_dve"], 2 * h)
                for j in range(2):
                    last = mm(ps[j][:, :], kdd[:, h, :], vx[h % 2][:, 4 * j:4 * j + 4, :].rearrange("p b e -> p (b e)"),
                              start=True, stop=True)
                last.then_inc(S["sdn_pe"], 1)

            pe.wait_ge(S["s_ev"], 2 * H)
            pe.wait_ge(S["bp_dve"], KD)
            for h in range(2):
                decode_state(h)

            for j in range(2):
                for t, m in enumerate(TILES):
                    pe.wait_ge(S["on"], t + 1)
                    if j == 0 and t == 0:
                        pe.wait_ge(S["osq"], 3 * H)
                    for q in range(4):
                        h = 4 * j + q
                        last = flip(ps[2 + NT * j + t][:, q * m:(q + 1) * m], oTok[0:m, t, h * P:(h + 1) * P], m)
                    last.then_inc(S["ot_pe"], 1)

            pe.wait_ge(S["y_done"], 6)
            for d in range(KD):
                item = IN_ITEMS + BP_ITEMS + d // 2
                if d % 2 == 0:
                    ring_wait(item)
                if d >= 2:
                    pe.wait_ge(S["bd_dve"], d - 1)
                w = slots[item % RA].rearrange("p (k n) -> p k n", k=KD)
                for k in range(KD):
                    last = mm(ps[2 + d % 2][:, 0:T], w[:, k, P * (d % 2):P * (d % 2) + P], zT[:, k, :],
                              start=(k == 0), stop=(k == KD - 1))
                last.then_inc(S["bd_pe"], 1)
                if 2 <= d + 1 < H:
                    decode_state(d + 1)
            pe.wait_ge(S["bd_dve"], KD)
            for j in range(WO_ITEMS):
                item = IN_ITEMS + BP_ITEMS + BD_ITEMS + j
                ring_wait(item)
                w = slots[item % RA].rearrange("p (k n) -> p k n", k=KD)
                for t, m in enumerate(TILES):
                    n = NT * j + t
                    if n >= 2:
                        pe.wait_ge(S["wo_dve"], n - 1)
                    for k in range(KD):
                        last = mm(ps[4 + n % 2][0:m, 0:256], merged[:, k, P * t:P * t + m], w[:, k, :],
                                  start=(k == 0), stop=(k == KD - 1))
                    last.then_inc(S["wo_pe"], 1)

            pe.wait_ge(S["wo_dve"], NT * WO_ITEMS)
            for j in range(2):
                for t, m in enumerate(TILES):
                    pe.wait_ge(S["h2_dve"], t + 1)
                    for q in range(4):
                        k = 4 * j + q
                        last = flip(ps[NT * j + t][:, q * m:(q + 1) * m], h2[0:m, t, k * P:(k + 1) * P], m)
                    last.then_inc(S["h2_t"], 1)
            pe.wait_ge(S["h2_ev"], 6)
            for t, m in enumerate(TILES):
                for k in range(KD):
                    last = mm(ps[6][0:m, 36 * t:36 * t + 36], h2T[:, k, P * t:P * t + m], wr[:, k, :],
                              start=(k == 0), stop=(k == KD - 1))
            last.then_inc(S["route_pe"], 1)
            pe.wait_ge(S["rt_d"], 2 + 1)
            for t, m in enumerate(TILES):
                for s in range(t + 1):
                    mm(ps[7][0:m, NE * t:NE * t + NE], (strU[0:m, 0:m] if s == t else ones[:, 0:m]),
                       picks[0:TILES[s], s, :], start=(s == 0), stop=(s == t))
            for s, m in enumerate(TILES):
                last = mm(ps[7][:, NE * NT:NE * NT + NE], ones[0:m, :], picks[0:m, s, :],
                          start=(s == 0), stop=(s == NT - 1))
            last.then_inc(S["route_pe"], 1)

            def wait_from(s, v):
                if not isinstance(v, int) or v >= 1:
                    pe.wait_ge(s, v)

            def loaded(u, j, i):
                base = -(-(A_ITEMS - j) // RA) if u == 0 else 0
                pe.wait_ge(ring_in[RA * u + j], (i + 1 + base) * 16)

            def act_flip(q, v):
                pe.wait_ge(S["m_act"], q + 1)
                wait_from(S["m_aTev"], q)
                for c in range(2):
                    last = flip(ps[4][:, P * c:P * c + P], act_[v][:, P * c:P * c + P], P)
                last.then_inc(S["m_aT"], 1)

            def down(q, v, i):
                pe.wait_ge(S["m_aTev"], q + 1)
                wait_from(S["m_dnA"], q)
                wait_from(S["m_dnV"], q)
                loaded(v, 4, i)
                loaded(v, 5, i)
                for half in range(2):
                    for c in range(2):
                        for e in range(2):
                            w = slots[RA * v + 4 + e].rearrange("p (c n) -> p c n", c=2)
                            last = mm(ps[5 + half][CAP * e:CAP * e + CAP, :], actT[v][:, c, CAP * e:CAP * e + CAP],
                                      w[:, c, 512 * half:512 * half + 512], start=(c == 0), stop=(c == 1))
                last.then_inc(S["m_dn"], 1)

            def pair(i, u):
                p = 2 * i + u
                before = not isinstance(p, int) or p >= 1
                pe.wait_ge(S[f"gather{u}"], (i + 1) * 16)
                wait_from(S["m_TevA"], p)
                wait_from(S["m_TevV"], p)
                for k in range(KD):
                    last = flip(ps[k // 4][:, P * (k % 4):P * (k % 4) + P], xg[u][:, k * P:(k + 1) * P], P)
                last.then_inc(S["m_T"], 1)
                pe.wait_ge(S["m_TevA"], p + 1)
                pe.wait_ge(S["m_TevV"], p + 1)
                wait_from(S["m_act"], p - 1)
                for j in range(4):
                    loaded(u, j, i)
                for k in range(KD):
                    if k == 4 and before:
                        act_flip(p - 1, 1 - u)
                    for j in range(4):
                        e = CAP * (j // 2)
                        last = mm(ps[2 + u][e:e + CAP, FE * (j % 2):FE * (j % 2) + FE], xgT[u][:, k, e:e + CAP],
                                  slots[RA * u + j].rearrange("p (k n) -> p k n", k=KD)[:, k, :],
                                  start=(k == 0 and j % 2 == 0), stop=(k == KD - 1 and j % 2 == 1),
                                  skip_group_check=True)
                last.then_inc(S["m_gu"], 1)
                if before:
                    down(p - 1, 1 - u, i if u else i - 1)

            pe.wait_ge(S["route"], 1)
            for i in range(PEEL):
                for u in range(2):
                    pair(i, u)
            end = pe.value_load(more_i[0:1, 0:1], min_val=0, max_val=(ROUNDS - 1) * PAIRS // 2) + PAIRS // 2
            with pe.Fori(PEEL, end) as i:
                for u in range(2):
                    pair(i, u)
            act_flip(2 * end - 1, 1)
            down(2 * end - 1, 1, end - 1)

        @block.vector
        def _(dve):
            V = nc.vector
            chain = [0]

            def link(ins):
                chain[0] += 1
                ins.then_inc(S["dve_chain"], 1)
                dve.wait_ge(S["dve_chain"], chain[0])

            def last_as(ins, s, v):
                ins.then_inc(S[s], 1)
                dve.wait_ge(S[s], v)

            def spread(v, m, n):
                return v.unsqueeze(2).to_broadcast([m, v.shape[1], n])

            last_as(V.memset(sc[:, :], 1.0), "sc_one", 1)
            dve.wait_ge(S["sq_sum"], NT)
            V.tensor_scalar(rs1, ss1, 1.0 / D, EPS, ALU.mult, ALU.add).then_inc(S["mean_sq"], 1)
            dve.wait_ge(S["root"], 1)
            link(V.reciprocal(rs1, rs1))
            for t, m in enumerate(TILES):
                V.tensor_scalar(xt[0:m, t, :], xt[0:m, t, :], rs1[0:m, t:t + 1], None, ALU.mult).then_inc(S["xn"], 1)
            dve.wait_ge(S["small_t"], 1)
            last_as(V.tensor_copy(smallT[:, 0:109], ps[2][:, 0:109]), "small_ev", 1)
            dve.wait_ge(S["small_t"], 3)
            for j in range(2):
                V.tensor_copy(cT[:, 12 * j:12 * j + 12, :].rearrange("p c r -> p (c r)"), ps[3 + j][:, 0:288]).then_inc(S["small_ev"], 1)
            dve.wait_ge(S["small_t"], 4)
            V.tensor_copy(pcT.rearrange("p c r -> p (c r)"), ps[5][:, 0:480]).then_inc(S["small_ev"], 1)
            XB = [6, 7, 0, 1, 2, 3]
            for t, m in enumerate(TILES):
                for j in range(2):
                    dve.wait_ge(S["x_t"], 2 * t + j + 1)
                    V.tensor_tensor(hT[:, 4 * j:4 * j + 4, P * t:P * t + m],
                                    ps[XB[2 * t + j]][:, 0:4 * m].rearrange("p (k t) -> p k t", k=4),
                                    spread(smallT[:, 96 + 4 * j:100 + 4 * j], P, m), ALU.mult).then_inc(S["ht_done"], 1)

            dve.wait_ge(S["pe_ab"], 1)
            for t, m in enumerate(TILES):
                last = V.tensor_copy(ab[0:m, t, :], ps[6][0:m, 16 * t:16 * t + 16])
                if t < NT - 1:
                    last.then_inc(S["dve_chain"], 1)
                    chain[0] += 1
            link(last)
            hb = dtb.unsqueeze(1).to_broadcast([P, NT, H])
            link(V.tensor_tensor(t1, ab[:, :, H:2 * H], hb, ALU.add))
            link(V.tensor_scalar(t2, t1, -1.0, None, ALU.mult))
            V.tensor_tensor(t2, t1, t2, ALU.max).then_inc(S["ab_ev"], 1)
            dve.wait_ge(S["soft"], 3)
            V.tensor_scalar(t4, t2, 1.0, None, ALU.add).then_inc(S["ab_ev"], 1)
            link(V.tensor_scalar(beta, beta, 1.0, None, ALU.add))
            link(V.reciprocal(beta, beta))
            dve.wait_ge(S["ab_ev"], 2)
            link(V.tensor_scalar(g_, t4, -1.0, None, ALU.add))
            link(V.tensor_tensor(t2, t2, g_, ALU.subtract))
            link(V.reciprocal(g_, t4))
            link(V.tensor_tensor(t2, t2, g_, ALU.mult))
            dve.wait_ge(S["soft"], 4)
            link(V.tensor_tensor(t2, t2, t3, ALU.add))
            link(V.tensor_scalar(t1, t1, 0.0, None, ALU.max))
            link(V.tensor_tensor(t2, t2, t1, ALU.add))
            link(V.tensor_tensor(t2, t2, alog.unsqueeze(1).to_broadcast([P, NT, H]), ALU.mult))
            link(V.tensor_scalar(g_, t2, -1.0, None, ALU.mult))
            dve.wait_ge(S["masks"], 1)
            V.tensor_tensor(gbd[0:TS], spread(g_[0:TS, 2, :], TS, BD),
                            bmask[0:TS].unsqueeze(1).to_broadcast([TS, H, BD]), ALU.mult).then_inc(S["g_done"], 1)

            def conv(n):
                dve.wait_ge(S["proj_free"], free[n])
                dve.wait_ge(S["e_cache"], n + 1)
                if n >= 2:
                    dve.wait_ge(S["silu"], 3 * (n - 1))
                e, c = E[n % 3], C[n % 2]
                link(V.tensor_scalar(c, e[:, 0:NACC], smallT[:, n:n + 1], None, ALU.mult))
                for j in range(1, CW):
                    ins = V.scalar_tensor_tensor(c, e[:, j:j + NACC], smallT[:, NQKV * j + n:NQKV * j + n + 1], c,
                                                 ALU.mult, ALU.add)
                    if j < CW - 1:
                        link(ins)
                ins.then_inc(S["conv"], 1)

            for n in range(NQKV):
                conv(n)
                if n == 1:
                    dve.wait_ge(S["pe_G"], 1)
                    dve.wait_ge(S["g_done"], 1)
                    for t, m in enumerate(TILES):
                        link(V.tensor_copy(Gc[0:m, t, :], ps[6][0:m, 64 + 8 * t:72 + 8 * t]))
                        link(V.tensor_copy(Gl[0:m, t, :], ps[6][0:m, 96 + 8 * t:104 + 8 * t]))
                    link(V.tensor_copy(eGd, ps[6][:, 128:192].rearrange("p (h b) -> p h b", h=H)))
                    V.tensor_tensor(kds, Gl, Gc, ALU.subtract).then_inc(S["g_scal"], 1)
                if n == N_V + 1:
                    dve.wait_ge(S["ssd"], N_V)
                    for t, m in enumerate(TILES):
                        link(V.tensor_scalar(rqk[0:m, t, 0:H], ps[7][0:m, 16 * t:16 * t + H], float(DK), EPS * DK, ALU.mult, ALU.add))
                        ins = V.tensor_scalar(rqk[0:m, t, H:2 * H], ps[7][0:m, 16 * t + H:16 * t + 2 * H], EPS, None, ALU.add)
                        if t < NT - 1:
                            link(ins)
                    ins.then_inc(S["ss_sc"], 1)
                if n == N_V + 3:
                    dve.wait_ge(S["ss_sqrt"], 1)
                    dve.wait_ge(S["g_exp"], 4)
                    link(V.reciprocal(rqk, rqk))
                    rq, rk = rqk[:, :, 0:H], rqk[:, :, H:2 * H]
                    link(V.tensor_tensor(brk, beta, rk, ALU.mult))
                    link(V.tensor_tensor(kds, kds, rk, ALU.mult))
                    link(V.tensor_tensor(nber, brk, t1, ALU.mult))
                    link(V.tensor_scalar(nber, nber, -1.0, None, ALU.mult))

            def window(g):
                n = N_POOL + g
                dve.wait_ge(S["proj_free"], free[n])
                dve.wait_ge(S["e_cache"], n + 1)
                e = EP[g % 2]
                src, w = e, 1
                for L in range(g + 1):
                    dst = wa[L % 2]
                    link(V.tensor_tensor(dst[:, 2 * w - 1:EPW], src[:, 2 * w - 1:EPW], src[:, w - 1:EPW - w], ALU.add))
                    src, w = dst, 2 * w
                link(V.tensor_tensor(pooled[:, g, 0:w], src[:, PBUF:PBUF + w], invc[:, 0:w], ALU.mult))
                link(V.tensor_tensor(pooled[:, g, 0:w], pooled[:, g, 0:w], e[:, PBUF:PBUF + w], ALU.subtract))
                link(V.scalar_tensor_tensor(pooled[:, g, w:TP], src[:, PBUF + w:PE0], 1.0 / w, e[:, PBUF + w:PE0],
                                            ALU.mult, ALU.subtract))

                def new(a):
                    return a[:, PE0:EPW].rearrange("p (b r) -> p b r", b=BD)[:, :, PBUF:]

                last_as(V.scalar_tensor_tensor(pooled[:, g, TP:T].rearrange("p (b t) -> p b t", b=BD), new(src), 1.0 / w,
                                               new(e), ALU.mult, ALU.subtract), "pool_dve", g + 1)

            link(V.reciprocal(invc, invc))
            for g in range(NG):
                window(g)

            def rows(h):
                if h >= 1:
                    dve.wait_ge(S["rows"], h)
                for j, (mask, v) in enumerate(((triU, g_[:, 0:2, h]), (ident, brk[:, 0:2, h]), (ident, rqk[:, 0:2, h]))):
                    V.tensor_tensor(RB[:, j, :].rearrange("p (c t) -> p c t", c=2),
                                    mask.unsqueeze(1).to_broadcast([P, 2, P]), spread(v, P, P), ALU.mult).then_inc(S["rb"], 1)

            def prep(h):
                dve.wait_ge(S["rows"], h + 1)
                for c in range(2):
                    V.tensor_scalar(Dt[:, P * c:P * c + P], ps[3][:, P * c:P * c + P], Gc[:, c, h:h + 1], 0.0,
                                    ALU.subtract, ALU.min).then_inc(S["dt"], 1)
                dve.wait_ge(S["expd"], 2 * h + 2)
                dve.wait_ge(S["qk_pe"], h + 1)
                link(V.tensor_tensor(Dt.rearrange("p (c t) -> p c t", c=2), Dt.rearrange("p (c t) -> p c t", c=2),
                                     triU.unsqueeze(1).to_broadcast([P, 2, P]), ALU.mult))
                for c in range(2):
                    for j, to in enumerate((aqT, AT)):
                        link(V.scalar_tensor_tensor(to[:, 2 * h + c, :], ps[5][:, TP * c + P * j:TP * c + P * j + P],
                                                    rqk[:, c, H + h:H + h + 1], Dt[:, P * c:P * c + P], ALU.mult, ALU.mult))
                link(V.tensor_tensor(egq, egq, ps[4][:, P:TP], ALU.mult))
                for to, bank, at in ((aqT, 4, 0), (AT, 3, TP)):
                    v = to[:, 2 * h:2 * h + 2, :]
                    link(V.tensor_tensor(v, v, ps[bank][:, at:at + TP].rearrange("p (c t) -> p c t", c=2), ALU.mult))
                V.tensor_tensor(qkvT[:, h, P:TP], qkvT[:, h, P:TP], egq, ALU.mult).then_inc(S["prep_done"], 1)

            dve.wait_ge(S["silu"], 3 * NQKV)
            dve.wait_ge(S["small_ev"], 4)
            dve.wait_ge(S["wp_pe"], NG)
            rows(0)
            for h in range(H):
                prep(h)
                if h + 1 < H:
                    rows(h + 1)

            vals = (g_, brk, rqk[:, :, 0:H], beta)
            for j in range(4):
                mask = U4[:, :] if j == 0 else ident[0:TS, 0:TS]
                V.tensor_tensor(rbd[:, j], mask.unsqueeze(1).to_broadcast([TS, H, TS]),
                                spread(vals[j][0:TS, 2, :], TS, TS), ALU.mult).then_inc(S["decrb"], 1)
            dve.wait_ge(S["dec_act"], 2)
            link(V.tensor_tensor(Dd[0:TS], rows_d[0:TS, 0], spread(Gc[0:TS, 2, :], TS, TS), ALU.subtract))
            V.tensor_scalar(Dd[0:TS], Dd[0:TS], 0.0, None, ALU.min).then_inc(S["decdve"], 1)
            dve.wait_ge(S["dec_act"], 4)
            link(V.tensor_tensor(Dd[0:TS], Dd[0:TS], U4[:, :].unsqueeze(1).to_broadcast([TS, H, TS]), ALU.mult))
            link(V.tensor_tensor(Dd[0:TS], Dd[0:TS], spread(rqk[0:TS, 2, H:2 * H], TS, TS), ALU.mult))
            dve.wait_ge(S["decqk"], 1)
            d5 = ps[5][0:TS, :].rearrange("p (h r t) -> p h r t", h=H, r=2)
            link(V.tensor_tensor(aqd[0:TS], d5[:, :, 0, :], Dd[0:TS], ALU.mult))
            link(V.tensor_tensor(aqd[0:TS], aqd[0:TS], rows_d[0:TS, 2], ALU.mult))
            link(V.tensor_tensor(Nd[0:TS], d5[:, :, 1, :], Dd[0:TS], ALU.mult))
            link(V.tensor_tensor(Nd[0:TS], Nd[0:TS], rows_d[0:TS, 1], ALU.mult))
            link(V.tensor_tensor(tmpd, egd, rows_d[:, 2], ALU.mult))
            link(V.tensor_tensor(qkvT[:, 0:H, TP:T], qkvT[:, 0:H, TP:T], tmpd, ALU.mult))
            V.tensor_tensor(rows_d[:, 1], rows_d[:, 1], egd, ALU.mult).then_inc(S["decdve"], 1)
            V.tensor_tensor(Nd[0:TS], Nd[0:TS], S4[:, :].unsqueeze(1).to_broadcast([TS, H, TS]), ALU.mult).then_inc(S["decdve"], 1)

            dve.wait_ge(S["diag"], 16 * 8 + 16 * 8)
            dve.wait_ge(S["memsets"], 1 + 1)
            link(V.tensor_scalar(And, And, -1.0, None, ALU.mult))
            xd = Xd.rearrange("p (i c) -> p i c", i=16)
            an = And.rearrange("p (j i) -> p j i", i=16)
            for i in range(1, 16):
                pr = prod[:, 0:i * i].rearrange("p (c j) -> p c j", j=i)
                link(V.tensor_tensor(pr, xd[:, 0:i, 0:i].rearrange("p j c -> p c j"),
                                     an[:, 0:i, i].unsqueeze(1).to_broadcast([P, i, i]), ALU.mult))
                ins = V.tensor_reduce(xd[:, i, 0:i], pr, AX.X, ALU.add)
                if i < 15:
                    link(ins)
            ins.then_inc(S["sub_done"], 1)

            dve.wait_ge(S["dinv_pe"], 1)
            dve.wait_ge(S["decdve"], 3)
            eye_d = ident[0:TS, 0:TS].unsqueeze(1).to_broadcast([TS, H, TS])

            def d_bank(i):
                return ps[i][0:TS, 0:H * TS].rearrange("p (h t) -> p h t", h=H)

            last_as(V.tensor_copy(tmpd[0:TS], d_bank(6)), "dinv_dve", 1)
            last_as(V.tensor_tensor(IAd[0:TS], eye_d, tmpd[0:TS], ALU.subtract), "dinv_dve", 2)
            dve.wait_ge(S["dinv_pe"], 2)
            last_as(V.tensor_copy(N2d[0:TS], d_bank(7)), "dinv_dve", 3)
            dve.wait_ge(S["dinv_pe"], 3)
            link(V.tensor_tensor(Nd[0:TS], eye_d, Nd[0:TS], ALU.subtract))
            V.tensor_tensor(TTd, Nd[0:TS], d_bank(6), ALU.add).then_inc(S["dinv_dve"], 1)

            def mask_level(n):
                L, h = divmod(n, H)
                if n >= 2:
                    dve.wait_ge(S["y_pe"], n - 1)
                V.tensor_tensor(am[n % 2].rearrange("p (c t) -> p c t", c=2), AT[:, 2 * h:2 * h + 2, :],
                                lvl[L].unsqueeze(1).to_broadcast([P, 2, P]), ALU.mult).then_inc(S["atm"], 1)

            def merge(n):
                L, h = divmod(n, H)
                dve.wait_ge(S["xx_pe"], n + 1)
                if n == 0:
                    dve.wait_ge(S["xt_ev"], 4)
                bank = ps[4 + n % 2]
                for j, to in enumerate((X, XT)):
                    if j == 0 and L == 2:
                        continue
                    v = to[:, 2 * h:2 * h + 2, :]
                    ins = V.tensor_tensor(v, v, bank[:, TP * j:TP * j + TP].rearrange("p (c t) -> p c t", c=2), ALU.subtract)
                    if j == 0:
                        link(ins)
                ins.then_inc(S["merge"], 1)

            for n in range(3 * H + 1):
                if n < 3 * H:
                    mask_level(n)
                if n >= 1:
                    merge(n - 1)

            def scan_r(n):
                c, h = divmod(n, H)
                dve.wait_ge(S["vt_pe"], n + 1)
                bank = ps[2 + n % 2]
                if n >= 2:
                    dve.wait_ge(S["vn_pe"], n - 1)
                    dve.wait_ge(S["s_pe"], n - 1)
                ins = V.tensor_scalar(R[n % 2], bank[:, 0:P], beta[:, c, h:h + 1], None, ALU.mult)
                if c == 1:
                    link(ins)
                    ins = V.scalar_tensor_tensor(R[n % 2], bank[:, 2 * P:3 * P], nber[:, c, h:h + 1], R[n % 2],
                                                 ALU.mult, ALU.add)
                ins.then_inc(S["R_done"], 1)
                V.tensor_scalar(kd[n % 2], bank[:, P:2 * P], kds[:, c, h:h + 1], None, ALU.mult).then_inc(S["kd_done"], 1)

            def scan_s(n):
                c, h = divmod(n, H)
                dve.wait_ge(S["s_pe"], n + 1)
                if c == 0:
                    ins = V.tensor_copy(St[:, h, :], ps[0][:, 0:P])
                else:
                    ins = V.scalar_tensor_tensor(St[:, h, :], St[:, h, :], eGl[:, 1, h:h + 1], ps[0][:, 0:P],
                                                 ALU.mult, ALU.add)
                ins.then_inc(S["s_ev"], 1)

            def branch_pool(d):
                dve.wait_ge(S["bp_pe"], d + 1)
                V.scalar_tensor_tensor(gT[:, d, :], gT[:, d, :], 1.0, ps[1][:, 0:T], ALU.add, ALU.mult).then_inc(S["bp_dve"], 1)

            def spread_v(h):
                if h >= 2:
                    dve.wait_ge(S["sdn_pe"], h - 1)
                V.tensor_tensor(vx[h % 2], vnd[:, h, :].unsqueeze(1).to_broadcast([TS, BD, P]),
                                spread(bmask[0:TS], TS, P), ALU.mult).then_inc(S["vx_done"], 1)

            def new_state(h):
                dve.wait_ge(S["sd_mul"], h + 1)
                dve.wait_ge(S["sdn_pe"], h + 1)
                for j in range(2):
                    v = Sd[:, h % 2, 4 * j:4 * j + 4, :].rearrange("p b e -> p (b e)")
                    V.tensor_tensor(v, v, ps[j][:, :], ALU.add).then_inc(S["sdn_dve"], 1)

            dve.wait_ge(S["merge"], 3 * H)
            dve.wait_ge(S["xx_pe"], 3 * H)
            dve.wait_ge(S["sd_pe"], H)
            link(V.tensor_tensor(tmpd, sdv[:, :, 1, :], rows_d[:, 1], ALU.mult))
            link(V.tensor_tensor(RTd, qkvT[:, 2 * H:3 * H, TP:T], rows_d[:, 3], ALU.mult))
            link(V.tensor_copy(oTd, sdv[:, :, 0, :]))
            V.tensor_tensor(RTd, RTd, tmpd, ALU.subtract).then_inc(S["rtd"], 1)
            dve.wait_ge(S["proj_free"], free[N_PROJ - 1])
            for n in range(2 * H + 2):
                if n < 2 * H:
                    scan_r(n)
                if n >= 2:
                    scan_s(n - 2)
                if n in BP_AT:
                    branch_pool(BP_AT[n])
                if n == KDD_AT:
                    dve.wait_ge(S["kdd_pe"], 1)
                    for j in range(2):
                        V.tensor_tensor(kdd[:, 4 * j:4 * j + 4, :], ps[5 + 2 * j][0:TS, :].rearrange("p (h e) -> p h e", h=4),
                                        spread(kds[0:TS, 2, 4 * j:4 * j + 4], TS, P), ALU.mult).then_inc(S["kdd_ev"], 1)
                if n == OD_AT:
                    dve.wait_ge(S["vnd_pe"], 2)
                    V.tensor_tensor(oTd, oTd, ps[5][:, 0:H * TS].rearrange("p (h t) -> p h t", h=H), ALU.add).then_inc(S["od_dve"], 1)
                if n == OD_AT + 1:
                    spread_v(0)

            dve.wait_ge(S["osq"], 3 * H)
            V.tensor_scalar(orr, oss, 1.0 / P, EPS, ALU.mult, ALU.add).then_inc(S["mean_sq"], 1)
            dve.wait_ge(S["out_dma"], 32)
            spread_v(1)
            dve.wait_ge(S["root"], 1 + 1)
            link(V.reciprocal(orr, orr))
            for t, m in enumerate(TILES):
                v = oTok[0:m, t].rearrange("p (h e) -> p h e", h=H)
                V.tensor_tensor(v, v, spread(orr[0:m, t, :], m, P), ALU.mult).then_inc(S["on"], 1)
            for h in range(2):
                new_state(h)
                spread_v(h + 2)

            for j in range(2):
                for t, m in enumerate(TILES):
                    dve.wait_ge(S["ot_pe"], NT * j + t + 1)
                    v = zT[:, 4 * j:4 * j + 4, P * t:P * t + m]
                    V.scalar_tensor_tensor(v, ps[2 + NT * j + t][:, 0:4 * m].rearrange("p (h t) -> p h t", h=4),
                                           smallT[:, 108:109], v, ALU.mult, ALU.mult).then_inc(S["y_done"], 1)

            for d in range(KD):
                dve.wait_ge(S["bd_pe"], d + 1)
                link(V.scalar_tensor_tensor(gT[:, KD + d, :], gT[:, KD + d, :], 1.0, ps[2 + d % 2][:, 0:T], ALU.add, ALU.mult))
                V.tensor_tensor(merged[:, d, :], gT[:, d, :], gT[:, KD + d, :], ALU.add).then_inc(S["bd_dve"], 1)
                if 2 <= d + 1 < H:
                    new_state(d + 1)
                    if d + 3 < H:
                        spread_v(d + 3)

            dve.wait_ge(S["xr_in"], 16 * NT)
            for n in range(NT * WO_ITEMS):
                j, t = divmod(n, NT)
                m = TILES[t]
                dve.wait_ge(S["wo_pe"], n + 1)
                cols = slice(256 * j, 256 * j + 256)
                V.scalar_tensor_tensor(x2[0:m, t, cols], ps[4 + n % 2][0:m, 0:256], 0.5, xr[0:m, t, cols],
                                       ALU.mult, ALU.add).then_inc(S["wo_dve"], 1)

            dve.wait_ge(S["sq_sum"], NT + NT)
            V.tensor_scalar(rs1, ss1, 1.0 / D, EPS, ALU.mult, ALU.add).then_inc(S["mean_sq"], 1)
            dve.wait_ge(S["root"], 2 + 1)
            link(V.reciprocal(rs1, rs1))
            dve.wait_ge(S["nb_in"], 32)

            def by_block(v):
                return v.rearrange("p (q k) -> p k q", k=KD)

            dve.wait_ge(S["wo_dve"], NT * WO_ITEMS)
            for t, m in enumerate(TILES):
                V.scalar_tensor_tensor(h2[0:m, t, :].rearrange("p (k q) -> p k q", k=KD), by_block(x2[0:m, t, :]),
                                       rs1[0:m, t:t + 1], by_block(n2b[0:m, :]), ALU.mult, ALU.mult).then_inc(S["h2_dve"], 1)

            link(V.memset(r[:, :, :], 0.0))
            link(V.memset(lg8, -3.0e38))
            dve.wait_ge(S["route_pe"], 1)
            for t, m in enumerate(TILES):
                link(V.tensor_tensor(lg[0:m, t, :], ps[6][0:m, 36 * t:36 * t + 36], rb_[0:m, :], ALU.add))
            link(V.tensor_copy(lg8[:, :, 0:NGR], lg[:, :, 0:NGR]))
            for t in range(NT):
                link(V.max(mx8[:, t, :], lg8[:, t, :]))
                link(V.max_index(mi[:, t, 0:8], mx8[:, t, :], lg8[:, t, :]))
            V.tensor_tensor(eg4, lg[:, :, 0:NGR], mx8[:, :, 0:1].to_broadcast([P, NT, NGR]), ALU.subtract).then_inc(S["rt_d"], 1)
            link(V.tensor_copy(gs, mi[:, :, 0:1]))
            e0 = ecst[:, 0, :]
            link(V.tensor_tensor(goh, e0[:, 0:NGR].unsqueeze(1).to_broadcast([P, NT, NGR]),
                                 gs.to_broadcast([P, NT, NGR]), ALU.is_equal))
            link(V.tensor_tensor(prodr, lg[:, :, NGR:].rearrange("p t (g e) -> p t g e", g=NGR),
                                 goh.unsqueeze(3).to_broadcast([P, NT, NGR, EPG]), ALU.mult))
            link(V.tensor_reduce(les, prodr.rearrange("p t g e -> p t e g"), AX.X, ALU.add))
            for t in range(NT):
                link(V.max(mx8[:, t, :], les[:, t, :]))
                link(V.max_index(mi[:, t, 8:16], mx8[:, t, :], les[:, t, :]))
            V.tensor_tensor(ed, mx8[:, :, 1:2], mx8[:, :, 0:1], ALU.subtract).then_inc(S["rt_d"], 1)
            link(V.tensor_copy(eid, mi[:, :, 8:10]))
            link(V.scalar_tensor_tensor(eid, gs.to_broadcast([P, NT, 2]), float(EPG), eid, ALU.mult, ALU.add))
            for k in range(2):
                link(V.tensor_tensor(oh[k], e0.unsqueeze(1).to_broadcast([P, NT, NE]),
                                     eid[:, :, k:k + 1].to_broadcast([P, NT, NE]), ALU.is_equal))
            V.tensor_tensor(picks, oh[0], oh[1], ALU.add).then_inc(S["rt_d"], 1)
            dve.wait_ge(S["rt_e"], 2)
            link(V.tensor_reduce(pg, eg4, AX.X, ALU.add))
            link(V.tensor_scalar(w12[:, :, 1:2], ed, 1.0, None, ALU.add))
            link(V.tensor_tensor(w12[:, :, 0:1], w12[:, :, 1:2], pg, ALU.mult))
            link(V.reciprocal(w12[:, :, 0:1], w12[:, :, 0:1]))
            link(V.tensor_tensor(w12[:, :, 1:2], w12[:, :, 0:1], ed, ALU.mult))
            dve.wait_ge(S["route_pe"], 1 + 1)
            for t, m in enumerate(TILES):
                link(V.tensor_copy(rk_[0:m, t, :], ps[7][0:m, NE * t:NE * t + NE]))
            link(V.tensor_reduce(cnt, ps[7][:, NE * NT:NE * NT + NE], AX.X, ALU.max))
            for k in range(2):
                link(V.tensor_tensor(prode, oh[k], rk_, ALU.mult))
                link(V.tensor_reduce(rank[:, :, k:k + 1], prode, AX.X, ALU.add))
                link(V.tensor_tensor(prode, oh[k], ecst[:, 1, :].unsqueeze(1).to_broadcast([P, NT, NE]), ALU.mult))
                link(V.tensor_reduce(tpos[:, :, k:k + 1], prode, AX.X, ALU.add))
            link(V.tensor_scalar(rnd, rank, float(CAP), None, ALU.is_ge))
            for q in range(2, ROUNDS):
                link(V.scalar_tensor_tensor(rnd, rank, float(CAP * q), rnd, ALU.is_ge, ALU.add))
            link(V.scalar_tensor_tensor(tpos, rank, float(TBL), tpos, ALU.mult, ALU.add))
            link(V.scalar_tensor_tensor(tpos, rnd, float(PAIRS - CAP * TBL), tpos, ALU.mult, ALU.add))
            link(V.tensor_copy(places[:, :, 0:2], tpos))
            link(V.tensor_scalar(itf, cnt, 0.0, None, ALU.is_gt))
            for q in range(1, ROUNDS):
                link(V.scalar_tensor_tensor(itf, cnt, float(CAP * q), itf, ALU.is_gt, ALU.add))
            V.tensor_scalar(more_i[:, :], itf, float(PAIRS // 2), -float(PAIRS // 2), ALU.mult, ALU.add).then_inc(S["route"], 1)
            dve.wait_ge(S["route"], 1)
            dve.wait_ge(S["tbl"], 16 * (2 + 2 * NT))
            V.tensor_scalar(get[:, :], put[:, :], 1, None, ALU.logical_shift_right).then_inc(S["get_done"], 1)

            def wait_from(s, v):
                if not isinstance(v, int) or v >= 1:
                    dve.wait_ge(s, v)

            def results(q, v, cnt):
                dve.wait_ge(S["m_dn"], q + 1)
                wait_from(S[f"dn_out{v}"], cnt * 16)
                V.tensor_copy(dn[v][:, 512:1024], ps[6][:, :]).then_inc(S["m_dnV"], 1)

            def pair(i, u):
                p = 2 * i + u
                dve.wait_ge(S["m_T"], p + 1)
                V.tensor_copy(xgT[u][:, 0:4, :].rearrange("p k t -> p (k t)"), ps[0][:, :]).then_inc(S["m_TevV"], 1)
                dve.wait_ge(S["m_sg"], p + 1)
                V.tensor_tensor(act_[u].rearrange("p (c q) -> p c q", c=2), sg[u].rearrange("p (q c) -> p c q", c=2),
                                ps[2 + u][:, FE:2 * FE].rearrange("p (q c) -> p c q", c=2), ALU.mult).then_inc(S["m_act"], 1)
                if not isinstance(p, int) or p >= 1:
                    results(p - 1, 1 - u, i if u else i - 1)

            for i in range(PEEL):
                for u in range(2):
                    pair(i, u)
            end = dve.value_load(more_i[0:1, 0:1], min_val=0, max_val=(ROUNDS - 1) * PAIRS // 2) + PAIRS // 2
            with dve.Fori(PEEL, end) as i:
                for u in range(2):
                    pair(i, u)
            results(2 * end - 1, 1, end - 1)

            dve.wait_ge(S["fin_in"], 16 * NT)
            for t, m in enumerate(TILES):
                for k in range(2):
                    ins = V.scalar_tensor_tensor(x2[0:m, t, :], yg[t][0:m, D * k:D * k + D], w12[0:m, t, k:k + 1], x2[0:m, t, :],
                                                 ALU.mult, ALU.add)
                    if k == 0:
                        link(ins)
                ins.then_inc(S["fin_sum"], 1)
            dve.wait_ge(S["sq_sum"], 2 * NT + NT)
            V.tensor_scalar(rs1, ss1, 1.0 / D, EPS, ALU.mult, ALU.add).then_inc(S["mean_sq"], 1)
            dve.wait_ge(S["root"], 3 + 1)
            link(V.reciprocal(rs1, rs1))
            for t, m in enumerate(TILES):
                V.scalar_tensor_tensor(x2[0:m, t, :], x2[0:m, t, :], rs1[0:m, t:t + 1], fnb[0:m, :],
                                       ALU.mult, ALU.mult).then_inc(S["fin_y"], 1)


_INS = ['x_prompt', 'x_sample', 'cache_pool', 'cache_conv', 'state_delta', 'norm1_w', 'w_in', 'w_pool', 'pool_scale',
        'w_conv', 'a_log', 'dt_bias', 'o_norm_w', 'w_branch_pool', 'w_branch_delta', 'w_out', 'norm2_w',
        'w_router_group', 'b_router_group', 'w_router_expert', 'b_router_expert', 'w_gate', 'w_up', 'w_down',
        'final_norm_w']
_OUTS = [(1, TP, D), (BD, TD, D), (1, 1, PBUF, NG * P), (1, 1, CW - 1, NQKV * P), (1, 1, H, DK, DK),
         (1, BD, PBUF, NG * P), (1, BD, CW - 1, NQKV * P), (1, BD, H, DK, DK)]


def kernel(**inputs):
    import numpy as _np
    import concourse.bacc as _bacc
    from concourse import mybir as _mybir
    from concourse.bass_utils import run_bass_kernel_spmd as _run

    nc = _bacc.Bacc("TRN2", target_bir_lowering=False, num_devices=1)
    arrays, args = {}, []
    for name in _INS:
        a = _np.ascontiguousarray(inputs[name])
        arrays[f"in_{name}_dram"] = a
        args.append(nc.dram_tensor(f"in_{name}_dram", a.shape, _mybir.dt.from_np(a.dtype), kind="ExternalInput").ap())
    for i, shape in enumerate(_OUTS):
        args.append(nc.dram_tensor(f"out_{i}_dram", shape, _mybir.dt.float32, kind="ExternalOutput").ap())
    hybrid_step(nc, *args)
    r = _run(nc, [arrays], core_ids=[0])
    return tuple(r.results[0][f"out_{i}_dram"] for i in range(len(_OUTS)))
```

```python
from contextlib import ExitStack

import concourse.bass as bass
from concourse import mybir

F32 = mybir.dt.float32
I32 = mybir.dt.int32
U32 = mybir.dt.uint32
ALU = mybir.AluOpType
ACT = mybir.ActivationFunctionType
AX = mybir.AxisListType

P = 128
D = 1024
KD = D // P
TP = 256
BD, TD = 8, 4
TS = BD * TD
T = TP + TS
TILES = [P, P, TS]
NT = len(TILES)
H = 8
DK = 128
NG = 4
PBUF = 15
CW = 4
NQKV = 3 * H
POOL_C, QKV_C = 0, NG * P
AB_C = QKV_C + NQKV * P
Z_C = AB_C + 2 * H
GATE_C = Z_C + H * P
NE, NGR, EPG = 32, 4, 8
FE = 256
QE = 4
CAP = P // QE
ROUNDS = -(-T // CAP)
QUADS = NE // QE
TBL = ROUNDS * QUADS
MORE_MAX = (ROUNDS - 1) * QUADS // 2
SKIP = 100000
EPS = 1e-6
SLOT = 8 * 256
RA = 6

PROJ = ([QKV_C + P * c for c in range(NQKV)] + [POOL_C + P * g for g in range(NG)]
        + [Z_C + P * h for h in range(H)] + [GATE_C + P * m for m in range(2 * KD)])
N_V, N_POOL, N_Z, N_GATE, N_PROJ = 2 * H, NQKV, NQKV + NG, NQKV + NG + H, len(PROJ)
IN_ITEMS = N_PROJ // 2
BP_ITEMS, BD_ITEMS, WO_ITEMS = 2, 4, 4
A_ITEMS = IN_ITEMS + BP_ITEMS + BD_ITEMS + WO_ITEMS

ARENA = 50560
CE = CW - 1 + TP
EW = CE + BD * (CW - 1 + TD)
PE0 = PBUF + TP
EPW = PE0 + BD * (PBUF + TD)
NACC = EW - (CW - 1)
RAWC = CE - (CW - 1)
RAWN = EW - RAWC

LEAD_GATES = 9
Z_AHEAD = 2
GATE_AT = {2 * j: N_GATE + LEAD_GATES + j for j in range(2 * KD - LEAD_GATES)}
STATE_AT = {2 * h + 2: h for h in range(H)}
BP_AT = {2 * d + 2: d for d in range(KD)}
KDD_AT, RTD_AT, VND_AT, OD_AT, ODT_AT = 1, 3, 5, 7, 9
OSQ = [n + 1 + (H if n >= ODT_AT - 1 else 0) for n in range(2 * H)]
DIAG_AT = (N_GATE + 2) // 2 + RA - 1
FIRST_LOADS = [*range(RA, 3 * QE), *[i % RA for i in range(A_ITEMS - RA, A_ITEMS)]]
WO_STEPS = [(t, j) for j in range(WO_ITEMS) for t in range(2)] + [(2, None)]
WO_PARTS = WO_STEPS[:-1] + [(2, j) for j in range(WO_ITEMS)]
PEEL = 2


def hybrid_step(nc, x_prompt, x_sample, cache_pool, cache_conv, state_delta, norm1_w, w_in, w_pool,
                pool_scale, w_conv, a_log, dt_bias, o_norm_w, w_branch_pool, w_branch_delta, w_out,
                norm2_w, w_router_group, b_router_group, w_router_expert, b_router_expert, w_gate,
                w_up, w_down, final_norm_w, y_prompt, y_sample, new_pool_prompt, new_conv_prompt,
                new_delta_prompt, new_pool_sample, new_conv_sample, new_delta_sample):
    x_rows = [x_prompt[0, 0:P, :], x_prompt[0, P:TP, :], x_sample.rearrange("b t d -> (b t) d")]
    y_rows = [y_prompt[0, 0:P, :], y_prompt[0, P:TP, :], y_sample.rearrange("b t d -> (b t) d")]

    def dram(name, shape, dt=F32):
        return nc.dram_tensor(name, shape, dt, kind="Internal").ap()

    def image(name):
        flat = dram(name, (8 * (16 * 2 * H * P + 16),))
        blocks = flat.rearrange("(m r) -> m r", m=8)[:, 0:16 * 2 * H * P]
        return (flat[0:P * 2 * H * P].rearrange("(p n) -> p n", p=P),
                blocks.rearrange("m (j g i) -> m j g i", j=16, g=2 * H)[:, :, :, 0:16])

    a_image, a_blocks = image("a_image")
    x_image, x_blocks = image("x_image")
    h2_dram = dram("h2_dram", (T, D))
    two_dram = dram("two_dram", (2 * T, D))

    with ExitStack() as ctx:
        def sb(name, shape, dt=F32):
            return ctx.enter_context(nc.sbuf_tensor(name, shape, dt))

        def sem(name):
            return ctx.enter_context(nc.semaphore(name))

        ps = [ctx.enter_context(nc.psum_tensor(f"ps{i}", [P, 512], F32)) for i in range(8)]

        arena = sb("arena", [P, ARENA])

        class Cut:
            def __init__(self, at):
                self.at = at

            def take(self, n, parts=P):
                self.at += n
                assert self.at <= ARENA, self.at
                return arena[0:parts, self.at - n:self.at]

        slots = [arena[:, SLOT * i:SLOT * (i + 1)] for i in range(2 * RA)]

        low = Cut(RA * SLOT)
        AT = low.take(2 * H * P).rearrange("p (g i) -> p g i", i=P)
        X = low.take(2 * H * P).rearrange("p (g i) -> p g i", i=P)
        XT = low.take(2 * H * P).rearrange("p (g i) -> p g i", i=P)
        aqT = low.take(2 * H * P).rearrange("p (g i) -> p g i", i=P)
        Sd = low.take(2 * BD * P).rearrange("p (u b v) -> p u b v", u=2, b=BD)
        rows_d = low.take(4 * H * TS).rearrange("p (r h i) -> p r h i", r=4, h=H)
        rbd_room = low.take(4 * H * TS)
        rbd = rbd_room[0:TS, :].rearrange("p (r h i) -> p r h i", r=4, h=H)
        assert low.at <= 2 * RA * SLOT
        conv_raw = arena[0:BD * (CW - 1), RA * SLOT:RA * SLOT + NQKV * P]
        pool_raw = arena[0:BD * PBUF, RA * SLOT + NQKV * P:RA * SLOT + NQKV * P + NG * P]
        pooled = Sd.rearrange("p u b v -> p (u b v)")[:, 0:NG * T].rearrange("p (g t) -> p g t", g=NG)
        dec = Cut(RA * SLOT)
        Rd = dec.take(H * P, TS).rearrange("p (h e) -> p h e", h=H)
        vnd = dec.take(H * P, TS).rearrange("p (h e) -> p h e", h=H)
        kdd = dec.take(H * P, TS).rearrange("p (h e) -> p h e", h=H)
        St = dec.take(H * P).rearrange("p (h v) -> p h v", h=H)
        vx = [v.rearrange("p (b e) -> p b e", b=BD) for v in
              (Rd.rearrange("p h e -> p (h e)"), St.rearrange("p h v -> p (h v)")[0:TS, :])]
        assert dec.at <= RA * SLOT + 2 * 2 * H * P

        high = Cut(2 * RA * SLOT)
        base_b = high.at
        hT = high.take(KD * T).rearrange("p (k t) -> p k t", k=KD)
        merged = hT
        qkvT = high.take(NQKV * T).rearrange("p (c t) -> p c t", c=NQKV)
        zT = high.take(H * T).rearrange("p (c t) -> p c t", c=H)
        gT = high.take(2 * KD * T).rearrange("p (c t) -> p c t", c=2 * KD)
        xt = gT.rearrange("p c t -> p (c t)")[:, 0:NT * D].rearrange("p (n d) -> p n d", n=NT)
        work0 = high.at
        E = [high.take(EW) for _ in range(3)]
        EP = [high.take(EPW) for _ in range(2)]
        C = [high.take(NACC) for _ in range(2)]
        SQ = [high.take(T) for _ in range(2)]
        wa = [Sd.rearrange("p u b v -> p (u b v)")[:, NG * T + EPW * j:NG * T + EPW * (j + 1)] for j in range(2)]
        work1 = high.at
        stage = high.take(NQKV * P)
        b_end = high.at
        oTok = stage.rearrange("p (n d) -> p n d", n=NT)
        ypT = high.take(NG * T).rearrange("p (g t) -> p g t", g=NG)
        cT = rows_d.rearrange("p r h i -> p (r h i)")[:, 0:NQKV * BD * (CW - 1)].rearrange("p (c r) -> p c r", c=NQKV)
        pcT = rbd_room[:, 0:NG * BD * PBUF].rearrange("p (c r) -> p c r", c=NG)
        RB = high.take(3 * TP).rearrange("p (r t) -> p r t", r=3)
        Dt = high.take(TP)
        egq = high.take(P)
        smallrows = RB[0:109, 0, 0:P]
        smallT = high.take(P)
        ident = high.take(P)
        ones = high.take(P)
        triU = high.take(P)
        lvl = [high.take(P) for _ in range(3)]
        rb_room = RB.rearrange("p r t -> p (r t)")
        wpool = rb_room[:, P:P + NG * P].rearrange("p (g d) -> p g d", g=NG)
        wab = rb_room[:, P + NG * P:P + NG * P + KD * 2 * H].rearrange("p (k n) -> p k n", k=KD)
        wk = Cut(work0)
        Xd = wk.take(256)
        And = wk.take(256)
        prod = wk.take(256)
        egd = wk.take(H * TS).rearrange("p (h i) -> p h i", h=H)
        tmpd = wk.take(H * TS).rearrange("p (h i) -> p h i", h=H)
        Dd = wk.take(H * TS).rearrange("p (h i) -> p h i", h=H)
        Nd = wk.take(H * TS).rearrange("p (h i) -> p h i", h=H)
        IAd = wk.take(H * TS).rearrange("p (h i) -> p h i", h=H)
        N2d = wk.take(H * TS).rearrange("p (h i) -> p h i", h=H)
        aqd = wk.take(H * TS).rearrange("p (h i) -> p h i", h=H)
        TTd = wk.take(H * TS, TS).rearrange("p (h i) -> p h i", h=H)
        assert wk.at <= work1, (wk.at, work1)
        am = [Dt, RB[:, 2, :]]
        Y = [RB[:, 0, :], RB[:, 1, :]]
        rbf = RB.rearrange("p r t -> p (r t)")
        R = [rbf[:, 0:P], rbf[:, P:2 * P]]
        vn = [rbf[:, 2 * P:3 * P], rbf[:, 3 * P:4 * P]]
        kd = [rbf[:, 4 * P:5 * P], rbf[:, 5 * P:6 * P]]
        osq = [prod[:, 0:P], prod[:, P:2 * P]]

        sc = sb("sc", [P, 640])
        scat = [0]

        def scal(*dims):
            n = 1
            for d in dims:
                n *= d
            v = sc[:, scat[0]:scat[0] + n]
            scat[0] += n
            assert scat[0] <= 640
            if len(dims) == 2:
                v = v.rearrange("p (a b) -> p a b", a=dims[0])
            return v

        ss1, rs1 = scal(NT), scal(NT)
        ab = scal(NT, 2 * H)
        beta, g_ = scal(NT, H), scal(NT, H)
        t1, t2, t3, t4 = scal(NT, H), scal(NT, H), scal(NT, H), scal(NT, H)
        Gc, Gl = scal(NT, H), scal(NT, H)
        rqk = scal(NT, 2 * H)
        brk, nber, kds, eGl = scal(NT, H), scal(NT, H), scal(NT, H), scal(NT, H)
        eGd = scal(H, BD)
        oss, orr = scal(NT, H), scal(NT, H)
        gbd = scal(H, BD)
        sb_small = sb("sb_small", [P, 64])
        dtb, alog = sb_small[:, 8:8 + H], sb_small[:, 16:16 + H]
        bmask, invc = sb_small[:, 24:24 + BD], sb_small[:, 32:48]
        U4 = sb("U4", [TS, TS])
        B4 = sb("B4", [TS, TS])
        S4 = sb("S4", [TS, TS])

        qk_at = base_b + KD * T
        b = Cut(qk_at)
        x2 = b.take(NT * D).rearrange("p (n d) -> p n d", n=NT)
        xr = b.take(NT * D).rearrange("p (n d) -> p n d", n=NT)
        h2 = xr
        column_no = b.take(P)
        strU = b.take(P)
        assert b.at <= qk_at + NQKV * T
        b = Cut(qk_at + NQKV * T)
        n2b = b.take(D)
        fnb = b.take(D)
        h2T = b.take(KD * T).rearrange("p (k t) -> p k t", k=KD)
        xg = [b.take(D) for _ in range(2)]
        xgT_room = b.take(2 * KD * P)
        xgT = [xgT_room[:, KD * P * j:KD * P * (j + 1)].rearrange("p (k t) -> p k t", k=KD) for j in range(2)]
        sg = [b.take(FE) for _ in range(2)]
        act_ = [b.take(FE) for _ in range(2)]
        actT = [b.take(FE).rearrange("p (c t) -> p c t", c=2) for _ in range(2)]
        assert b.at <= b_end, (b.at, b_end)
        b = Cut(base_b)
        dn = [b.take(D) for _ in range(2)]
        assert b.at <= qk_at
        slot_1h = xgT_room[:, 0:NT * 2 * P].rearrange("p (n k s) -> p n k s", n=NT, k=2)
        quad_1h = xgT_room[:, NT * 2 * P:NT * 2 * (P + TBL)].rearrange("p (n k s) -> p n k s", n=NT, k=2)
        spare = [h2.rearrange("p n d -> p (n d)")[:, 0:SLOT], h2T.rearrange("p k t -> p (k t)")[:, 0:SLOT]]
        yb = Cut(qk_at + NT * D)
        yg = [yb.take(2 * D), xgT_room[:, 0:2 * D], h2T.rearrange("p k t -> p (k t)")[:, 0:2 * D]]

        wr = sb("wr", [P, KD, 36])
        rb_ = sb("rb_", [P, 36])
        r = sb("r", [P, NT, 36 + 12 * 8 + 7 * 32])
        tok1 = sb("tok1", [P, NT, 2])
        mi = sb("mi", [P, NT, 16], U32)
        beyond = sb("beyond", [P, TBL])
        put = sb("put", [P, TBL], I32)
        get = sb("get", [P, TBL], I32)
        idc = sb("idc", [P, 4], I32)
        ecst = sb("ecst", [P, 3, NE])
        over = sb("over", [P, ROUNDS])
        more_i = sb("more_i", [P, 1], I32)
        ones_eps = sb_small[:, 0:1]
        RTd, oTd = N2d, IAd
        sdv = ps[7][:, :].rearrange("p (h r t) -> p h r t", h=H, r=2)

        rcat = [0]

        def rcut(*dims):
            n = 1
            for d in dims:
                n *= d
            v = r[:, :, rcat[0]:rcat[0] + n]
            rcat[0] += n
            assert rcat[0] <= r.shape[2]
            return v.rearrange("p t (a b) -> p t a b", a=dims[0]) if len(dims) == 2 else v

        lg, lg8, mx8, les = rcut(NGR + NE), rcut(8), rcut(8), rcut(EPG)
        prodr = rcut(NGR, EPG)
        oh, prode = rcut(2, NE), rcut(2, NE)
        picks, rk_ = rcut(NE), rcut(NE)
        eg4, ed, gs, goh, eid = rcut(NGR), rcut(1), rcut(1), rcut(NGR), rcut(2)
        pg, w12, rank, rnd, quad, slot = rcut(1), rcut(2), rcut(2), rcut(2), rcut(2), rcut(2)
        full = rcut(2, ROUNDS - 1)
        cnt, itf, itc = sb_small[:, 1:2], sb_small[:, 2:3], sb_small[:, 48:48 + ROUNDS]

        class Sems(dict):
            def __missing__(self, n):
                self[n] = sem(n)
                return self[n]

        S = Sems()
        ring_in = [sem(f"ring_in{i}") for i in range(2 * RA)]

        def item_read(i):
            if i < IN_ITEMS:
                return S["proj"], 2 * i + 2
            i -= IN_ITEMS
            if i < BP_ITEMS:
                return S["bp_pe"], 4 * (i + 1)
            i -= BP_ITEMS
            if i < BD_ITEMS:
                return S["bd_pe"], 2 * (i + 1)
            return S["wo_pe"], len(WO_STEPS)

        free = [0] * N_PROJ
        for n in range(N_PROJ):
            free[n] = (free[n - 1] if n else 0) + (2 if n < N_POOL else 3 if n < N_Z else 1)

        block = ctx.enter_context(nc.Block())

        @block.sync
        def _(sp):
            for n in range(NT):
                sp.dma_start(xt[0:TILES[n], n, :], x_rows[n]).then_inc(S["x_in"], 16)
            sp.dma_start(wab, w_in[0, :, AB_C:Z_C].rearrange("(k p) n -> p k n", p=P)).then_inc(S["misc_in"], 16)

            def diagonal_blocks():
                sp.wait_ge(S["memsets"], 1)
                sp.dma_start(x_image, X.rearrange("p g i -> p (g i)")).then_inc(S["diag"], 16)
                sp.wait_ge(S["prep_done"], H)
                sp.dma_start(a_image, AT.rearrange("p g i -> p (g i)")).then_inc(S["diag"], 16)
                sp.wait_ge(S["diag"], 16 * 2)
                for m in range(8):
                    sp.dma_start(And[16 * m:16 * m + 16, :].rearrange("g (j i) -> g j i", i=16),
                                 a_blocks[m].rearrange("j g i -> g j i")).then_inc(S["diag"], 16)
                sp.wait_ge(S["sub_done"], 1)
                for m in range(8):
                    sp.dma_start(x_blocks[m].rearrange("i g c -> g i c"),
                                 Xd[16 * m:16 * m + 16, :].rearrange("g (i c) -> g i c", i=16)).then_inc(S["diag"], 16)
                sp.wait_ge(S["diag"], 16 * 18)
                sp.dma_start(X.rearrange("p g i -> p (g i)"), x_image).then_inc(S["diag"], 16)

            for i in range(A_ITEMS):
                if i >= RA:
                    s, v = item_read(i - RA)
                    sp.wait_ge(s, v)
                to = slots[i % RA]
                if i < IN_ITEMS:
                    c = PROJ[2 * i]
                    src = w_in[0, :, c:c + 256].rearrange("(k p) n -> p k n", p=P)
                elif i < IN_ITEMS + BP_ITEMS:
                    c = 512 * (i - IN_ITEMS)
                    src = w_branch_pool[0, :, c:c + 512].rearrange("(k p) n -> p k n", p=P)
                else:
                    j = i - IN_ITEMS - BP_ITEMS
                    w = w_branch_delta if j < BD_ITEMS else w_out
                    c = 256 * (j % BD_ITEMS)
                    src = w[0, :, c:c + 256].rearrange("(k p) n -> p k n", p=P)
                sp.dma_start(to.rearrange("p (k n) -> p k n", n=src.shape[2]), src).then_inc(ring_in[i % RA], 16)
                if i == DIAG_AT:
                    diagonal_blocks()

            def expert_weights(i, u, w):
                q = 2 * i + u
                for j in range(3 * QE):
                    part, e = divmod(j, QE)
                    if e == 0:
                        sp.wait_ge(S[("m_gate", "m_up", "m_dn")[part]], q)
                    if u == 1 and j < 2 and isinstance(i, int):
                        continue
                    slot_load(j, (w_gate, w_up, w_down)[part], w + e)

            def slot_load(j, t, e, to=None):
                src = t[0, e] if isinstance(e, int) else t[0, bass.ds(e, 1)].rearrange("e a b -> (e a) b")
                a = src.shape[0] // P
                sp.dma_start((slots[j] if to is None else to).rearrange("p (a n) -> p a n", a=a),
                             src.rearrange("(p a) n -> p a n", a=a)).then_inc(ring_in[j] if to is None else S[f"spare_in{j}"], 16)

            sp.wait_ge(S["y_done"], 6)
            sp.wait_ge(S["sd_out"], 16 * H)
            for j in FIRST_LOADS:
                if j < RA:
                    s, v = item_read(max(i for i in range(A_ITEMS) if i % RA == j))
                    sp.wait_ge(s, v)
                slot_load(j, (w_gate, w_up, w_down)[j // QE], j % QE)
            sp.wait_ge(S["h2_out"], 16 * NT)
            sp.wait_ge(S["h2_t"], 6)
            slot_load(0, w_gate, QE, spare[0])
            sp.wait_ge(S["route_pe"], 1)
            slot_load(1, w_gate, QE + 1, spare[1])
            expert_weights(0, 1, QE)
            sp.wait_ge(S["route"], 1)
            end = sp.value_load(more_i[0:1, 0:1], min_val=0, max_val=MORE_MAX) + QUADS // 2
            with sp.Fori(1, end) as i:
                for u in range(2):
                    expert_weights(i, u, (i % (QUADS // 2)) * (2 * QE) + QE * u)
            for n, m in enumerate(TILES):
                sp.wait_ge(S["fin_y"], 1 + n)
                sp.dma_start(y_rows[n], x2[0:m, n, :]).then_inc(S["yout"], 16)
            sp.wait_ge(S["yout"], 16 * NT)

        @block.gpsimd
        def _(pool):
            chain = [0]

            def link(ins):
                chain[0] += 1
                ins.then_inc(S["pool_chain"], 1)
                pool.wait_ge(S["pool_chain"], chain[0])

            def fill(view, parts, pattern, base, mult, op, keep=1.0, other=0.0):
                link(nc.gpsimd.memset(view, keep))
                link(nc.gpsimd.affine_select(out=view, in_=view, compare_op=op, fill=other, base=base,
                                             pattern=pattern, channel_multiplier=mult))

            link(nc.gpsimd.memset(ident, 1.0))
            nc.gpsimd.affine_select(out=ident, in_=ident, compare_op=ALU.is_equal, fill=0.0, base=0,
                                    pattern=[[1, P]], channel_multiplier=-1).then_inc(S["ident"], 1)
            link(nc.gpsimd.memset(ones, 1.0))
            fill(triU, P, [[1, P]], 0, -1, ALU.is_ge)
            for u in (U4, B4, S4):
                link(nc.gpsimd.memset(u[:, :], 1.0))
                v = u[:, :].rearrange("p (b t) -> p b t", t=TD)
                link(nc.gpsimd.affine_select(out=v, in_=v, compare_op=ALU.is_ge, fill=0.0, base=0,
                                             pattern=[[-TD, BD], [0, TD]], channel_multiplier=1))
                link(nc.gpsimd.affine_select(out=v, in_=v, compare_op=ALU.is_ge, fill=0.0, base=TD - 1,
                                             pattern=[[TD, BD], [0, TD]], channel_multiplier=-1))
            for u, b0 in ((U4, 0), (S4, -1)):
                link(nc.gpsimd.affine_select(out=u[:, :], in_=u[:, :], compare_op=ALU.is_ge, fill=0.0, base=b0,
                                             pattern=[[1, TS]], channel_multiplier=-1))
            for s, m in zip((16, 32, 64), lvl):
                link(nc.gpsimd.memset(m, 0.0))
                for q in range(P // (2 * s)):
                    sub = m[:, 2 * s * q + s:2 * s * (q + 1)]
                    link(nc.gpsimd.memset(sub, 1.0))
                    link(nc.gpsimd.affine_select(out=sub, in_=sub, compare_op=ALU.is_ge, fill=0.0,
                                                 base=-2 * s * q, pattern=[[0, s]], channel_multiplier=1))
                    link(nc.gpsimd.affine_select(out=sub, in_=sub, compare_op=ALU.is_ge, fill=0.0,
                                                 base=2 * s * q + s - 1, pattern=[[0, s]], channel_multiplier=-1))
            link(nc.gpsimd.memset(bmask, 1.0))
            link(nc.gpsimd.affine_select(out=bmask, in_=bmask, compare_op=ALU.is_ge, fill=0.0, base=0,
                                         pattern=[[-TD, BD]], channel_multiplier=1))
            link(nc.gpsimd.affine_select(out=bmask, in_=bmask, compare_op=ALU.is_ge, fill=0.0, base=TD - 1,
                                         pattern=[[TD, BD]], channel_multiplier=-1))
            link(nc.gpsimd.iota(invc, pattern=[[1, 16]], base=1, channel_multiplier=0,
                                allow_small_or_imprecise_dtypes=True))
            for j, pattern in enumerate(([[1, NE]], [[1, QUADS], [0, QE]], [[0, QUADS], [CAP, QE]])):
                link(nc.gpsimd.iota(ecst[:, j, :] if j == 0 else ecst[:, j, :].rearrange("p (a b) -> p a b", b=QE),
                                    pattern=pattern, base=0, channel_multiplier=0, allow_small_or_imprecise_dtypes=True))
            link(nc.gpsimd.iota(over[:, :], pattern=[[CAP, ROUNDS]], base=0, channel_multiplier=0,
                                allow_small_or_imprecise_dtypes=True))
            link(nc.gpsimd.iota(tok1[:, :, :], pattern=[[2 * P, NT], [1, 2]], base=1, channel_multiplier=2,
                                allow_small_or_imprecise_dtypes=True))
            nc.gpsimd.iota(beyond[:, :], pattern=[[1, TBL]], base=SKIP + 1, channel_multiplier=TBL,
                           allow_small_or_imprecise_dtypes=True).then_inc(S["masks"], 1)
            pool.wait_ge(S["masks"], 1)
            for e in E:
                link(nc.gpsimd.memset(e[:, 0:CW - 1], 0.0))
            for e in EP:
                ins = nc.gpsimd.memset(e[:, 0:PBUF], 0.0)
                if e is EP[0]:
                    link(ins)
            ins.then_inc(S["pads"], 1)
            pool.wait_ge(S["small_ev"], 4)
            for n in range(NQKV):
                if n >= 3:
                    pool.wait_ge(S["conv"], n - 2)
                    pool.wait_ge(S["raw_t"], n - 2)
                nc.gpsimd.tensor_copy(
                    E[n % 3][:, CE:EW].rearrange("p (b r) -> p b r", b=BD)[:, :, 0:CW - 1],
                    cT[:, n, :].rearrange("p (b r) -> p b r", b=BD)).then_inc(S["e_cache"], 1)
            for g in range(NG):
                if g >= 2:
                    pool.wait_ge(S["pool_dve"], g - 1)
                    pool.wait_ge(S["newp_t"], g - 1)
                nc.gpsimd.tensor_copy(
                    EP[g % 2][:, PE0:EPW].rearrange("p (b r) -> p b r", b=BD)[:, :, 0:PBUF],
                    pcT[:, g, :].rearrange("p (b r) -> p b r", b=BD)).then_inc(S["e_cache"], 1)
            nc.gpsimd.memset(X, 0.0).then_inc(S["memsets"], 1)
            pool.wait_ge(S["pool_dve"], NG)
            pool.wait_ge(S["newp_t"], NG)
            link(nc.gpsimd.memset(Xd, 0.0))
            xd = Xd.rearrange("p (i c) -> p i c", i=16)
            nc.gpsimd.affine_select(out=xd, in_=xd, compare_op=ALU.not_equal, fill=1.0, base=0,
                                    pattern=[[1, 16], [-1, 16]], channel_multiplier=0).then_inc(S["memsets"], 1)
            def spread(v, m, n):
                return v.unsqueeze(2).to_broadcast([m, v.shape[1], n])

            pool.wait_ge(S["conv"], NQKV)
            pool.wait_ge(S["wp_pe"], NG)
            for h in range(H):
                if h >= 1:
                    pool.wait_ge(S["rows"], h)
                for j, (mask, v) in enumerate(((triU, g_[:, 0:2, h]), (ident, brk[:, 0:2, h]), (ident, rqk[:, 0:2, h]))):
                    nc.gpsimd.tensor_tensor(RB[:, j, :].rearrange("p (c t) -> p c t", c=2),
                                            mask.unsqueeze(1).to_broadcast([P, 2, P]), spread(v, P, P),
                                            ALU.mult).then_inc(S["rb"], 1)
            vals = (g_, brk, rqk[:, :, 0:H], beta)
            for j in range(4):
                mask = U4[:, :] if j == 0 else ident[0:TS, 0:TS]
                nc.gpsimd.tensor_tensor(rbd[:, j], mask.unsqueeze(1).to_broadcast([TS, H, TS]),
                                        spread(vals[j][0:TS, 2, :], TS, TS), ALU.mult).then_inc(S["decrb"], 1)

            for h in range(H):
                pool.wait_ge(S[f"s2_in{h % 2}"], 16 * (h // 2 + 1))
                nc.gpsimd.tensor_tensor(Sd[:, h % 2], Sd[:, h % 2],
                                        eGd[:, h, :].unsqueeze(2).to_broadcast([P, BD, P]),
                                        ALU.mult).then_inc(S["sd_mul"], 1)

            pool.wait_ge(S["sq_sum"], NT + NT * WO_ITEMS)
            for u in range(2):
                link(nc.gpsimd.memset(xg[u], 0.0))
            fill(strU, P, [[1, P]], -1, -1, ALU.is_ge)
            nc.gpsimd.iota(column_no, pattern=[[1, P]], base=0, channel_multiplier=0,
                           allow_small_or_imprecise_dtypes=True).then_inc(S["cols"], 1)
            pool.wait_ge(S["get_done"], 1)
            pool.wait_ge(S["h2_out"], 16 * NT)
            last_row = pool.alloc_register("last_row")
            pool.reg_mov(last_row, T - 1)
            last_two = pool.alloc_register("last_two")
            pool.reg_mov(last_two, 2 * T - 1)

            def column(table, p, to, n):
                src = table[:, p:p + 1] if isinstance(p, int) else table[:, bass.ds(p, 1)]
                nc.gpsimd.tensor_copy(idc[:, to:to + 1], src).then_inc(S["idc_done"], 1)
                pool.wait_ge(S["idc_done"], n)
                pool.sem_inc(S["idc_seen"], 1)

            def gather(p, u, n):
                if not isinstance(p, int) or p >= 2:
                    pool.wait_ge(S["m_T"], p - 1)
                column(get, p, u, n)
                pool.indirect_dma_start(
                    out=xg[u], out_offset=None, in_=h2_dram[:, :],
                    in_offset=bass.IndirectOffsetOnAxis(ap=idc[:, u:u + 1], axis=0),
                    bounds_check=last_row, oob_is_err=False).then_inc(S[f"gather{u}"], 16)

            def scatter(q, v, n):
                pool.wait_ge(S["m_dnA"], q + 1)
                pool.wait_ge(S["m_dnV"], q + 1)
                column(put, q, 2 + v, n)
                pool.indirect_dma_start(
                    out=two_dram[:, :], out_offset=bass.IndirectOffsetOnAxis(ap=idc[:, 2 + v:3 + v], axis=0),
                    in_=dn[v], in_offset=None,
                    bounds_check=last_two, oob_is_err=False).then_inc(S[f"dn_out{v}"], 16)

            for p in range(2 * PEEL):
                gather(p, p % 2, p + 1 if p < 3 else 2 * p - 2)
                if p >= 3:
                    scatter(p - 3, (p - 3) % 2, 2 * p - 1)
            end = pool.value_load(more_i[0:1, 0:1], min_val=0, max_val=MORE_MAX) + QUADS // 2
            with pool.Fori(PEEL, end) as i:
                for u in range(2):
                    gather(2 * i + u, u, i * 4 + (2 * u - 2))
                    scatter(2 * i + (u - 3), 1 - u, i * 4 + (2 * u - 1))
            for j in (3, 2, 1):
                scatter(end * 2 - j, j % 2, end * 4 + (1 - j))

        @block.scalar
        def _(act):
            chain = [0]

            def link(ins):
                chain[0] += 1
                ins.then_inc(S["act_chain"], 1)
                act.wait_ge(S["act_chain"], chain[0])

            for a, rows in ((w_conv[0].rearrange("j (c p) -> (j c) p", p=P), (0, 96)),
                            (norm1_w[0].rearrange("(k p) -> k p", p=P), (96, 104)),
                            (pool_scale[0].rearrange("(k p) -> k p", p=P), (104, 108)),
                            (o_norm_w, (108, 109))):
                act.dma_start(smallrows[rows[0]:rows[1], :], a).then_inc(S["small_in"], 16)
            act.dma_start(conv_raw, cache_conv[0].rearrange("b r c -> (b r) c")).then_inc(S["cache_in"], 16)
            act.dma_start(pool_raw, cache_pool[0].rearrange("b r c -> (b r) c")).then_inc(S["cache_in"], 16)
            def load_state(h, again):
                act.dma_start(Sd[:, h % 2], state_delta[0, :, h].rearrange("b k v -> k b v")).then_inc(
                    S[f"s{'2' if again else ''}_in{h % 2}"], 16)

            act.wait_ge(S["x_in"], 16 * NT)
            act.wait_ge(S["sc_one"], 1)
            for n, m in enumerate(TILES):
                nc.scalar.activation(hT.rearrange("p k t -> p (k t)")[0:m, 0:D], xt[0:m, n, :], ACT.Square,
                                     accum_out=ss1[0:m, n:n + 1]).then_inc(S["sq_sum"], 1)
                act.wait_ge(S["sq_sum"], n + 1)
            act.wait_ge(S["mean_sq"], 1)
            nc.scalar.activation(rs1, rs1, ACT.Sqrt).then_inc(S["root"], 1)
            for to, src in ((dtb, dt_bias.partition_broadcast(P).rearrange("p a b -> p (a b)")),
                            (alog, a_log.partition_broadcast(P).rearrange("p a b -> p (a b)")),
                            (wpool, w_pool[0].rearrange("g c d -> c g d")),
                            (wr[:, :, 0:NGR], w_router_group[0].rearrange("(p k) g -> p k g", k=KD)),
                            (wr[:, :, NGR:NGR + NE], w_router_expert[0].rearrange("(p k) g e -> p k (g e)", k=KD)),
                            (rb_[:, 0:NGR], b_router_group.partition_broadcast(P).rearrange("p a b -> p (a b)")),
                            (rb_[:, NGR:NGR + NE], b_router_expert.partition_broadcast(P).rearrange("p a b c -> p (a b c)"))):
                act.dma_start(to, src).then_inc(S["misc_in"], 16)
            act.dma_start(new_pool_sample[0, :, 0:PBUF - TD, :], cache_pool[0, :, TD:PBUF, :]).then_inc(S["out_dma"], 16)

            def evac(n):
                act.wait_ge(S["proj"], n + 1)
                src = ps[n % 2]
                if n < NQKV:
                    if n >= 3:
                        act.wait_ge(S["conv"], n - 2)
                        act.wait_ge(S["raw_t"], n - 2)
                    else:
                        act.wait_ge(S["pads"], 1)
                    dst, at, lead, w = E[n % 3], CW - 1, CE, CW - 1
                elif n < N_Z:
                    g = n - NQKV
                    if g >= 2:
                        act.wait_ge(S["pool_dve"], g - 1)
                        act.wait_ge(S["newp_t"], g - 1)
                    dst, at, lead, w = EP[g % 2], PBUF, PE0, PBUF
                if n < N_Z:
                    nc.scalar.activation(dst[:, at:at + TP], src[:, 0:TP], ACT.Copy).then_inc(S["proj_free"], 1)
                    nc.scalar.activation(dst[:, lead:].rearrange("p (b r) -> p b r", b=BD)[:, :, w:],
                                         src[:, TP:T].rearrange("p (b t) -> p b t", b=BD),
                                         ACT.Copy).then_inc(S["proj_free"], 1)
                    if n >= N_POOL:
                        nc.scalar.activation(C[n % 2][:, 0:TS], src[:, TP:T], ACT.Copy).then_inc(S["proj_free"], 1)
                elif n < N_GATE:
                    nc.scalar.activation(zT[:, n - N_Z, :], src[:, 0:T], ACT.Silu).then_inc(S["proj_free"], 1)
                else:
                    nc.scalar.activation(gT[:, n - N_GATE, :], src[:, 0:T], ACT.Tanh, scale=0.5).then_inc(S["proj_free"], 1)

            def silu(n):
                act.wait_ge(S["conv"], n + 1)
                nc.scalar.activation(qkvT[:, n, 0:TP], C[n % 2][:, 0:TP], ACT.Silu).then_inc(S["silu"], 1)
                nc.scalar.activation(qkvT[:, n, TP:T - TD].rearrange("p (b t) -> p b t", t=TD),
                                     C[n % 2][:, CE:CE + 7 * (BD - 1)].rearrange("p (b t) -> p b t", t=7)[:, :, 0:TD],
                                     ACT.Silu).then_inc(S["silu"], 1)
                nc.scalar.activation(qkvT[:, n, T - TD:T], C[n % 2][:, NACC - TD:NACC], ACT.Silu).then_inc(S["silu"], 1)
                if n < N_V:
                    if n >= 2:
                        act.wait_ge(S["ssd"], n - 1)
                    act.wait_ge(S["silu"], 3 * n + 3)
                    nc.scalar.activation(SQ[n % 2], qkvT[:, n, :], ACT.Square).then_inc(S["sqd"], 1)

            def raw_rows(j):
                act.wait_ge(S["raw_t"], 4 * j + 4)
                nc.scalar.activation(stage[0:RAWN, 512 * j:512 * j + 512], ps[2 + j % 2][0:RAWN, :],
                                     ACT.Copy).then_inc(S["raw_ev"], 1)

            for n in range(NQKV):
                evac(n)
                if n >= 1:
                    silu(n - 1)
                if n == 2:
                    act.wait_ge(S["ab_ev"], 1)
                    nc.scalar.activation(t2, t2, ACT.Exp, scale=-1.0).then_inc(S["soft"], 1)
                    nc.scalar.activation(beta, ab[:, :, 0:H], ACT.Exp, scale=-1.0).then_inc(S["soft"], 1)
                    nc.scalar.activation(alog, alog, ACT.Exp).then_inc(S["soft"], 1)
                    act.wait_ge(S["ab_ev"], 2)
                    nc.scalar.activation(t3, t4, ACT.Ln).then_inc(S["soft"], 1)
                if n == 6:
                    act.wait_ge(S["g_scal"], 1)
                    nc.scalar.activation(t1, Gc, ACT.Exp).then_inc(S["g_exp"], 1)
                    nc.scalar.activation(kds, kds, ACT.Exp).then_inc(S["g_exp"], 1)
                    nc.scalar.activation(eGl, Gl, ACT.Exp).then_inc(S["g_exp"], 1)
                    nc.scalar.activation(eGd, eGd, ACT.Exp).then_inc(S["g_exp"], 1)
                if n % 4 == 1 and n >= 5:
                    raw_rows(n // 4 - 1)
                if n == N_V + 2:
                    act.wait_ge(S["ss_sc"], 1)
                    nc.scalar.activation(rqk, rqk, ACT.Sqrt).then_inc(S["ss_sqrt"], 1)
            silu(NQKV - 1)
            raw_rows(NQKV // 4 - 1)
            act.wait_ge(S["raw_ev"], NQKV // 4)
            act.dma_start(new_conv_prompt[0, 0], stage[0:CW - 1, :]).then_inc(S["stage_out"], 16)
            for b_ in range(BD):
                at = CW - 1 + 7 * b_ + TD
                act.dma_start(new_conv_sample[0, b_], stage[at:at + CW - 1, :]).then_inc(S["stage_out"], 16)

            def rows_exp(h):
                act.wait_ge(S["dt"], 2 * h + 2)
                nc.scalar.activation(egq, ps[3][:, P:TP], ACT.Exp).then_inc(S["expd"], 1)
                nc.scalar.activation(Dt, Dt, ACT.Exp).then_inc(S["expd"], 1)

            def pool_rows(g):
                act.wait_ge(S["wp_pe"], g + 1)
                nc.scalar.activation(ypT[:, g, :], ps[7][:, 0:T], ACT.Copy,
                                     scale=smallT[:, 104 + g:105 + g]).then_inc(S["wp_ev"], 1)

            for n in range(N_POOL, N_Z):
                evac(n)
            act.wait_ge(S["stage_out"], 16 * (1 + BD))
            act.wait_ge(S["newp_t"], NG)
            nc.scalar.activation(stage[0:PBUF, 0:512], ps[2][0:PBUF, :], ACT.Copy).then_inc(S["newp_ev"], 1)
            nc.scalar.activation(stage[0:TS, 512:1024], ps[6][0:TS, :], ACT.Copy).then_inc(S["newp_ev"], 1)
            act.wait_ge(S["newp_ev"], 2)
            act.dma_start(new_pool_prompt[0, 0], stage[0:PBUF, 0:512]).then_inc(S["newo"], 16)
            for b_ in range(BD):
                act.dma_start(new_pool_sample[0, b_, PBUF - TD:PBUF, :],
                              stage[TD * b_:TD * b_ + TD, 512:1024]).then_inc(S["newo"], 16)
            for n in range(Z_AHEAD):
                evac(N_Z + n)
            for g in range(NG):
                pool_rows(g)
            for h in range(H):
                rows_exp(h)
                evac(N_Z + Z_AHEAD + h)
            evac(N_Z + Z_AHEAD + H)

            act.wait_ge(S["decrows"], 1)
            rows_f = rows_d.rearrange("p r h i -> p (r h i)")
            nc.scalar.activation(rows_f[:, 0:512], ps[3][:, :], ACT.Copy).then_inc(S["dec_act"], 1)
            nc.scalar.activation(rows_f[:, 512:1024], ps[4][:, :], ACT.Copy).then_inc(S["dec_act"], 1)
            act.wait_ge(S["dec_act"], 1)
            nc.scalar.activation(egd, rows_d[:, 0], ACT.Exp).then_inc(S["dec_act"], 1)
            act.wait_ge(S["decdve"], 1)
            nc.scalar.activation(Dd[0:TS], Dd[0:TS], ACT.Exp).then_inc(S["dec_act"], 1)
            for h in range(2):
                load_state(h, False)
            for n in range(N_GATE + 3, N_GATE + LEAD_GATES):
                evac(n)

            for j in range(4):
                act.wait_ge(S["xt_pe"], j + 1)
                nc.scalar.activation(XT[:, 4 * j:4 * j + 4, :].rearrange("p g i -> p (g i)"), ps[2 + j][:, :],
                                     ACT.Copy).then_inc(S["xt_ev"], 1)
            for n in range(3 * H):
                if n in GATE_AT:
                    evac(GATE_AT[n])
                act.wait_ge(S["y_pe"], n + 1)
                if n >= 2:
                    act.wait_ge(S["xx_pe"], n - 1)
                nc.scalar.activation(Y[n % 2], ps[2 + n % 2][:, 0:TP], ACT.Copy).then_inc(S["y_ev"], 1)
                if n - 1 in STATE_AT:
                    h = STATE_AT[n - 1]
                    act.wait_ge(S["sd_pe"], h + 1)
                    load_state((h + 2) % H, h + 2 >= H)

            def scan_vn(n):
                act.wait_ge(S["vn_pe"], n + 1)
                if n >= 2:
                    act.wait_ge(S["s_pe"], n - 1)
                nc.scalar.activation(vn[n % 2], ps[4][:, 0:P], ACT.Copy).then_inc(S["vn_ev"], 1)

            squares = [0]

            def o_square(src, t, h):
                n, m = squares[0], TILES[t]
                squares[0] += 1
                if n >= 2:
                    act.wait_ge(S["osq"], n - 1)
                nc.scalar.activation(osq[n % 2][0:m], src, ACT.Square,
                                     accum_out=oss[0:m, t, h:h + 1]).then_inc(S["osq"], 1)

            def scan_o(n):
                c, h = divmod(n, H)
                act.wait_ge(S["o_pe"], n + 1)
                src = ps[6][:, 0:P]
                nc.scalar.activation(oTok[:, c, h * P:(h + 1) * P], src, ACT.Copy)
                o_square(src, c, h)

            act.wait_ge(S["newo"], 16 * (1 + BD))
            for n in range(2 * H + 1):
                if n in (RTD_AT, VND_AT, ODT_AT):
                    done, to = {RTD_AT: ("rtd_t", Rd), VND_AT: ("vnd_pe", vnd), ODT_AT: ("od_t", None)}[n]
                    act.wait_ge(S[done], 1)
                    for j in range(2):
                        dst = oTok[0:TS, 2, 512 * j:512 * j + 512] if to is None else to[:, 4 * j:4 * j + 4, :].rearrange("p h e -> p (h e)")
                        nc.scalar.activation(dst, ps[5 + 2 * j][0:TS, :], ACT.Copy).then_inc(S["dec_ev"], 1)
                    if n == ODT_AT:
                        for h in range(H):
                            o_square(ps[5 + 2 * (h // 4)][0:TS, P * (h % 4):P * (h % 4) + P], 2, h)
                if n < 2 * H:
                    scan_vn(n)
                if n >= 1:
                    scan_o(n - 1)
            act.wait_ge(S["s_ev"], 2 * H)
            act.dma_start(new_delta_prompt[0, 0].rearrange("h k v -> k h v"), St).then_inc(S["out_dma"], 16)

            act.wait_ge(S["mean_sq"], 1 + 1)
            nc.scalar.activation(orr, orr, ACT.Sqrt).then_inc(S["root"], 1)

            for h in range(H):
                act.wait_ge(S["sdn_dve"], 2 * h + 2)
                act.dma_start(new_delta_sample[0, :, h].rearrange("b k v -> k b v"), Sd[:, h % 2]).then_inc(S["sd_out"], 16)
                if h + 2 < H:
                    act.wait_ge(S["sd_out"], 16 * (h + 1))
                    load_state(h + 2, True)

            act.wait_ge(S["y_done"], 6)
            for n, m in enumerate(TILES):
                act.dma_start(xr[0:m, n, :], x_rows[n]).then_inc(S["xr_in"], 16)
            act.wait_ge(S["bd_dve"], KD)
            act.dma_start(n2b, norm2_w.partition_broadcast(P).rearrange("p a b -> p (a b)")).then_inc(S["nb_in"], 16)
            act.dma_start(fnb, final_norm_w.partition_broadcast(P)).then_inc(S["nb_in"], 16)

            for n, (t, j) in enumerate(WO_PARTS):
                m = TILES[t]
                act.wait_ge(S["wo_dve"], n + 1)
                if n >= 8:
                    act.wait_ge(S["sq_sum"], NT + n - 7)
                nc.scalar.activation(xg[n // 4 % 2][0:m, 256 * (n % 4):256 * (n % 4) + 256], x2[0:m, t, 256 * j:256 * j + 256],
                                     ACT.Square, accum_out=oss[0:m, t, j:j + 1]).then_inc(S["sq_sum"], 1)
            act.wait_ge(S["mean_sq"], 2 + 1)
            nc.scalar.activation(rs1, rs1, ACT.Sqrt).then_inc(S["root"], 1)
            for n, m in enumerate(TILES):
                act.wait_ge(S["h2_dve"], 1 + n)
                act.dma_start(h2_dram[P * n:P * n + m, :], h2[0:m, n, :]).then_inc(S["h2_out"], 16)
            for t, m in enumerate(TILES):
                for j in range(2):
                    act.wait_ge(S["h2_t"], 2 * t + j + 1)
                    nc.scalar.activation(h2T[:, 4 * j:4 * j + 4, P * t:P * t + m],
                                         ps[NT * j + t][:, 0:4 * m].rearrange("p (k t) -> p k t", k=4),
                                         ACT.Copy).then_inc(S["h2_ev"], 1)
            act.wait_ge(S["rt_d"], 1)
            nc.scalar.activation(eg4, eg4, ACT.Exp).then_inc(S["rt_e"], 1)
            act.wait_ge(S["rt_d"], 2)
            nc.scalar.activation(ed, ed, ACT.Exp).then_inc(S["rt_e"], 1)
            act.wait_ge(S["route"], 1)

            def wait_from(s, v):
                if not isinstance(v, int) or v >= 1:
                    act.wait_ge(s, v)

            def quad_acts(i, u):
                q = 2 * i + u
                act.wait_ge(S["m_T"], q + 1)
                nc.scalar.activation(xgT[u][:, 4:8, :].rearrange("p k t -> p (k t)"), ps[1][:, :],
                                     ACT.Copy).then_inc(S["m_TevA"], 1)
                act.wait_ge(S["m_gate"], q + 1)
                wait_from(S["m_act"], q - 1)
                nc.scalar.activation(sg[u], ps[2][:, 0:FE], ACT.Silu).then_inc(S["m_sg"], 1)
                act.wait_ge(S["m_aT"], q + 1)
                nc.scalar.activation(actT[u].rearrange("p c t -> p (c t)"), ps[4][:, 0:FE], ACT.Copy).then_inc(S["m_aTev"], 1)
                act.wait_ge(S["m_dn"], q + 1)
                wait_from(S[f"dn_out{u}"], i * 16)
                nc.scalar.activation(dn[u][:, 0:512], ps[5][:, :], ACT.Copy).then_inc(S["m_dnA"], 1)

            for i in range(PEEL):
                for u in range(2):
                    quad_acts(i, u)
            end = act.value_load(more_i[0:1, 0:1], min_val=0, max_val=MORE_MAX) + QUADS // 2
            with act.Fori(PEEL, end) as i:
                for u in range(2):
                    quad_acts(i, u)

            for v in range(2):
                act.wait_ge(S[f"dn_out{v}"], end * 16)
            for n, m in enumerate(TILES):
                act.dma_start(yg[n][0:m, :], two_dram[2 * P * n:2 * P * n + 2 * m, :].rearrange("(p k) d -> p (k d)", k=2)).then_inc(S[f"fin_in{n}"], 16)
            nc.scalar.activation(t4[:, 0, 0:1], t4[:, 0, 0:1], ACT.Sqrt)

            for n, m in enumerate(TILES):
                act.wait_ge(S["fin_sum"], n + 1)
                if n >= 2:
                    act.wait_ge(S["sq_sum"], NT + NT * WO_ITEMS + n - 1)
                nc.scalar.activation(xg[n % 2][0:m, :], x2[0:m, n, :], ACT.Square,
                                     accum_out=ss1[0:m, n:n + 1]).then_inc(S["sq_sum"], 1)
                act.wait_ge(S["mean_sq"], 3 + 1 + n)
                nc.scalar.activation(rs1[0:m, n:n + 1], rs1[0:m, n:n + 1], ACT.Sqrt).then_inc(S["root"], 1)
            act.wait_ge(S["sd_out"], 16 * H)
            act.wait_ge(S["out_dma"], 32)

        @block.tensor
        def _(pe):
            mm = nc.tensor.matmul

            def flip(out, in_, m):
                return nc.tensor.transpose(out, in_, ident[0:m, 0:m])

            pe.wait_ge(S["ident"], 1)
            pe.wait_ge(S["small_in"], 16 * 4)
            flip(ps[2][:, 0:109], smallrows, 109).then_inc(S["small_t"], 1)
            XB = [6, 7, 0, 1, 3, 4]
            for t, m in enumerate(TILES):
                pe.wait_ge(S["xn"], t + 1)
                for j in range(2):
                    for q in range(4):
                        k = 4 * j + q
                        last = flip(ps[XB[2 * t + j]][:, q * m:(q + 1) * m], xt[0:m, t, k * P:(k + 1) * P], m)
                    last.then_inc(S["x_t"], 1)
            pe.wait_ge(S["ht_done"], 6)
            def proj(n):
                item = n // 2
                if n % 2 == 0:
                    pe.wait_ge(ring_in[item % RA], 16 * (item // RA + 1))
                if n >= 2:
                    pe.wait_ge(S["proj_free"], free[n - 2])
                w = slots[item % RA].rearrange("p (k n) -> p k n", k=KD)
                for k in range(KD):
                    last = mm(ps[n % 2][:, 0:T], w[:, k, P * (n % 2):P * (n % 2) + P], hT[:, k, :],
                              start=(k == 0), stop=(k == KD - 1))
                last.then_inc(S["proj"], 1)

            def squares(n):
                pe.wait_ge(S["sqd"], n + 1)
                for t, m in enumerate(TILES):
                    last = mm(ps[7][0:m, 16 * t + n:16 * t + n + 1], SQ[n % 2][:, P * t:P * t + m], ones[:, 0:1],
                              start=True, stop=True)
                last.then_inc(S["ssd"], 1)

            def raw_flip(n):
                pe.wait_ge(S["proj_free"], free[n])
                pe.wait_ge(S["e_cache"], n + 1)
                j = n // 4
                if n % 4 == 0 and j >= 2:
                    pe.wait_ge(S["raw_ev"], j - 1)
                flip(ps[2 + j % 2][0:RAWN, P * (n % 4):P * (n % 4) + P], E[n % 3][:, RAWC:EW], P).then_inc(S["raw_t"], 1)

            for n in range(NQKV + 1):
                if n < NQKV:
                    proj(n)
                if n == 0:
                    pe.wait_ge(S["small_ev"], 1)
                    pe.wait_ge(S["cache_in"], 32)
                    for c in range(NQKV):
                        last = flip(ps[(5, 2)[c // 12]][:, 24 * (c % 12):24 * (c % 12) + 24], conv_raw[:, c * P:(c + 1) * P], 24)
                        if c % 12 == 11:
                            last.then_inc(S["small_t"], 1)
                    for g in range(NG):
                        last = flip(ps[4][:, 120 * g:120 * g + 120], pool_raw[:, g * P:(g + 1) * P], 120)
                    last.then_inc(S["small_t"], 1)
                if n == 1:
                    pe.wait_ge(S["small_ev"], 4)
                if n == 2:
                    pe.wait_ge(S["misc_in"], 16 * 8)
                    for t, m in enumerate(TILES):
                        for k in range(KD):
                            last = mm(ps[6][0:m, 16 * t:16 * t + 16], hT[:, k, P * t:P * t + m], wab[:, k, :],
                                      start=(k == 0), stop=(k == KD - 1))
                    last.then_inc(S["pe_ab"], 1)
                if n == 4:
                    pe.wait_ge(S["masks"], 1)
                    pe.wait_ge(S["g_done"], 1)
                    for t in range(2):
                        mm(ps[6][:, 64 + 8 * t:72 + 8 * t], triU, g_[:, t], start=True, stop=True)
                        mm(ps[6][:, 96 + 8 * t:104 + 8 * t], ones, g_[:, t], start=True, stop=True)
                    mm(ps[6][0:TS, 80:88], U4[:, :], g_[0:TS, 2], start=True, stop=True)
                    mm(ps[6][0:TS, 112:120], B4[:, :], g_[0:TS, 2], start=True, stop=True)
                    mm(ps[6][:, 128:192], ones[0:TS, :], gbd[0:TS].rearrange("p h b -> p (h b)"),
                       start=True, stop=True).then_inc(S["pe_G"], 1)
                if n >= 1:
                    raw_flip(n - 1)
                if n >= 2 and n - 2 < N_V:
                    squares(n - 2)

            def new_pool(g):
                pe.wait_ge(S["proj_free"], free[N_POOL + g])
                if g == 0:
                    pe.wait_ge(S["raw_ev"], NQKV // 4)
                    pe.wait_ge(S["g_scal"], 1)
                flip(ps[2][0:PBUF, g * P:(g + 1) * P], EP[g % 2][:, TP:TP + PBUF], P)
                flip(ps[6][0:TS, g * P:(g + 1) * P], C[g % 2][:, 0:TS], P).then_inc(S["newp_t"], 1)

            def pool_mix(g):
                pe.wait_ge(S["pool_dve"], g + 1)
                if g == 0:
                    pe.wait_ge(S["ss_sc"], 1)
                else:
                    pe.wait_ge(S["wp_ev"], g)
                mm(ps[7][:, 0:T], wpool[:, g, :], pooled[:, g, :], start=True, stop=True).then_inc(S["wp_pe"], 1)

            for g in range(NG):
                proj(N_POOL + g)
                if g >= 1:
                    new_pool(g - 1)
            new_pool(NG - 1)
            for n in range(Z_AHEAD):
                proj(N_Z + n)
            for g in range(NG):
                pool_mix(g)

            def prep(h):
                pe.wait_ge(S["rb"], 3 * h + 3)
                if h >= 1:
                    pe.wait_ge(S["prep_done"], h)
                mm(ps[3][:, 0:TP], ones, RB[:, 0, :], start=True, stop=True)
                mm(ps[3][:, TP:2 * TP], ones, RB[:, 1, :], start=True, stop=True)
                mm(ps[4][:, 0:TP], ones, RB[:, 2, :], start=True, stop=True).then_inc(S["rows"], 1)
                for c in range(2):
                    last = mm(ps[5][:, TP * c:TP * c + TP].rearrange("p (r t) -> p r t", r=2),
                              qkvT[:, H + h, P * c:P * c + P], qkvT[:, h:h + H + 1:H, P * c:P * c + P],
                              start=True, stop=True)
                last.then_inc(S["qk_pe"], 1)

            pe.wait_ge(S["silu"], 3 * NQKV)
            for h in range(H):
                proj(N_Z + Z_AHEAD + h)
                prep(h)
            proj(N_Z + Z_AHEAD + H)

            pe.wait_ge(S["decrb"], 4)
            pe.wait_ge(S["prep_done"], H)
            for r_ in range(4):
                last = mm(ps[3 + r_ // 2][:, TP * (r_ % 2):TP * (r_ % 2) + TP], ones[0:TS, :],
                          rbd[:, r_].rearrange("p h i -> p (h i)"), start=True, stop=True)
            last.then_inc(S["decrows"], 1)
            d5 = ps[5][0:TS, :].rearrange("p (h r t) -> p h r t", h=H, r=2)
            for h in range(H):
                last = mm(d5[:, h], qkvT[:, H + h, TP:T], qkvT[:, h:h + H + 1:H, TP:T], start=True, stop=True)
            last.then_inc(S["decqk"], 1)

            for n in range(N_GATE + 3, N_GATE + LEAD_GATES):
                proj(n)
                if n == N_GATE + 5:
                    pe.wait_ge(S["decdve"], 3)
                    for h in range(H):
                        last = flip(ps[6][0:TS, TS * h:TS * h + TS], Nd[0:TS, h, :], TS)
                    last.then_inc(S["dinv_pe"], 1)
                if n == N_GATE + 6:
                    pe.wait_ge(S["dinv_dve"], 1)
                    for h in range(H):
                        last = mm(ps[7][0:TS, TS * h:TS * h + TS], tmpd[0:TS, h, :], Nd[0:TS, h, :], start=True, stop=True)
                    last.then_inc(S["dinv_pe"], 1)
                if n == N_GATE + 7:
                    pe.wait_ge(S["dinv_dve"], 3)
                    for h in range(H):
                        last = mm(ps[6][0:TS, TS * h:TS * h + TS], IAd[0:TS, h, :], N2d[0:TS, h, :], start=True, stop=True)
                    last.then_inc(S["dinv_pe"], 1)

            pe.wait_ge(S["diag"], 16 * 19)
            pe.wait_ge(S["newp_ev"], 2)
            pe.wait_ge(S["decdve"], 3)
            pe.wait_ge(S["dec_act"], 2)
            for j in range(4):
                for q in range(4):
                    last = flip(ps[2 + j][:, P * q:P * q + P], X[:, 4 * j + q, :], P)
                last.then_inc(S["xt_pe"], 1)

            def state_products(h):
                pe.wait_ge(S[f"s_in{h % 2}"], 16 * (h // 2 + 1))
                for b_ in range(BD):
                    at = TP + TD * b_
                    last = mm(sdv[:, h, :, TD * b_:TD * b_ + TD], Sd[:, h % 2, b_, :], qkvT[:, h:h + H + 1:H, at:at + TD],
                              start=True, stop=True)
                last.then_inc(S["sd_pe"], 1)

            def merge_y(n):
                L, h = divmod(n, H)
                pe.wait_ge(S["atm"], n + 1)
                if n == 0:
                    pe.wait_ge(S["xt_ev"], 4)
                if n >= 2:
                    pe.wait_ge(S["y_ev"], n - 1)
                if n >= H:
                    pe.wait_ge(S["merge"], n - H + 1)
                for c in range(2):
                    last = mm(ps[2 + n % 2][:, P * c:P * c + P], am[n % 2][:, P * c:P * c + P], X[:, 2 * h + c, :],
                              start=True, stop=True)
                last.then_inc(S["y_pe"], 1)

            def merge_x(n):
                L, h = divmod(n, H)
                pe.wait_ge(S["y_ev"], n + 1)
                if n >= 2:
                    pe.wait_ge(S["merge"], n - 1)
                for c in range(2):
                    if L < 2:
                        mm(ps[4 + n % 2][:, P * c:P * c + P], XT[:, 2 * h + c, :], Y[n % 2][:, P * c:P * c + P],
                           start=True, stop=True)
                    last = mm(ps[4 + n % 2][:, TP + P * c:TP + P * c + P], Y[n % 2][:, P * c:P * c + P],
                              XT[:, 2 * h + c, :], start=True, stop=True)
                last.then_inc(S["xx_pe"], 1)

            for n in range(3 * H + 1):
                if n in GATE_AT:
                    proj(GATE_AT[n])
                if n < 3 * H:
                    merge_y(n)
                if n >= 1:
                    merge_x(n - 1)
                if n in STATE_AT:
                    state_products(STATE_AT[n])

            def scan_a(n):
                c, h = divmod(n, H)
                if n >= 2:
                    pe.wait_ge(S["kd_done"], n - 1)
                bank = ps[2 + n % 2]
                flip(bank[:, 0:P], qkvT[:, 2 * H + h, P * c:P * c + P], P)
                last = flip(bank[:, P:2 * P], qkvT[:, H + h, P * c:P * c + P], P)
                if c == 1:
                    pe.wait_ge(S["s_ev"], h + 1)
                    last = mm(bank[:, 2 * P:3 * P], qkvT[:, H + h, P:TP], St[:, h, :], start=True, stop=True)
                last.then_inc(S["vt_pe"], 1)

            def scan_b(n):
                c, h = divmod(n, H)
                pe.wait_ge(S["R_done"], n + 1)
                if n >= 1:
                    pe.wait_ge(S["vn_ev"], n)
                mm(ps[4][:, 0:P], XT[:, 2 * h + c, :], R[n % 2], start=True, stop=True).then_inc(S["vn_pe"], 1)

            def scan_c(n):
                c, h = divmod(n, H)
                pe.wait_ge(S["vn_ev"], n + 1)
                pe.wait_ge(S["kd_done"], n + 1)
                if n >= 1:
                    pe.wait_ge(S["osq"], OSQ[n - 1])
                if n >= 1:
                    pe.wait_ge(S["s_ev"], n)
                o = ps[6][:, 0:P]
                if c == 1:
                    mm(o, qkvT[:, h, P:TP], St[:, h, :], start=True, stop=False)
                mm(o, aqT[:, 2 * h + c, :], vn[n % 2], start=(c == 0), stop=True).then_inc(S["o_pe"], 1)
                mm(ps[0][:, 0:P], kd[n % 2], vn[n % 2], start=True, stop=True).then_inc(S["s_pe"], 1)

            def by_rows(src, done):
                for h in range(H):
                    last = flip(ps[5 + 2 * (h // 4)][0:TS, P * (h % 4):P * (h % 4) + P], src(h), P)
                last.then_inc(S[done], 1)

            def ring_wait(item):
                pe.wait_ge(ring_in[item % RA], 16 * (item // RA + 1))

            def branch_pool(d):
                item = IN_ITEMS + d // 4
                if d % 4 == 0:
                    ring_wait(item)
                if d >= 1:
                    pe.wait_ge(S["bp_dve"], d)
                w = slots[item % RA].rearrange("p (k n) -> p k n", k=NG)
                for k in range(NG):
                    last = mm(ps[1][:, 0:T], w[:, k, P * (d % 4):P * (d % 4) + P], ypT[:, k, :],
                              start=(k == 0), stop=(k == NG - 1))
                last.then_inc(S["bp_pe"], 1)

            pe.wait_ge(S["merge"], 3 * H)
            pe.wait_ge(S["proj_free"], free[N_PROJ - 1])
            pe.wait_ge(S["dinv_dve"], 4)
            for n in range(2 * H + 2):
                if n < 2 * H:
                    scan_a(n)
                if 1 <= n < 2 * H + 1:
                    scan_b(n - 1)
                if n >= 2:
                    scan_c(n - 2)
                if n in BP_AT:
                    branch_pool(BP_AT[n])
                if n == KDD_AT:
                    pe.wait_ge(S["rtd"], 1)
                    by_rows(lambda h: qkvT[:, H + h, TP:T], "kdd_pe")
                if n == RTD_AT:
                    pe.wait_ge(S["kdd_ev"], 2)
                    by_rows(lambda h: RTd[:, h, :], "rtd_t")
                if n == VND_AT:
                    pe.wait_ge(S["dec_ev"], 2)
                    for h in range(H):
                        last = mm(ps[5 + 2 * (h // 4)][0:TS, P * (h % 4):P * (h % 4) + P], TTd[:, h, :], Rd[:, h, :],
                                  start=True, stop=True)
                    last.then_inc(S["vnd_pe"], 1)
                if n == OD_AT:
                    pe.wait_ge(S["dec_ev"], 2 + 2)
                    for h in range(H):
                        last = mm(ps[5][:, TS * h:TS * h + TS], vnd[:, h, :], aqd[0:TS, h, :], start=True, stop=True)
                    last.then_inc(S["vnd_pe"], 1)
                if n == ODT_AT:
                    pe.wait_ge(S["od_dve"], 1)
                    by_rows(lambda h: oTd[:, h, :], "od_t")

            def decode_state(h):
                pe.wait_ge(S["vx_done"], h + 1)
                if h >= 1:
                    pe.wait_ge(S["sdn_dve"], 2 * h)
                for j in range(2):
                    last = mm(ps[j][:, :], kdd[:, h, :], vx[h % 2][:, 4 * j:4 * j + 4, :].rearrange("p b e -> p (b e)"),
                              start=True, stop=True)
                last.then_inc(S["sdn_pe"], 1)

            pe.wait_ge(S["s_ev"], 2 * H)
            pe.wait_ge(S["bp_dve"], KD)
            decode_state(0)

            for j in range(2):
                for t, m in enumerate(TILES):
                    pe.wait_ge(S["on"], t + 1)
                    if j == 0 and t == 0:
                        pe.wait_ge(S["osq"], 3 * H)
                    for q in range(4):
                        h = 4 * j + q
                        last = flip(ps[2 + NT * j + t][:, q * m:(q + 1) * m], oTok[0:m, t, h * P:(h + 1) * P], m)
                    last.then_inc(S["ot_pe"], 1)

            decode_state(1)

            pe.wait_ge(S["y_done"], 6)
            for d in range(KD):
                item = IN_ITEMS + BP_ITEMS + d // 2
                if d % 2 == 0:
                    ring_wait(item)
                if d >= 2:
                    pe.wait_ge(S["bd_dve"], d - 1)
                w = slots[item % RA].rearrange("p (k n) -> p k n", k=KD)
                for k in range(KD):
                    last = mm(ps[2 + d % 2][:, 0:T], w[:, k, P * (d % 2):P * (d % 2) + P], zT[:, k, :],
                              start=(k == 0), stop=(k == KD - 1))
                last.then_inc(S["bd_pe"], 1)
                if 2 <= d + 1 < H:
                    decode_state(d + 1)
            pe.wait_ge(S["bd_dve"], KD)
            for n, (t, j) in enumerate(WO_STEPS):
                m = TILES[t]
                if n >= 2:
                    pe.wait_ge(S["wo_dve"], n - 1)
                if t < 2:
                    item = IN_ITEMS + BP_ITEMS + BD_ITEMS + j
                    if t == 0:
                        ring_wait(item)
                    w = slots[item % RA].rearrange("p (k n) -> p k n", k=KD)
                    for k in range(KD):
                        last = mm(ps[4 + n % 2][0:m, 0:256], merged[:, k, P * t:P * t + m], w[:, k, :],
                                  start=(k == 0), stop=(k == KD - 1))
                else:
                    for k in range(KD):
                        for q in range(WO_ITEMS):
                            w = slots[(IN_ITEMS + BP_ITEMS + BD_ITEMS + q) % RA].rearrange("p (k n) -> p k n", k=KD)
                            last = mm(ps[4 + n % 2][m * q:m * q + m, 0:256], merged[:, k, TP:T], w[:, k, :],
                                      start=(k == 0), stop=(k == KD - 1))
                last.then_inc(S["wo_pe"], 1)

            pe.wait_ge(S["wo_dve"], NT * WO_ITEMS)

            def logits(t):
                m = TILES[t]
                pe.wait_ge(S["h2_ev"], 2 * t + 2)
                for k in range(KD):
                    last = mm(ps[6][0:m, 36 * t:36 * t + 36], h2T[:, k, P * t:P * t + m], wr[:, k, :],
                              start=(k == 0), stop=(k == KD - 1))
                return last

            for t, m in enumerate(TILES):
                pe.wait_ge(S["h2_dve"], t + 1)
                for j in range(2):
                    for q in range(4):
                        k = 4 * j + q
                        last = flip(ps[NT * j + t][:, q * m:(q + 1) * m], h2[0:m, t, k * P:(k + 1) * P], m)
                    last.then_inc(S["h2_t"], 1)
                if t >= 1:
                    logits(t - 1)
            last = logits(NT - 1)
            last.then_inc(S["route_pe"], 1)
            pe.wait_ge(S["rt_d"], 2 + 1)
            pe.wait_ge(S["cols"], 1)
            for t, m in enumerate(TILES):
                for s in range(t + 1):
                    mm(ps[7][0:m, NE * t:NE * t + NE], (strU[0:m, 0:m] if s == t else ones[:, 0:m]),
                       picks[0:TILES[s], s, :], start=(s == 0), stop=(s == t))
            for s, m in enumerate(TILES):
                last = mm(ps[7][:, NE * NT:NE * NT + NE], ones[0:m, :], picks[0:m, s, :],
                          start=(s == 0), stop=(s == NT - 1))
            last.then_inc(S["route_pe"], 1)
            pe.wait_ge(S["places"], 2)
            pairs = [(t, k) for t in range(NT) for k in range(2)]
            for t, k in pairs:
                m = TILES[t]
                last = mm(ps[6][:, 0:TBL], slot_1h[0:m, t, k, :], quad_1h[0:m, t, k, :],
                          start=((t, k) == pairs[0]), stop=((t, k) == pairs[-1]))
            last.then_inc(S["route_pe"], 1)

            def wait_from(s, v):
                if not isinstance(v, int) or v >= 1:
                    pe.wait_ge(s, v)

            def loaded(part, q):
                for j in range(QE * part, QE * part + QE):
                    base = -(-(A_ITEMS - j) // RA) if j < RA else 0
                    if j < 2 and isinstance(q, int) and q == 1:
                        pe.wait_ge(S[f"spare_in{j}"], 16)
                    elif j < 2 and not (isinstance(q, int) and q == 0):
                        pe.wait_ge(ring_in[j], (q + base) * 16)
                    else:
                        pe.wait_ge(ring_in[j], (q + 1 + base) * 16)

            def quad_products(i, u):
                q = 2 * i + u
                pe.wait_ge(S[f"gather{u}"], (i + 1) * 16)
                wait_from(S["m_TevA"], q)
                wait_from(S["m_TevV"], q)
                for k in range(KD):
                    last = flip(ps[k // 4][:, P * (k % 4):P * (k % 4) + P], xg[u][:, k * P:(k + 1) * P], P)
                last.then_inc(S["m_T"], 1)
                pe.wait_ge(S["m_TevA"], q + 1)
                pe.wait_ge(S["m_TevV"], q + 1)
                for part, done in enumerate(("m_gate", "m_up")):
                    wait_from(S[("m_sg", "m_act")[part]], q)
                    loaded(part, q)
                    for k in range(KD):
                        for e in range(QE):
                            at = spare[e] if isinstance(q, int) and q == 1 and part == 0 and e < 2 else slots[QE * part + e]
                            w = at.rearrange("p (k n) -> p k n", k=KD)
                            last = mm(ps[2 + part][CAP * e:CAP * e + CAP, 0:FE], xgT[u][:, k, CAP * e:CAP * e + CAP],
                                      w[:, k, :], start=(k == 0), stop=(k == KD - 1))
                    last.then_inc(S[done], 1)
                pe.wait_ge(S["m_act"], q + 1)
                wait_from(S["m_aTev"], q)
                for c in range(2):
                    last = flip(ps[4][:, P * c:P * c + P], act_[u][:, P * c:P * c + P], P)
                last.then_inc(S["m_aT"], 1)
                pe.wait_ge(S["m_aTev"], q + 1)
                wait_from(S["m_dnA"], q)
                wait_from(S["m_dnV"], q)
                loaded(2, q)
                for half in range(2):
                    for c in range(2):
                        for e in range(QE):
                            w = slots[2 * QE + e].rearrange("p (c n) -> p c n", c=2)
                            last = mm(ps[5 + half][CAP * e:CAP * e + CAP, :], actT[u][:, c, CAP * e:CAP * e + CAP],
                                      w[:, c, 512 * half:512 * half + 512], start=(c == 0), stop=(c == 1))
                last.then_inc(S["m_dn"], 1)

            pe.wait_ge(S["route"], 1)
            for i in range(PEEL):
                for u in range(2):
                    quad_products(i, u)
            end = pe.value_load(more_i[0:1, 0:1], min_val=0, max_val=MORE_MAX) + QUADS // 2
            with pe.Fori(PEEL, end) as i:
                for u in range(2):
                    quad_products(i, u)

        @block.vector
        def _(dve):
            V = nc.vector
            chain = [0]

            def link(ins):
                chain[0] += 1
                ins.then_inc(S["dve_chain"], 1)
                dve.wait_ge(S["dve_chain"], chain[0])

            def last_as(ins, s, v):
                ins.then_inc(S[s], 1)
                dve.wait_ge(S[s], v)

            def spread(v, m, n):
                return v.unsqueeze(2).to_broadcast([m, v.shape[1], n])

            last_as(V.memset(sc[:, :], 1.0), "sc_one", 1)
            dve.wait_ge(S["sq_sum"], NT)
            V.tensor_scalar(rs1, ss1, 1.0 / D, EPS, ALU.mult, ALU.add).then_inc(S["mean_sq"], 1)
            dve.wait_ge(S["root"], 1)
            link(V.reciprocal(rs1, rs1))
            for t, m in enumerate(TILES):
                V.tensor_scalar(xt[0:m, t, :], xt[0:m, t, :], rs1[0:m, t:t + 1], None, ALU.mult).then_inc(S["xn"], 1)
            dve.wait_ge(S["small_t"], 1)
            last_as(V.tensor_copy(smallT[:, 0:109], ps[2][:, 0:109]), "small_ev", 1)
            XB = [6, 7, 0, 1, 3, 4]
            for t, m in enumerate(TILES):
                for j in range(2):
                    dve.wait_ge(S["x_t"], 2 * t + j + 1)
                    V.tensor_tensor(hT[:, 4 * j:4 * j + 4, P * t:P * t + m],
                                    ps[XB[2 * t + j]][:, 0:4 * m].rearrange("p (k t) -> p k t", k=4),
                                    spread(smallT[:, 96 + 4 * j:100 + 4 * j], P, m), ALU.mult).then_inc(S["ht_done"], 1)

            dve.wait_ge(S["small_t"], 3)
            for j in range(2):
                V.tensor_copy(cT[:, 12 * j:12 * j + 12, :].rearrange("p c r -> p (c r)"), ps[(5, 2)[j]][:, 0:288]).then_inc(S["small_ev"], 1)
            dve.wait_ge(S["small_t"], 4)
            V.tensor_copy(pcT.rearrange("p c r -> p (c r)"), ps[4][:, 0:480]).then_inc(S["small_ev"], 1)

            def conv(n):
                dve.wait_ge(S["proj_free"], free[n])
                dve.wait_ge(S["e_cache"], n + 1)
                if n >= 2:
                    dve.wait_ge(S["silu"], 3 * (n - 1))
                e, c = E[n % 3], C[n % 2]
                link(V.tensor_scalar(c, e[:, 0:NACC], smallT[:, n:n + 1], None, ALU.mult))
                for j in range(1, CW):
                    ins = V.scalar_tensor_tensor(c, e[:, j:j + NACC], smallT[:, NQKV * j + n:NQKV * j + n + 1], c,
                                                 ALU.mult, ALU.add)
                    if j < CW - 1:
                        link(ins)
                ins.then_inc(S["conv"], 1)

            for n in range(NQKV):
                conv(n)
                if n == 2:
                    dve.wait_ge(S["pe_ab"], 1)
                    for t, m in enumerate(TILES):
                        last = V.tensor_copy(ab[0:m, t, :], ps[6][0:m, 16 * t:16 * t + 16])
                        if t < NT - 1:
                            last.then_inc(S["dve_chain"], 1)
                            chain[0] += 1
                    link(last)
                    hb = dtb.unsqueeze(1).to_broadcast([P, NT, H])
                    link(V.tensor_tensor(t1, ab[:, :, H:2 * H], hb, ALU.add))
                    link(V.tensor_scalar(t2, t1, -1.0, None, ALU.mult))
                    V.tensor_tensor(t2, t1, t2, ALU.max).then_inc(S["ab_ev"], 1)
                    dve.wait_ge(S["soft"], 3)
                    V.tensor_scalar(t4, t2, 1.0, None, ALU.add).then_inc(S["ab_ev"], 1)
                    link(V.tensor_scalar(beta, beta, 1.0, None, ALU.add))
                    link(V.reciprocal(beta, beta))
                    dve.wait_ge(S["ab_ev"], 2)
                    link(V.tensor_scalar(g_, t4, -1.0, None, ALU.add))
                    link(V.tensor_tensor(t2, t2, g_, ALU.subtract))
                    link(V.reciprocal(g_, t4))
                    link(V.tensor_tensor(t2, t2, g_, ALU.mult))
                    dve.wait_ge(S["soft"], 4)
                    link(V.tensor_tensor(t2, t2, t3, ALU.add))
                    link(V.tensor_scalar(t1, t1, 0.0, None, ALU.max))
                    link(V.tensor_tensor(t2, t2, t1, ALU.add))
                    link(V.tensor_tensor(t2, t2, alog.unsqueeze(1).to_broadcast([P, NT, H]), ALU.mult))
                    link(V.tensor_scalar(g_, t2, -1.0, None, ALU.mult))
                    dve.wait_ge(S["masks"], 1)
                    V.tensor_tensor(gbd[0:TS], spread(g_[0:TS, 2, :], TS, BD),
                                    bmask[0:TS].unsqueeze(1).to_broadcast([TS, H, BD]), ALU.mult).then_inc(S["g_done"], 1)
                if n == 4:
                    dve.wait_ge(S["pe_G"], 1)
                    dve.wait_ge(S["g_done"], 1)
                    for t, m in enumerate(TILES):
                        link(V.tensor_copy(Gc[0:m, t, :], ps[6][0:m, 64 + 8 * t:72 + 8 * t]))
                        link(V.tensor_copy(Gl[0:m, t, :], ps[6][0:m, 96 + 8 * t:104 + 8 * t]))
                    link(V.tensor_copy(eGd, ps[6][:, 128:192].rearrange("p (h b) -> p h b", h=H)))
                    V.tensor_tensor(kds, Gl, Gc, ALU.subtract).then_inc(S["g_scal"], 1)
                if n == N_V + 1:
                    dve.wait_ge(S["ssd"], N_V)
                    for t, m in enumerate(TILES):
                        link(V.tensor_scalar(rqk[0:m, t, 0:H], ps[7][0:m, 16 * t:16 * t + H], float(DK), EPS * DK, ALU.mult, ALU.add))
                        ins = V.tensor_scalar(rqk[0:m, t, H:2 * H], ps[7][0:m, 16 * t + H:16 * t + 2 * H], EPS, None, ALU.add)
                        if t < NT - 1:
                            link(ins)
                    ins.then_inc(S["ss_sc"], 1)
                if n == N_V + 3:
                    dve.wait_ge(S["ss_sqrt"], 1)
                    dve.wait_ge(S["g_exp"], 4)
                    link(V.reciprocal(rqk, rqk))
                    rq, rk = rqk[:, :, 0:H], rqk[:, :, H:2 * H]
                    link(V.tensor_tensor(brk, beta, rk, ALU.mult))
                    link(V.tensor_tensor(kds, kds, rk, ALU.mult))
                    link(V.tensor_tensor(nber, brk, t1, ALU.mult))
                    link(V.tensor_scalar(nber, nber, -1.0, None, ALU.mult))

            def window(g):
                n = N_POOL + g
                dve.wait_ge(S["proj_free"], free[n])
                dve.wait_ge(S["e_cache"], n + 1)
                e = EP[g % 2]
                src, w = e, 1
                for L in range(g + 1):
                    dst = wa[L % 2]
                    link(V.tensor_tensor(dst[:, 2 * w - 1:EPW], src[:, 2 * w - 1:EPW], src[:, w - 1:EPW - w], ALU.add))
                    src, w = dst, 2 * w
                link(V.tensor_tensor(pooled[:, g, 0:w], src[:, PBUF:PBUF + w], invc[:, 0:w], ALU.mult))
                link(V.tensor_tensor(pooled[:, g, 0:w], pooled[:, g, 0:w], e[:, PBUF:PBUF + w], ALU.subtract))
                link(V.scalar_tensor_tensor(pooled[:, g, w:TP], src[:, PBUF + w:PE0], 1.0 / w, e[:, PBUF + w:PE0],
                                            ALU.mult, ALU.subtract))

                def new(a):
                    return a[:, PE0:EPW].rearrange("p (b r) -> p b r", b=BD)[:, :, PBUF:]

                last_as(V.scalar_tensor_tensor(pooled[:, g, TP:T].rearrange("p (b t) -> p b t", b=BD), new(src), 1.0 / w,
                                               new(e), ALU.mult, ALU.subtract), "pool_dve", g + 1)

            link(V.reciprocal(invc, invc))
            for g in range(NG):
                window(g)

            def prep(h):
                dve.wait_ge(S["rows"], h + 1)
                for c in range(2):
                    V.tensor_scalar(Dt[:, P * c:P * c + P], ps[3][:, P * c:P * c + P], Gc[:, c, h:h + 1], 0.0,
                                    ALU.subtract, ALU.min).then_inc(S["dt"], 1)
                dve.wait_ge(S["expd"], 2 * h + 2)
                dve.wait_ge(S["qk_pe"], h + 1)
                link(V.tensor_tensor(Dt.rearrange("p (c t) -> p c t", c=2), Dt.rearrange("p (c t) -> p c t", c=2),
                                     triU.unsqueeze(1).to_broadcast([P, 2, P]), ALU.mult))
                for c in range(2):
                    for j, to in enumerate((aqT, AT)):
                        link(V.scalar_tensor_tensor(to[:, 2 * h + c, :], ps[5][:, TP * c + P * j:TP * c + P * j + P],
                                                    rqk[:, c, H + h:H + h + 1], Dt[:, P * c:P * c + P], ALU.mult, ALU.mult))
                link(V.tensor_tensor(egq, egq, ps[4][:, P:TP], ALU.mult))
                for to, bank, at in ((aqT, 4, 0), (AT, 3, TP)):
                    v = to[:, 2 * h:2 * h + 2, :]
                    link(V.tensor_tensor(v, v, ps[bank][:, at:at + TP].rearrange("p (c t) -> p c t", c=2), ALU.mult))
                V.tensor_tensor(qkvT[:, h, P:TP], qkvT[:, h, P:TP], egq, ALU.mult).then_inc(S["prep_done"], 1)

            dve.wait_ge(S["silu"], 3 * NQKV)
            dve.wait_ge(S["small_ev"], 4)
            dve.wait_ge(S["wp_pe"], NG)
            for h in range(H):
                prep(h)

            dve.wait_ge(S["dec_act"], 2)
            link(V.tensor_tensor(Dd[0:TS], rows_d[0:TS, 0], spread(Gc[0:TS, 2, :], TS, TS), ALU.subtract))
            V.tensor_scalar(Dd[0:TS], Dd[0:TS], 0.0, None, ALU.min).then_inc(S["decdve"], 1)
            dve.wait_ge(S["dec_act"], 4)
            link(V.tensor_tensor(Dd[0:TS], Dd[0:TS], U4[:, :].unsqueeze(1).to_broadcast([TS, H, TS]), ALU.mult))
            link(V.tensor_tensor(Dd[0:TS], Dd[0:TS], spread(rqk[0:TS, 2, H:2 * H], TS, TS), ALU.mult))
            dve.wait_ge(S["decqk"], 1)
            d5 = ps[5][0:TS, :].rearrange("p (h r t) -> p h r t", h=H, r=2)
            link(V.tensor_tensor(aqd[0:TS], d5[:, :, 0, :], Dd[0:TS], ALU.mult))
            link(V.tensor_tensor(aqd[0:TS], aqd[0:TS], rows_d[0:TS, 2], ALU.mult))
            link(V.tensor_tensor(Nd[0:TS], d5[:, :, 1, :], Dd[0:TS], ALU.mult))
            link(V.tensor_tensor(Nd[0:TS], Nd[0:TS], rows_d[0:TS, 1], ALU.mult))
            link(V.tensor_tensor(tmpd, egd, rows_d[:, 2], ALU.mult))
            link(V.tensor_tensor(qkvT[:, 0:H, TP:T], qkvT[:, 0:H, TP:T], tmpd, ALU.mult))
            V.tensor_tensor(rows_d[:, 1], rows_d[:, 1], egd, ALU.mult).then_inc(S["decdve"], 1)
            V.tensor_tensor(Nd[0:TS], Nd[0:TS], S4[:, :].unsqueeze(1).to_broadcast([TS, H, TS]), ALU.mult).then_inc(S["decdve"], 1)

            dve.wait_ge(S["diag"], 16 * 10)
            dve.wait_ge(S["memsets"], 1 + 1)
            link(V.tensor_scalar(And, And, -1.0, None, ALU.mult))
            xd = Xd.rearrange("p (i c) -> p i c", i=16)
            an = And.rearrange("p (j i) -> p j i", i=16)
            for i in range(1, 16):
                pr = prod[:, 0:i * i].rearrange("p (c j) -> p c j", j=i)
                link(V.tensor_tensor(pr, xd[:, 0:i, 0:i].rearrange("p j c -> p c j"),
                                     an[:, 0:i, i].unsqueeze(1).to_broadcast([P, i, i]), ALU.mult))
                ins = V.tensor_reduce(xd[:, i, 0:i], pr, AX.X, ALU.add)
                if i < 15:
                    link(ins)
            ins.then_inc(S["sub_done"], 1)

            dve.wait_ge(S["dinv_pe"], 1)
            dve.wait_ge(S["decdve"], 3)
            eye_d = ident[0:TS, 0:TS].unsqueeze(1).to_broadcast([TS, H, TS])

            def d_bank(i):
                return ps[i][0:TS, 0:H * TS].rearrange("p (h t) -> p h t", h=H)

            last_as(V.tensor_copy(tmpd[0:TS], d_bank(6)), "dinv_dve", 1)
            last_as(V.tensor_tensor(IAd[0:TS], eye_d, tmpd[0:TS], ALU.subtract), "dinv_dve", 2)
            dve.wait_ge(S["dinv_pe"], 2)
            last_as(V.tensor_copy(N2d[0:TS], d_bank(7)), "dinv_dve", 3)
            dve.wait_ge(S["dinv_pe"], 3)
            link(V.tensor_tensor(Nd[0:TS], eye_d, Nd[0:TS], ALU.subtract))
            V.tensor_tensor(TTd, Nd[0:TS], d_bank(6), ALU.add).then_inc(S["dinv_dve"], 1)

            def mask_level(n):
                L, h = divmod(n, H)
                if n >= 2:
                    dve.wait_ge(S["y_pe"], n - 1)
                V.tensor_tensor(am[n % 2].rearrange("p (c t) -> p c t", c=2), AT[:, 2 * h:2 * h + 2, :],
                                lvl[L].unsqueeze(1).to_broadcast([P, 2, P]), ALU.mult).then_inc(S["atm"], 1)

            def merge(n):
                L, h = divmod(n, H)
                dve.wait_ge(S["xx_pe"], n + 1)
                if n == 0:
                    dve.wait_ge(S["xt_ev"], 4)
                bank = ps[4 + n % 2]
                for j, to in enumerate((X, XT)):
                    if j == 0 and L == 2:
                        continue
                    v = to[:, 2 * h:2 * h + 2, :]
                    ins = V.tensor_tensor(v, v, bank[:, TP * j:TP * j + TP].rearrange("p (c t) -> p c t", c=2), ALU.subtract)
                    if j == 0:
                        link(ins)
                ins.then_inc(S["merge"], 1)

            for n in range(3 * H + 1):
                if n < 3 * H:
                    mask_level(n)
                if n >= 1:
                    merge(n - 1)

            def scan_r(n):
                c, h = divmod(n, H)
                dve.wait_ge(S["vt_pe"], n + 1)
                bank = ps[2 + n % 2]
                if n >= 2:
                    dve.wait_ge(S["vn_pe"], n - 1)
                    dve.wait_ge(S["s_pe"], n - 1)
                ins = V.tensor_scalar(R[n % 2], bank[:, 0:P], beta[:, c, h:h + 1], None, ALU.mult)
                if c == 1:
                    link(ins)
                    ins = V.scalar_tensor_tensor(R[n % 2], bank[:, 2 * P:3 * P], nber[:, c, h:h + 1], R[n % 2],
                                                 ALU.mult, ALU.add)
                ins.then_inc(S["R_done"], 1)
                V.tensor_scalar(kd[n % 2], bank[:, P:2 * P], kds[:, c, h:h + 1], None, ALU.mult).then_inc(S["kd_done"], 1)

            def scan_s(n):
                c, h = divmod(n, H)
                dve.wait_ge(S["s_pe"], n + 1)
                if c == 0:
                    ins = V.tensor_copy(St[:, h, :], ps[0][:, 0:P])
                else:
                    ins = V.scalar_tensor_tensor(St[:, h, :], St[:, h, :], eGl[:, 1, h:h + 1], ps[0][:, 0:P],
                                                 ALU.mult, ALU.add)
                ins.then_inc(S["s_ev"], 1)

            def branch_pool(d):
                dve.wait_ge(S["bp_pe"], d + 1)
                V.scalar_tensor_tensor(gT[:, d, :], gT[:, d, :], 1.0, ps[1][:, 0:T], ALU.add, ALU.mult).then_inc(S["bp_dve"], 1)

            def spread_v(h):
                if h >= 2:
                    dve.wait_ge(S["sdn_pe"], h - 1)
                V.tensor_tensor(vx[h % 2], vnd[:, h, :].unsqueeze(1).to_broadcast([TS, BD, P]),
                                spread(bmask[0:TS], TS, P), ALU.mult).then_inc(S["vx_done"], 1)

            def new_state(h):
                dve.wait_ge(S["sd_mul"], h + 1)
                dve.wait_ge(S["sdn_pe"], h + 1)
                for j in range(2):
                    v = Sd[:, h % 2, 4 * j:4 * j + 4, :].rearrange("p b e -> p (b e)")
                    V.tensor_tensor(v, v, ps[j][:, :], ALU.add).then_inc(S["sdn_dve"], 1)

            dve.wait_ge(S["merge"], 3 * H)
            dve.wait_ge(S["xx_pe"], 3 * H)
            dve.wait_ge(S["sd_pe"], H)
            link(V.tensor_tensor(tmpd, sdv[:, :, 1, :], rows_d[:, 1], ALU.mult))
            link(V.tensor_tensor(RTd, qkvT[:, 2 * H:3 * H, TP:T], rows_d[:, 3], ALU.mult))
            link(V.tensor_copy(oTd, sdv[:, :, 0, :]))
            V.tensor_tensor(RTd, RTd, tmpd, ALU.subtract).then_inc(S["rtd"], 1)
            dve.wait_ge(S["proj_free"], free[N_PROJ - 1])
            for n in range(2 * H + 2):
                if n < 2 * H:
                    scan_r(n)
                if n >= 2:
                    scan_s(n - 2)
                if n in BP_AT:
                    branch_pool(BP_AT[n])
                if n == KDD_AT:
                    dve.wait_ge(S["kdd_pe"], 1)
                    for j in range(2):
                        V.tensor_tensor(kdd[:, 4 * j:4 * j + 4, :], ps[5 + 2 * j][0:TS, :].rearrange("p (h e) -> p h e", h=4),
                                        spread(kds[0:TS, 2, 4 * j:4 * j + 4], TS, P), ALU.mult).then_inc(S["kdd_ev"], 1)
                if n == OD_AT:
                    dve.wait_ge(S["vnd_pe"], 2)
                    V.tensor_tensor(oTd, oTd, ps[5][:, 0:H * TS].rearrange("p (h t) -> p h t", h=H), ALU.add).then_inc(S["od_dve"], 1)
                if n == OD_AT + 1:
                    spread_v(0)

            dve.wait_ge(S["osq"], 3 * H)
            V.tensor_scalar(orr, oss, 1.0 / P, EPS, ALU.mult, ALU.add).then_inc(S["mean_sq"], 1)
            dve.wait_ge(S["root"], 1 + 1)
            link(V.reciprocal(orr, orr))
            for t, m in enumerate(TILES):
                v = oTok[0:m, t].rearrange("p (h e) -> p h e", h=H)
                V.tensor_tensor(v, v, spread(orr[0:m, t, :], m, P), ALU.mult).then_inc(S["on"], 1)
            dve.wait_ge(S["out_dma"], 32)
            spread_v(1)
            new_state(0)
            spread_v(2)

            for j in range(2):
                for t, m in enumerate(TILES):
                    dve.wait_ge(S["ot_pe"], NT * j + t + 1)
                    v = zT[:, 4 * j:4 * j + 4, P * t:P * t + m]
                    V.scalar_tensor_tensor(v, ps[2 + NT * j + t][:, 0:4 * m].rearrange("p (h t) -> p h t", h=4),
                                           smallT[:, 108:109], v, ALU.mult, ALU.mult).then_inc(S["y_done"], 1)

            new_state(1)
            spread_v(3)

            for d in range(KD):
                dve.wait_ge(S["bd_pe"], d + 1)
                link(V.scalar_tensor_tensor(gT[:, KD + d, :], gT[:, KD + d, :], 1.0, ps[2 + d % 2][:, 0:T], ALU.add, ALU.mult))
                V.tensor_tensor(merged[:, d, :], gT[:, d, :], gT[:, KD + d, :], ALU.add).then_inc(S["bd_dve"], 1)
                if 2 <= d + 1 < H:
                    new_state(d + 1)
                    if d + 3 < H:
                        spread_v(d + 3)

            dve.wait_ge(S["xr_in"], 16 * NT)
            for n, (t, j) in enumerate(WO_PARTS):
                m = TILES[t]
                dve.wait_ge(S["wo_pe"], min(n + 1, len(WO_STEPS)))
                bank = min(n, len(WO_STEPS) - 1) % 2
                at = m * j if t == 2 else 0
                cols = slice(256 * j, 256 * j + 256)
                V.scalar_tensor_tensor(x2[0:m, t, cols], ps[4 + bank][at:at + m, 0:256], 0.5, xr[0:m, t, cols],
                                       ALU.mult, ALU.add).then_inc(S["wo_dve"], 1)

            dve.wait_ge(S["sq_sum"], NT + NT * WO_ITEMS)
            link(V.tensor_reduce(ss1, oss[:, :, 0:WO_ITEMS], AX.X, ALU.add))
            V.tensor_scalar(rs1, ss1, 1.0 / D, EPS, ALU.mult, ALU.add).then_inc(S["mean_sq"], 1)
            dve.wait_ge(S["root"], 2 + 1)
            link(V.reciprocal(rs1, rs1))
            dve.wait_ge(S["nb_in"], 32)

            def by_block(v):
                return v.rearrange("p (q k) -> p k q", k=KD)

            dve.wait_ge(S["wo_dve"], NT * WO_ITEMS)
            for t, m in enumerate(TILES):
                V.scalar_tensor_tensor(h2[0:m, t, :].rearrange("p (k q) -> p k q", k=KD), by_block(x2[0:m, t, :]),
                                       rs1[0:m, t:t + 1], by_block(n2b[0:m, :]), ALU.mult, ALU.mult).then_inc(S["h2_dve"], 1)

            link(V.memset(r[:, :, :], 0.0))
            link(V.memset(lg8, -3.0e38))
            dve.wait_ge(S["route_pe"], 1)
            for t, m in enumerate(TILES):
                link(V.tensor_tensor(lg[0:m, t, :], ps[6][0:m, 36 * t:36 * t + 36], rb_[0:m, :], ALU.add))
            link(V.tensor_copy(lg8[:, :, 0:NGR], lg[:, :, 0:NGR]))
            for t in range(NT):
                link(V.max(mx8[:, t, :], lg8[:, t, :]))
                link(V.max_index(mi[:, t, 0:8], mx8[:, t, :], lg8[:, t, :]))
            V.tensor_tensor(eg4, lg[:, :, 0:NGR], mx8[:, :, 0:1].to_broadcast([P, NT, NGR]), ALU.subtract).then_inc(S["rt_d"], 1)
            link(V.tensor_copy(gs, mi[:, :, 0:1]))
            e0 = ecst[:, 0, :]
            link(V.tensor_tensor(goh, e0[:, 0:NGR].unsqueeze(1).to_broadcast([P, NT, NGR]),
                                 gs.to_broadcast([P, NT, NGR]), ALU.is_equal))
            link(V.tensor_tensor(prodr, lg[:, :, NGR:].rearrange("p t (g e) -> p t g e", g=NGR),
                                 goh.unsqueeze(3).to_broadcast([P, NT, NGR, EPG]), ALU.mult))
            link(V.tensor_reduce(les, prodr.rearrange("p t g e -> p t e g"), AX.X, ALU.add))
            for t in range(NT):
                link(V.max(mx8[:, t, :], les[:, t, :]))
                link(V.max_index(mi[:, t, 8:16], mx8[:, t, :], les[:, t, :]))
            V.tensor_tensor(ed, mx8[:, :, 1:2], mx8[:, :, 0:1], ALU.subtract).then_inc(S["rt_d"], 1)
            link(V.tensor_copy(eid, mi[:, :, 8:10]))
            link(V.scalar_tensor_tensor(eid, gs.to_broadcast([P, NT, 2]), float(EPG), eid, ALU.mult, ALU.add))
            link(V.tensor_tensor(oh, e0.unsqueeze(1).unsqueeze(1).to_broadcast([P, NT, 2, NE]),
                                 eid.unsqueeze(3).to_broadcast([P, NT, 2, NE]), ALU.is_equal))
            V.tensor_tensor(picks, oh[:, :, 0, :], oh[:, :, 1, :], ALU.add).then_inc(S["rt_d"], 1)

            def of_expert(to, row):
                link(V.tensor_tensor(prode, oh, row.unsqueeze(1).unsqueeze(1).to_broadcast([P, NT, 2, NE]), ALU.mult))
                link(V.tensor_reduce(to, prode, AX.X, ALU.add))

            of_expert(quad, ecst[:, 1, :])
            of_expert(slot, ecst[:, 2, :])
            dve.wait_ge(S["route_pe"], 1 + 1)
            link(V.tensor_copy(rk_[:, 0:2, :], ps[7][:, 0:2 * NE].rearrange("p (t e) -> p t e", t=2)))
            link(V.tensor_copy(rk_[0:TS, 2, :], ps[7][0:TS, NE * 2:NE * 3]))
            V.tensor_reduce(cnt, ps[7][:, NE * NT:NE * NT + NE], AX.X, ALU.max).then_inc(S["rt_d"], 1)
            link(V.tensor_tensor(prode, oh, rk_.unsqueeze(2).to_broadcast([P, NT, 2, NE]), ALU.mult))
            link(V.tensor_reduce(rank, prode, AX.X, ALU.add))
            link(V.tensor_tensor(full, rank.unsqueeze(3).to_broadcast([P, NT, 2, ROUNDS - 1]),
                                 over[:, 1:].unsqueeze(1).unsqueeze(1).to_broadcast([P, NT, 2, ROUNDS - 1]), ALU.is_ge))
            link(V.tensor_reduce(rnd, full, AX.X, ALU.add))
            link(V.tensor_tensor(slot, slot, rank, ALU.add))
            link(V.scalar_tensor_tensor(slot, rnd, -float(CAP), slot, ALU.mult, ALU.add))
            link(V.scalar_tensor_tensor(quad, rnd, float(QUADS), quad, ALU.mult, ALU.add))
            dve.wait_ge(S["cols"], 1)
            V.tensor_tensor(slot_1h, column_no.unsqueeze(1).unsqueeze(1).to_broadcast([P, NT, 2, P]),
                            slot.unsqueeze(3).to_broadcast([P, NT, 2, P]), ALU.is_equal).then_inc(S["places"], 1)
            link(V.tensor_tensor(quad_1h, column_no[:, 0:TBL].unsqueeze(1).unsqueeze(1).to_broadcast([P, NT, 2, TBL]),
                                 quad.unsqueeze(3).to_broadcast([P, NT, 2, TBL]), ALU.is_equal))
            V.tensor_tensor(quad_1h, quad_1h, tok1[:, :, :].unsqueeze(3).to_broadcast([P, NT, 2, TBL]),
                            ALU.mult).then_inc(S["places"], 1)
            dve.wait_ge(S["rt_d"], 4)
            link(V.tensor_tensor(itc, cnt.to_broadcast([P, ROUNDS]), over[:, :], ALU.is_gt))
            link(V.tensor_reduce(itf, itc, AX.X, ALU.add))
            V.tensor_scalar(more_i[:, :], itf, float(QUADS // 2), -float(QUADS // 2), ALU.mult, ALU.add).then_inc(S["route"], 1)
            dve.wait_ge(S["route_pe"], 1 + 1 + 1)
            link(V.scalar_tensor_tensor(beyond[:, :], ps[6][:, 0:TBL], 0.5, beyond[:, :], ALU.is_lt, ALU.mult))
            link(V.scalar_tensor_tensor(put[:, :], beyond[:, :], -1.0, ps[6][:, 0:TBL], ALU.add, ALU.add))
            V.tensor_scalar(get[:, :], put[:, :], 1, None, ALU.logical_shift_right).then_inc(S["get_done"], 1)
            dve.wait_ge(S["rt_e"], 2)
            link(V.tensor_reduce(pg, eg4, AX.X, ALU.add))
            link(V.tensor_scalar(w12[:, :, 1:2], ed, 1.0, None, ALU.add))
            link(V.tensor_tensor(w12[:, :, 0:1], w12[:, :, 1:2], pg, ALU.mult))
            link(V.reciprocal(w12[:, :, 0:1], w12[:, :, 0:1]))
            link(V.tensor_tensor(w12[:, :, 1:2], w12[:, :, 0:1], ed, ALU.mult))

            def wait_from(s, v):
                if not isinstance(v, int) or v >= 1:
                    dve.wait_ge(s, v)

            def quad_acts(i, u):
                q = 2 * i + u
                dve.wait_ge(S["m_T"], q + 1)
                V.tensor_copy(xgT[u][:, 0:4, :].rearrange("p k t -> p (k t)"), ps[0][:, :]).then_inc(S["m_TevV"], 1)
                dve.wait_ge(S["m_sg"], q + 1)
                dve.wait_ge(S["m_up"], q + 1)
                wait_from(S["m_aT"], q - 1)
                V.tensor_tensor(act_[u].rearrange("p (c q) -> p c q", c=2), sg[u].rearrange("p (q c) -> p c q", c=2),
                                ps[3][:, 0:FE].rearrange("p (q c) -> p c q", c=2), ALU.mult).then_inc(S["m_act"], 1)
                dve.wait_ge(S["m_dn"], q + 1)
                wait_from(S[f"dn_out{u}"], i * 16)
                V.tensor_copy(dn[u][:, 512:1024], ps[6][:, :]).then_inc(S["m_dnV"], 1)

            for i in range(PEEL):
                for u in range(2):
                    quad_acts(i, u)
            end = dve.value_load(more_i[0:1, 0:1], min_val=0, max_val=MORE_MAX) + QUADS // 2
            with dve.Fori(PEEL, end) as i:
                for u in range(2):
                    quad_acts(i, u)

            def sums(t):
                m = TILES[t]
                dve.wait_ge(S[f"fin_in{t}"], 16)
                for k in range(2):
                    ins = V.scalar_tensor_tensor(x2[0:m, t, :], yg[t][0:m, D * k:D * k + D], w12[0:m, t, k:k + 1], x2[0:m, t, :],
                                                 ALU.mult, ALU.add)
                    if k == 0:
                        link(ins)
                ins.then_inc(S["fin_sum"], 1)

            def mean(t):
                m = TILES[t]
                dve.wait_ge(S["sq_sum"], NT + NT * WO_ITEMS + t + 1)
                V.tensor_scalar(rs1[0:m, t:t + 1], ss1[0:m, t:t + 1], 1.0 / D, EPS, ALU.mult, ALU.add).then_inc(S["mean_sq"], 1)

            def normed(t):
                m = TILES[t]
                dve.wait_ge(S["root"], 3 + 1 + t)
                link(V.reciprocal(rs1[0:m, t:t + 1], rs1[0:m, t:t + 1]))
                V.scalar_tensor_tensor(x2[0:m, t, :], x2[0:m, t, :], rs1[0:m, t:t + 1], fnb[0:m, :],
                                       ALU.mult, ALU.mult).then_inc(S["fin_y"], 1)

            sums(0)
            sums(1)
            for t in range(NT):
                mean(t)
                if t + 2 < NT:
                    sums(t + 2)
                normed(t)


_INS = ['x_prompt', 'x_sample', 'cache_pool', 'cache_conv', 'state_delta', 'norm1_w', 'w_in', 'w_pool', 'pool_scale',
        'w_conv', 'a_log', 'dt_bias', 'o_norm_w', 'w_branch_pool', 'w_branch_delta', 'w_out', 'norm2_w',
        'w_router_group', 'b_router_group', 'w_router_expert', 'b_router_expert', 'w_gate', 'w_up', 'w_down',
        'final_norm_w']
_OUTS = [(1, TP, D), (BD, TD, D), (1, 1, PBUF, NG * P), (1, 1, CW - 1, NQKV * P), (1, 1, H, DK, DK),
         (1, BD, PBUF, NG * P), (1, BD, CW - 1, NQKV * P), (1, BD, H, DK, DK)]


def kernel(**inputs):
    import numpy as _np
    import concourse.bacc as _bacc
    from concourse import mybir as _mybir
    from concourse.bass_utils import run_bass_kernel_spmd as _run

    nc = _bacc.Bacc("TRN2", target_bir_lowering=False, num_devices=1)
    arrays, args = {}, []
    for name in _INS:
        a = _np.ascontiguousarray(inputs[name])
        arrays[f"in_{name}_dram"] = a
        args.append(nc.dram_tensor(f"in_{name}_dram", a.shape, _mybir.dt.from_np(a.dtype), kind="ExternalInput").ap())
    for i, shape in enumerate(_OUTS):
        args.append(nc.dram_tensor(f"out_{i}_dram", shape, _mybir.dt.float32, kind="ExternalOutput").ap())
    hybrid_step(nc, *args)
    r = _run(nc, [arrays], core_ids=[0])
    return tuple(r.results[0][f"out_{i}_dram"] for i in range(len(_OUTS)))
```
